# Optimizing a Trainium2 kernel written in Bass

```python
import jax
import jax.numpy as jnp
from jax import lax
import numpy as np

D_MODEL = 1024
BATCH = 1
SEQ = 512
DEPTH = 2

N_MIXERS = 2
N_RWKV = (DEPTH + N_MIXERS - 1) // N_MIXERS
N_MLA = DEPTH // N_MIXERS
NORM_EPS = 1e-6

RWKV_HEAD = 64
RWKV_HEADS = D_MODEL // RWKV_HEAD
DECAY_LORA = 64
ICLR_LORA = 64
VRES_LORA = 32
GATE_LORA = 160
GN_EPS = 64e-5

MLA_HEADS = 16
QK_NOPE = 64
QK_ROPE = 32
V_HEAD = 64
Q_LORA = 384
KV_LORA = 256
ROPE_THETA = 10000.0
Q_BLOCK = 128

N_EXPERTS = 16
EXPERT_FF = 1024
EC_CAPACITY = 2

kernel_name = 'hybrid_rwkv7_mla_ecmoe_encoder'

def rms_norm(x, g, eps=NORM_EPS):
    xf = x.astype(jnp.float32)
    y = xf * lax.rsqrt(jnp.mean(xf * xf, -1, keepdims=True) + eps)
    return (y * g.astype(jnp.float32)).astype(x.dtype)

def centred_shift(x):
    zero = jnp.zeros_like(x[:, :1])
    prev = jnp.concatenate([zero, x[:, :-1]], axis=1)
    nxt = jnp.concatenate([x[:, 1:], zero], axis=1)
    return 0.5 * (prev + nxt)

def wkv7_scan(r, w, k, v, a, b, reverse):
    bsz, _, nh, hd = r.shape

    def step(state, inp):
        r_t, w_t, k_t, v_t, a_t, b_t = inp
        sa = jnp.einsum('bhij,bhj->bhi', state, a_t)
        state = (state * w_t[:, :, None, :] + sa[..., None] * b_t[:, :, None, :]
                 + v_t[..., None] * k_t[:, :, None, :])
        y_t = jnp.einsum('bhij,bhj->bhi', state, r_t)
        return state, y_t

    xs = tuple(jnp.moveaxis(t, 1, 0) for t in (r, w, k, v, a, b))
    s0 = jnp.zeros((bsz, nh, hd, hd), jnp.float32)
    _, ys = lax.scan(step, s0, xs, reverse=reverse)
    return jnp.moveaxis(ys, 0, 1)

def rwkv7_time_mix(h, v_first, mu, w_r, w_k, w_v, w_o, w0, w1, w2, a0, a1, a2,
                   g1, g2, k_k, k_a, r_k, gn_g, gn_b, vres):
    b, s, d = h.shape
    heads = lambda t: t.reshape(b, s, RWKV_HEADS, RWKV_HEAD)
    xx = centred_shift(h) - h
    xr, xw, xk, xv, xa, xg = [h + xx * mu[i] for i in range(6)]
    r = xr @ w_r
    k = xk @ w_k
    v = xv @ w_v
    if vres is None:
        v_first = v
    else:
        v0, v1, v2 = vres
        v = v + (v_first - v) * jax.nn.sigmoid(v0 + (xv @ v1) @ v2)
    g = jax.nn.sigmoid(xg @ g1) @ g2
    kk = heads((k * k_k).astype(jnp.float32))
    kk = kk / jnp.maximum(jnp.sqrt(jnp.sum(kk * kk, -1, keepdims=True)), 1e-12)
    r_h = heads(r).astype(jnp.float32)
    v_h = heads(v).astype(jnp.float32)
    r_k32 = r_k.astype(jnp.float32)
    y = jnp.zeros_like(r_h)
    bonus = jnp.zeros_like(r_h)
    for direction in range(2):
        w_log = -jax.nn.softplus(-(w0[direction] + jnp.tanh(xw @ w1[direction]) @ w2[direction])) - 0.5
        decay = jnp.exp(-jnp.exp(heads(w_log).astype(jnp.float32)))
        a = jax.nn.sigmoid(a0[direction] + (xa @ a1[direction]) @ a2[direction])
        k_d = heads(k * (1.0 + (a - 1.0) * k_a)).astype(jnp.float32)
        a_h = heads(a).astype(jnp.float32)
        y = y + wkv7_scan(r_h, decay, k_d, v_h, -kk, kk * a_h, reverse=(direction == 1))
        bonus = bonus + jnp.sum(r_h * k_d * r_k32, -1, keepdims=True) * v_h
    mean = jnp.mean(y, -1, keepdims=True)
    var = jnp.mean(jnp.square(y - mean), -1, keepdims=True)
    y = ((y - mean) * lax.rsqrt(var + GN_EPS)).reshape(b, s, d)
    y = y * gn_g.astype(jnp.float32) + gn_b.astype(jnp.float32) + bonus.reshape(b, s, d)
    out = (y.astype(h.dtype) * g) @ w_o
    return out, v_first

def rope_tables(positions):
    inv_freq = ROPE_THETA ** (-jnp.arange(0, QK_ROPE, 2, dtype=jnp.float32) / QK_ROPE)
    ang = positions.astype(jnp.float32)[..., None] * inv_freq
    return jnp.cos(ang)[:, :, None, :], jnp.sin(ang)[:, :, None, :]

def rope_tail(x, cos, sin):
    x_nope, x_rope = x[..., :QK_NOPE], x[..., QK_NOPE:]
    x1, x2 = jnp.split(x_rope.astype(jnp.float32), 2, axis=-1)
    rot = jnp.concatenate([x1 * cos - x2 * sin, x2 * cos + x1 * sin], -1).astype(x.dtype)
    return jnp.concatenate([x_nope, rot], -1)

def block_attention(q, k, v):
    b, s, nh, dq = q.shape
    scale = dq ** -0.5
    n_blk = s // Q_BLOCK
    qb = jnp.moveaxis(q.reshape(b, n_blk, Q_BLOCK, nh, dq), 1, 0)

    def one_block(q_blk):
        sc = jnp.einsum('bqhd,bkhd->bhqk', q_blk, k).astype(jnp.float32) * scale
        p = jax.nn.softmax(sc, axis=-1).astype(v.dtype)
        return jnp.einsum('bhqk,bkhd->bqhd', p, v)

    ob = lax.map(one_block, qb)
    return jnp.moveaxis(ob, 0, 1).reshape(b, s, nh, v.shape[-1])

def mla_mix(h, cos, sin, w_in, q_norm_g, kv_norm_g, w_uq, w_ukv, q_head_g, k_head_g, w_o):
    b, s, _ = h.shape
    c = h @ w_in
    c_q, c_kv, k_rope = jnp.split(c, [Q_LORA, Q_LORA + KV_LORA], axis=-1)
    q = (rms_norm(c_q, q_norm_g) @ w_uq).reshape(b, s, MLA_HEADS, QK_NOPE + QK_ROPE)
    kv = (rms_norm(c_kv, kv_norm_g) @ w_ukv).reshape(b, s, MLA_HEADS, QK_NOPE + V_HEAD)
    k_nope, v = kv[..., :QK_NOPE], kv[..., QK_NOPE:]
    k = jnp.concatenate(
        [k_nope, jnp.broadcast_to(k_rope[:, :, None, :], (b, s, MLA_HEADS, QK_ROPE))], -1)
    q = rope_tail(rms_norm(q, q_head_g), cos, sin)
    k = rope_tail(rms_norm(k, k_head_g), cos, sin)
    o = block_attention(q, k, v)
    return o.reshape(b, s, MLA_HEADS * V_HEAD) @ w_o

def expert_choice_ffn(h, w_router, w_gate, w_up, w_down):
    b, s, _ = h.shape
    cap = EC_CAPACITY * s // N_EXPERTS
    aff = jax.nn.softmax((h @ w_router).astype(jnp.float32), axis=-1)
    gates, idx = lax.top_k(jnp.swapaxes(aff, 1, 2), cap)
    b_idx = jnp.arange(b)[:, None, None]
    xe = h[b_idx, idx]
    hid = (jax.nn.silu(jnp.einsum('becd,edf->becf', xe, w_gate))
           * jnp.einsum('becd,edf->becf', xe, w_up))
    ye = jnp.einsum('becf,efd->becd', hid, w_down) * gates[..., None].astype(h.dtype)
    return jnp.zeros_like(h).at[b_idx, idx].add(ye)

def setup_inputs(seed: int = 0) -> dict:
    key = jax.random.key(seed)
    ks = iter(jax.random.split(key, 40))

    def nrm(shape, scale):
        return jax.random.normal(next(ks), shape, jnp.float32) * scale

    def gain(shape):
        return 1.0 + nrm(shape, 0.02)

    D, L, R, M = D_MODEL, DEPTH, N_RWKV, N_MLA
    return {
        'x': nrm((BATCH, SEQ, D), 1.0),
        'positions': (jnp.arange(SEQ, dtype=jnp.int32)[None, :]
                      + jax.random.randint(next(ks), (BATCH, 1), 0, 4096, dtype=jnp.int32)),
        'norm_mix_g': gain((L, D)),
        'norm_ffn_g': gain((L, D)),
        'rw_mu': jax.random.uniform(next(ks), (R, 6, D), jnp.float32),
        'rw_wr': nrm((R, D, D), D ** -0.5),
        'rw_wk': nrm((R, D, D), D ** -0.5),
        'rw_wv': nrm((R, D, D), D ** -0.5),
        'rw_wo': nrm((R, D, D), D ** -0.5),
        'rw_w0': -0.5 + nrm((R, 2, D), 0.5),
        'rw_w1': nrm((R, 2, D, DECAY_LORA), D ** -0.5),
        'rw_w2': nrm((R, 2, DECAY_LORA, D), 0.5 * DECAY_LORA ** -0.5),
        'rw_a0': nrm((R, 2, D), 0.1),
        'rw_a1': nrm((R, 2, D, ICLR_LORA), D ** -0.5),
        'rw_a2': nrm((R, 2, ICLR_LORA, D), 0.5 * ICLR_LORA ** -0.5),
        'rw_g1': nrm((R, D, GATE_LORA), D ** -0.5),
        'rw_g2': nrm((R, GATE_LORA, D), GATE_LORA ** -0.5),
        'rw_kk': 0.85 + nrm((R, D), 0.05),
        'rw_ka': 1.0 + nrm((R, D), 0.05),
        'rw_rk': nrm((R, RWKV_HEADS, RWKV_HEAD), 0.1),
        'rw_gn_g': gain((R, D)),
        'rw_gn_b': nrm((R, D), 0.02),
        'rw_v0': nrm((R - 1, D), 0.1),
        'rw_v1': nrm((R - 1, D, VRES_LORA), D ** -0.5),
        'rw_v2': nrm((R - 1, VRES_LORA, D), 0.5 * VRES_LORA ** -0.5),
        'mla_w_in': nrm((M, D, Q_LORA + KV_LORA + QK_ROPE), D ** -0.5),
        'mla_q_norm_g': gain((M, Q_LORA)),
        'mla_kv_norm_g': gain((M, KV_LORA)),
        'mla_w_uq': nrm((M, Q_LORA, MLA_HEADS * (QK_NOPE + QK_ROPE)), Q_LORA ** -0.5),
        'mla_w_ukv': nrm((M, KV_LORA, MLA_HEADS * (QK_NOPE + V_HEAD)), KV_LORA ** -0.5),
        'mla_q_head_g': gain((M, QK_NOPE + QK_ROPE)),
        'mla_k_head_g': gain((M, QK_NOPE + QK_ROPE)),
        'mla_w_o': nrm((M, MLA_HEADS * V_HEAD, D), (MLA_HEADS * V_HEAD) ** -0.5),
        'moe_router': nrm((L, D, N_EXPERTS), D ** -0.5),
        'moe_w_gate': nrm((L, N_EXPERTS, D, EXPERT_FF), D ** -0.5),
        'moe_w_up': nrm((L, N_EXPERTS, D, EXPERT_FF), D ** -0.5),
        'moe_w_down': nrm((L, N_EXPERTS, EXPERT_FF, D), EXPERT_FF ** -0.5),
    }

def reference(x, positions, norm_mix_g, norm_ffn_g,
              rw_mu, rw_wr, rw_wk, rw_wv, rw_wo, rw_w0, rw_w1, rw_w2,
              rw_a0, rw_a1, rw_a2, rw_g1, rw_g2, rw_kk, rw_ka, rw_rk,
              rw_gn_g, rw_gn_b, rw_v0, rw_v1, rw_v2,
              mla_w_in, mla_q_norm_g, mla_kv_norm_g, mla_w_uq, mla_w_ukv,
              mla_q_head_g, mla_k_head_g, mla_w_o,
              moe_router, moe_w_gate, moe_w_up, moe_w_down):
    cos, sin = rope_tables(positions)
    v_first = None
    for i in range(DEPTH):
        h = rms_norm(x, norm_mix_g[i])
        j = i // N_MIXERS
        if i % N_MIXERS == 0:
            vres = None if j == 0 else (rw_v0[j - 1], rw_v1[j - 1], rw_v2[j - 1])
            mix, v_first = rwkv7_time_mix(
                h, v_first, rw_mu[j], rw_wr[j], rw_wk[j], rw_wv[j], rw_wo[j],
                rw_w0[j], rw_w1[j], rw_w2[j], rw_a0[j], rw_a1[j], rw_a2[j],
                rw_g1[j], rw_g2[j], rw_kk[j], rw_ka[j], rw_rk[j],
                rw_gn_g[j], rw_gn_b[j], vres)
        else:
            mix = mla_mix(h, cos, sin, mla_w_in[j], mla_q_norm_g[j], mla_kv_norm_g[j],
                          mla_w_uq[j], mla_w_ukv[j], mla_q_head_g[j], mla_k_head_g[j],
                          mla_w_o[j])
        x = x + mix
        x = x + expert_choice_ffn(rms_norm(x, norm_ffn_g[i]), moe_router[i],
                                  moe_w_gate[i], moe_w_up[i], moe_w_down[i])
    return x


_drawn_inputs = setup_inputs


def setup_inputs(seed=0):
    import zlib

    import numpy as np

    out = dict(_drawn_inputs(seed))
    spreads = {}
    factors = {'rw_kk': 3.608,
     'rw_gn_g': 3.636,
     'rw_gn_b': 4.019,
     'mla_q_norm_g': 8.0,
     'mla_kv_norm_g': 8.0,
     'mla_q_head_g': 8.0,
     'mla_k_head_g': 8.0}
    for name, (base, spread) in spreads.items():
        noise = np.random.default_rng([zlib.crc32(name.encode()), seed]).standard_normal(out[name].shape)
        drawn = base * np.exp(spread * noise) if base else spread * noise
        out[name] = jnp.asarray(drawn.astype(out[name].dtype))
    for name, factor in factors.items():
        out[name] = (out[name] * factor).astype(out[name].dtype)
    return out
```

```python
from contextlib import ExitStack

import numpy as np

import concourse.bass as bass
from concourse import mybir

F32 = mybir.dt.float32
I32 = mybir.dt.int32
ALU = mybir.AluOpType
ACT = mybir.ActivationFunctionType
AX = mybir.AxisListType.X

P = 128
D = 1024
S = 512
NT = S // P
ND = D // P
NORM_EPS = 1e-6
HEAD = 64
LORA = 64
GATE = 160
GN_EPS = 64e-5
NPAIR = D // (2 * HEAD)
DECAY = -float(np.exp(-0.5))
LEVELS = 7
NOPE = 64
ROPE = 32
VH = 64
QL = 384
KVL = 256
QK = NOPE + ROPE
HALF = ROPE // 2
THETA = 10000.0
NE = 16
FF = 1024
CAP = 2 * S // NE
NB = 8
RING = 4
CHUNK = ND * 512
CPP = 12

V_MU, V_KK, V_KA, V_W0, V_A0, V_GNG, V_GNB, V_RK, V_N = 0, 6, 7, 8, 10, 12, 13, 14, 15


class Jobs:

    def __init__(self, order):
        self.at, self.count = {}, [0] * NB
        for name, bank in order:
            self.count[bank] += 1
            self.at[name] = (bank, self.count[bank])

    def __getitem__(self, name):
        return self.at[name]


def trunk(nc, a):
    with ExitStack() as ctx:
        sem = lambda name: ctx.enter_context(nc.semaphore(name))
        sb = lambda name, shape, dt=F32: ctx.enter_context(nc.sbuf_tensor(name, shape, dt))

        ARENA = 50 * 1024
        arena = sb("arena", [P, ARENA])
        ident = sb("ident", [P, P])
        small = sb("small", [P, 640])
        small_at = [0]

        def tiny(n):
            o = small_at[0]
            small_at[0] += n
            assert small_at[0] <= 640
            return small[:, o:o + n]

        def place(start):
            at = [start]

            def take(*shape):
                n = int(np.prod(shape))
                v = arena[:, at[0]:at[0] + n]
                at[0] += n
                assert at[0] <= ARENA, at[0]
                if len(shape) > 1:
                    names = "abcde"[:len(shape)]
                    v = v.rearrange(f"p ({' '.join(names)}) -> p {' '.join(names)}",
                                    **{c: s for c, s in zip(names, shape)})
                return v
            take.at = at
            return take

        ps = [ctx.enter_context(nc.psum_tensor(f"bank{b}", [P, 512], F32)) for b in range(NB)]

        RING0 = ARENA - RING * CHUNK
        ring = [arena[:, RING0 + s * CHUNK:RING0 + (s + 1) * CHUNK].rearrange("p (k n) -> p k n", k=ND)
                for s in range(RING)]
        common = place(0)
        x_sb = common(NT, D)

        h_tok = common(NT, D)
        hT = common(ND, S)
        AFTER_H = common.at[0]

        pre = place(AFTER_H)
        gain_row = pre(D)
        vec_rows = pre(P)
        w1_sb = pre(ND, 2 * LORA)
        a1_sb = pre(ND, 2 * LORA)
        g1_sb = pre(ND, GATE)
        keep = place(ARENA - (3 * ND * S + 4 * S + NPAIR * S))
        xmix = [keep(ND, S) for _ in range(3)]
        lora_w = keep(S)
        lora_a = keep(S)
        gate_a, gate_b = keep(S), keep(S)
        y_all = keep(NPAIR, S)
        assert pre.at[0] <= ARENA - (3 * ND * S + 4 * S + NPAIR * S)
        shift = h_tok.rearrange("p t d -> p (t d)").rearrange("p (k s) -> p k s", k=ND)

        body = place(0)
        w_sl = body(3, ND, P)
        w2_sl, a2_sl, g2a_sl, g2b_sl = body(P), body(P), body(P), body(P)
        strict_incl = [body(2, P) for _ in range(2)]
        pair_tri = [body(P) for _ in range(2)]
        level_mask = body(LEVELS, P)
        head_ones = body(P)
        chunk_start = body(S)
        rT, kT, vT, gT, kkn, kraw, ksum = (body(S) for _ in range(7))
        tw = [body(S) for _ in range(2)]
        ta = [body(S) for _ in range(2)]
        cs, cx = body(S), body(S)
        e_inc, e_neg, e_exc = body(S), body(S), body(S)
        AR = [body(NT, 2, P) for _ in range(2)]
        Bt = [body(NT, P) for _ in range(2)]
        Kt = [body(NT, P) for _ in range(2)]
        btok = [body(NT, P) for _ in range(2)]
        ktok = [body(NT, P) for _ in range(2)]
        vtok = body(NT, P)
        LTRB = [[body(NT, 2, P) for _ in range(2)] for _ in range(2)]
        TT = [[body(NT, P) for _ in range(2)] for _ in range(2)]
        Tm = [tw[0].rearrange("p (m j) -> p m j", m=NT), tw[1].rearrange("p (m j) -> p m j", m=NT)]
        Xm = [ta[0].rearrange("p (m j) -> p m j", m=NT), ta[1].rearrange("p (m j) -> p m j", m=NT)]
        MTRK = [[body(NT, 2, P) for _ in range(2)] for _ in range(2)]
        assert body.at[0] <= ARENA - (3 * ND * S + 4 * S + NPAIR * S), (body.at[0], ARENA)
        chain_x = e_inc.rearrange("p (h d v) -> p h d v", h=4, d=2)
        chain_u = e_neg[:, 0:256].rearrange("p (h d v) -> p h d v", h=2, d=2)
        states = [e_exc[:, z * 128:(z + 1) * 128].rearrange("p (d v) -> p d v", d=2) for z in range(2)]
        state_dec = e_exc[:, 256:384].rearrange("p (d v) -> p d v", d=2)
        ytok = cs.rearrange("p (t h v) -> p t h v", t=NT, h=2)
        ysq = cx
        rk_cols = kraw

        cols = tiny(V_N * ND)
        pc = tiny(V_N)
        half_col = tiny(2 * 2)
        end_dec = tiny(2 * NT).rearrange("p (d m) -> p d m", d=2)
        stat = tiny(8)
        stat2 = tiny(8)
        rstd8 = tiny(8)
        rstd16 = tiny(16)
        mhalf = tiny(16)
        ssum = tiny(4)
        rstd4 = tiny(4)
        iota_s = tiny(CAP)

        proj = place(AFTER_H + D)
        wo_sb = proj(ND, D)
        assert proj.at[0] <= RING0
        yT = hT

        moe = place(AFTER_H + D)
        xeT = moe(ND, 2 * CAP)
        hid = [moe(ND, CAP) for _ in range(2)]
        th = [moe(4 * CAP) for _ in range(2)]
        ye = moe(D)
        combT = moe(S)
        pick = moe(NT, 2 * CAP)
        pick_gate = moe(NT, 2 * CAP)
        aff = moe(NT, NE + 2)
        slot = moe(NT, NE + 2)
        affT, workT, maskT, cumT = moe(S), moe(S), moe(S), moe(S)
        top8 = moe(8)
        logit = moe(NT, NE)
        iota_i = moe(CAP).bitcast(I32)
        assert proj.at[0] + 0 <= RING0 - ND * NE
        router_sb = arena[:, RING0 - ND * NE:RING0].rearrange("p (k n) -> p k n", k=ND)

        hbuf = place(NT * D)
        prob_at = hbuf.at[0] + NT * S
        prob = [hbuf(NT, S) for _ in range(2)]
        inp = place(AFTER_H + D)
        win_sb = inp(ND, QL + KVL + ROPE)
        c_tok = inp(NT, QL + KVL + ROPE)
        mla = place(AFTER_H + D + ND * D)
        assert inp.at[0] <= mla.at[0]
        cT = mla((QL + KVL) // P, S)
        wq_sl = mla(QL // P, 2 * QK)
        wkv_sl = mla(KVL // P, 2 * (NOPE + VH))
        qk_tok = mla(2, NT * 2, QK)
        qk_sq = arena[:, prob_at:prob_at + 2 * NT * 2 * QK].rearrange("p (a b c) -> p a b c", a=2, b=NT * 2)
        v_tok = mla(NT, 2, VH)
        qkT = [[mla(S) for _ in range(2)] for _ in range(2)]
        probT = [mla(NT, S) for _ in range(2)]
        norm_rows = mla(P)
        head_gain = mla(2, QK)
        k_rope = mla(NT, ROPE)
        cos8, sin8 = mla(NT * 2, HALF), mla(NT * 2, HALF)
        ang, red, rnd = mla(NT, HALF), mla(NT, HALF), mla(NT, HALF)
        freq = mla(HALF)
        pos_f = mla(NT)
        pos_i = mla(NT).bitcast(I32)
        assert mla.at[0] <= RING0 - ND * NE, (mla.at[0], RING0)
        rtmp = [qk_sq.rearrange("p a b c -> p (a b c)")[:, z * 256:(z + 1) * 256].rearrange("p (a b c) -> p a b c", a=2, b=8)
                for z in range(4)]
        norm_cols = tiny(8)
        ss_c = tiny(8)
        rstd_c = tiny(8)
        ss16 = tiny(16)
        mx = tiny(8)
        nmx = tiny(8)
        lsum = tiny(8)
        linv = tiny(8)
        rmax = tiny(NT)
        rsum_t = tiny(NT)

        full = [sem(f"bank_full{b}") for b in range(NB)]
        free = [sem(f"bank_free{b}") for b in range(NB)]
        sq_ready = sem("squares_summed")
        rstd_ready = sem("rstd_ready")
        h_ready = sem("h_ready")
        consts_ready = sem("consts_ready")
        mix_ready = sem("mix_ready")
        mix_used = sem("mix_used")
        gate_ready = sem("gate_ready")
        cols_ready = sem("pair_cols_ready")
        ksq_ready = sem("ksq_ready")
        knorm_clamped = sem("knorm_clamped")
        knorm_root = sem("knorm_root")
        decay_in = sem("decay_tanh_ready")
        iclr_in = sem("iclr_tanh_ready")
        cum_ready = sem("cumulated_ready")
        exps_ready = sem("exps_ready")
        operands_ready = sem("operands_ready")
        bonus_in = sem("bonus_in_ready")
        init_ready = sem("inverse_started")
        ttinit_ready = sem("inverse_t_started")
        state_ready = sem("state_ready")
        ycen_ready = sem("y_centred")
        ysq_ready = sem("y_squares")
        yvar_ready = sem("y_variance")
        yrstd_ready = sem("y_rstd")
        ynorm_ready = sem("y_normed")
        yfeat_ready = sem("y_feature_major")
        moved = sem("moved")
        logit_ready = sem("logit_ready")
        exp_ready = sem("exp_ready")
        aff_ready = sem("aff_ready")
        slot_ready = sem("slot_ready")
        iota_ready = sem("iota_ready")
        pick_ready = sem("pick_ready")
        tanh_ready = sem("tanh_ready")
        hid_ready = sem("hid_ready")
        css_ready = sem("css_ready")
        crstd_ready = sem("crstd_ready")
        cnorm_ready = sem("cnorm_ready")
        red_ready = sem("angles_reduced")
        trig_ready = sem("trig_ready")
        freq_ready = sem("freq_ready")
        rope_in = sem("rope_in")
        qksq_ready = sem("qksq_ready")
        qkss_ready = sem("qkss_ready")
        qkrstd_ready = sem("qkrstd_ready")
        qk_ready = sem("qk_ready")
        max_ready = sem("max_ready")
        prob_exp = sem("prob_exp")
        prob_ready = sem("prob_ready")
        stage_sems = [sq_ready, rstd_ready, h_ready, consts_ready, mix_ready, mix_used, gate_ready,
                      cols_ready, ksq_ready, knorm_clamped, knorm_root, decay_in, iclr_in, cum_ready,
                      exps_ready, operands_ready, bonus_in, init_ready, ttinit_ready, state_ready,
                      ycen_ready, ysq_ready, yvar_ready, yrstd_ready, ynorm_ready, yfeat_ready, moved,
                      logit_ready, exp_ready, aff_ready, slot_ready, iota_ready, pick_ready, tanh_ready, hid_ready,
                      css_ready, crstd_ready, cnorm_ready, red_ready, trig_ready, freq_ready, rope_in,
                      qksq_ready, qkss_ready, qkrstd_ready, qk_ready, max_ready, prob_exp, prob_ready]
        arrive = sem("arrive")
        arrive_sp = sem("arrive_sp")
        go = {e: sem(f"go_{e}") for e in ("pe", "act", "dve", "sp")}
        ld_x = sem("ld_x")
        ld_x2 = sem("ld_x2")
        ld_gain = [sem(f"ld_gain{n}") for n in range(4)]
        ld_vec = sem("ld_vec")
        ld_lora = sem("ld_lora")
        ld_pair = sem("ld_pair")
        ld_wo = [sem(f"ld_wo{n}") for n in range(2)]
        ld_router = [sem(f"ld_router{n}") for n in range(2)]
        ld_chunk = [sem(f"ld_chunk{s}") for s in range(RING)]
        ld_win = sem("ld_win")
        ld_mla = sem("ld_mla")
        ld_pair2 = sem("ld_pair2")
        stored = sem("stored")
        chunk_used = [sem(f"chunk_used{n}") for n in range(2)]

        block = ctx.enter_context(nc.Block())

        def meet(eng, name):
            eng.drain().then_inc(arrive_sp if name == "sp" else arrive, 1)
            eng.wait_ge(go[name], 1)
            eng.sem_clear(go[name])

        def meet_pool(pool, names=("pe", "act", "dve"), credit=0):
            pool.drain()
            pool.wait_ge(arrive, 3)
            pool.sem_clear(arrive)
            if "sp" in names:
                pool.wait_ge(arrive_sp, 1)
                pool.sem_clear(arrive_sp)
            for s in full + free + stage_sems:
                pool.sem_clear(s)
            if credit:
                for s in free:
                    pool.sem_inc(s, credit)
            for n in names:
                pool.sem_inc(go[n], 1)

        def open_job(pe, jobs, name):
            b, n = jobs[name]
            if n > 1:
                pe.wait_ge(free[b], n - 1)
            return ps[b]

        def job_full(eng, jobs, name):
            b, n = jobs[name]
            eng.wait_ge(full[b], n)
            return ps[b]

        def job_read(eng, jobs, name):
            b, n = jobs[name]
            eng.wait_ge(free[b], n)

        norm_jobs = Jobs([(k, k) for k in range(ND)])

        def norm_act(act, x_loaded):
            if x_loaded:
                act.wait_ge(ld_x, 16 * NT)
            for t in range(NT):
                nc.scalar.activation(h_tok[:, t, :], x_sb[:, t, :], ACT.Square,
                                     accum_out=ssum[:, t:t + 1]).then_inc(sq_ready, 1)
            for k in range(0, ND, 2):
                b = job_full(act, norm_jobs, k)
                nc.scalar.copy(hT[:, k, :], b[:, :]).then_inc(free[norm_jobs[k][0]], 1)

        def norm_pool(pool):
            pool.wait_ge(sq_ready, NT)
            nc.gpsimd.tensor_scalar(ssum, ssum, 1.0 / D, NORM_EPS, ALU.mult, ALU.add)
            pool.drain()
            nc.gpsimd.tensor_tensor(rstd4, ssum, mhalf[:, 0:4], ALU.pow).then_inc(rstd_ready, 1)

        def norm_dve(dve, n):
            dve.wait_ge(ld_gain[n], 16)
            dve.wait_ge(rstd_ready, 1)
            for t in range(NT):
                nc.vector.scalar_tensor_tensor(h_tok[:, t, :], x_sb[:, t, :], rstd4[:, t:t + 1], gain_row,
                                               ALU.mult, ALU.mult).then_inc(h_ready, 1)
            for k in range(1, ND, 2):
                b = job_full(dve, norm_jobs, k)
                nc.vector.tensor_copy(hT[:, k, :], b[:, :]).then_inc(free[norm_jobs[k][0]], 1)

        def norm_pe(pe):
            pe.wait_ge(h_ready, NT)
            for k in range(ND):
                b = open_job(pe, norm_jobs, k)
                for t in range(NT):
                    last = nc.tensor.transpose(b[:, t * P:(t + 1) * P], h_tok[:, t, k * P:(k + 1) * P], ident[:, :])
                last.then_inc(full[norm_jobs[k][0]], 1)

        MIX = [(1, 0), (4, 1), (5, 2), (0, 0), (2, 1), (3, 2)]
        pre_jobs = Jobs([("cols", 0), ("w", 1), ("a", 2), ("ga", 3), ("gb", 4)])

        def pre_pe(pe):
            pe.wait_ge(ld_vec, 16 * 8)
            nc.tensor.transpose(ps[0][:, 0:V_N * ND], vec_rows[0:V_N * ND, :],
                                ident[0:V_N * ND, 0:V_N * ND]).then_inc(full[0], 1)
            pe.wait_ge(ld_lora, 16 * 6)
            for n, (name, w, m) in enumerate([("w", w1_sb, P), ("a", a1_sb, P), ("ga", g1_sb, P), ("gb", g1_sb, GATE - P)]):
                src = xmix[min(n, 2)]
                pe.wait_ge(mix_ready, ND * (min(n, 2) + 1))
                b = open_job(pe, pre_jobs, name)
                lo = P if name == "gb" else 0
                for k in range(ND):
                    last = nc.tensor.matmul(b[0:m, :], w[:, k, lo:lo + m], src[:, k, :],
                                            start=(k == 0), stop=(k == ND - 1))
                last.then_inc(full[pre_jobs[name][0]], 1)

        def pre_act(act):
            for name, dst, m, f in (("w", lora_w, P, ACT.Tanh), ("a", lora_a, P, ACT.Copy)):
                b = job_full(act, pre_jobs, name)
                nc.scalar.activation(dst[0:m, :], b[0:m, :], f).then_inc(free[pre_jobs[name][0]], 1)
            for name, dst, m in (("ga", gate_a, P), ("gb", gate_b, GATE - P)):
                b = job_full(act, pre_jobs, name)
                nc.scalar.activation(dst[0:m, :], b[0:m, :], ACT.Tanh, scale=0.5).then_inc(gate_ready, 1)

        def pre_dve(dve):
            job_full(dve, pre_jobs, "cols")
            nc.vector.tensor_copy(cols, ps[0][:, 0:V_N * ND])
            nc.vector.tensor_tensor(shift[:, :, 1:S - 1], hT[:, :, 0:S - 2], hT[:, :, 2:S], ALU.add)
            nc.vector.tensor_copy(shift[:, :, 0:1], hT[:, :, 1:2])
            nc.vector.tensor_copy(shift[:, :, S - 1:S], hT[:, :, S - 2:S - 1])
            dve.drain()
            for k in range(ND):
                nc.vector.scalar_tensor_tensor(shift[:, k, :], shift[:, k, :], 0.5, hT[:, k, :], ALU.mult, ALU.subtract)
            dve.drain()
            for n, (row, buf) in enumerate(MIX):
                if n >= 3:
                    dve.wait_ge(full[pre_jobs[("w", "a", "gb")[n - 3]][0]], 1)
                for k in range(ND):
                    nc.vector.scalar_tensor_tensor(xmix[buf][:, k, :], shift[:, k, :],
                                                   cols[:, (V_MU + row) * ND + k:(V_MU + row) * ND + k + 1],
                                                   hT[:, k, :], ALU.mult, ALU.add).then_inc(mix_ready, 1)
            dve.wait_ge(gate_ready, 2)
            nc.vector.tensor_scalar(gate_a, gate_a, 0.5, 0.5, ALU.mult, ALU.add)
            nc.vector.tensor_scalar(gate_b[0:GATE - P, :], gate_b[0:GATE - P, :], 0.5, 0.5, ALU.mult, ALU.add)

        ii, jj = cs.bitcast(I32), cx.bitcast(I32)

        def masks_pool(pool):
            nc.gpsimd.iota(ii[:, 0:P], [[0, P]], base=0, channel_multiplier=1)
            nc.gpsimd.iota(jj[:, 0:P], [[1, P]], base=0, channel_multiplier=0)
            for m in (strict_incl[0], strict_incl[1]):
                nc.gpsimd.memset(m, 1.0)
            nc.gpsimd.memset(chunk_start, 1.0)
            pool.drain()
            for d, sgn in ((0, 1), (1, -1)):
                for z in range(2):
                    v = strict_incl[d][:, z, :]
                    nc.gpsimd.affine_select(out=v, in_=v, compare_op=ALU.is_ge, fill=0.0, base=z - 1,
                                            pattern=[[sgn, P]], channel_multiplier=-sgn)
            nc.gpsimd.memset(chunk_start.rearrange("p (m j) -> p m j", m=NT)[:, :, 0:1], 0.0)
            pool.drain().then_inc(consts_ready, 1)

        def masks_dve(dve):
            dve.wait_ge(consts_ready, 1)
            nc.vector.tensor_tensor(ii[:, P:2 * P], ii[:, 0:P], jj[:, 0:P], ALU.bitwise_xor)
            dve.drain()
            xor = cs[:, 2 * P:3 * P]
            nc.vector.tensor_copy(xor, ii[:, P:2 * P])
            dve.drain()
            nc.vector.tensor_scalar(head_ones, xor, float(HEAD), None, ALU.is_lt)
            for n in range(LEVELS):
                nc.vector.tensor_scalar(cx[:, P:2 * P], xor, float(2 ** (n + 1)), None, ALU.is_lt)
                dve.drain()
                nc.vector.scalar_tensor_tensor(level_mask[:, n, :], xor, float(2 ** n), cx[:, P:2 * P],
                                               ALU.is_ge, ALU.mult)
                dve.drain()
            for d in range(2):
                nc.vector.tensor_tensor(pair_tri[d], level_mask[:, 0, :], strict_incl[1 - d][:, 0, :], ALU.mult)

        order = [("r", 0), ("k", 1), ("v", 2), ("w0", 3), ("w1", 4), ("a0", 5), ("a1", 6), ("g", 7),
                 ("kn", 0), ("vt", 1), ("bt0", 2), ("kt0", 3), ("bt1", 4), ("kt1", 5)]
        rot = 0
        for d in range(2):
            for h in range(2):
                for nm in ("LR0", "LR1", "L", "MR0", "MR1"):
                    order.append(((nm, d, h), rot % 6))
                    rot += 1
            for lv in range(1, LEVELS):
                for h in range(2):
                    order.append((("X", lv, d, h), 3 * h))
                for h in range(2):
                    if lv < LEVELS - 1:
                        order.append((("TX", lv, d, h), 3 * h + 1))
                    order.append((("XT", lv, d, h), 3 * h + 2))
        order += [("bonus", 0)]
        for m in range(NT):
            order += [(("cx", m, 0), 1), (("cx", m, 1), 2), (("cu", m), 3)]
            if m < NT - 1:
                order += [(("cs", m), 4)]
        order += [(("y", 0), 6), (("y", 1), 7), ("yT", 5)]
        rj = Jobs(order)

        def bc(v, *shape):
            return v.to_broadcast(list(shape))

        def pair_pe(pe, it):
            pe.wait_ge(ld_pair, (it + 1) * (16 * 7))
            for n, name in enumerate(("r", "k", "v")):
                b = open_job(pe, rj, name)
                for k in range(ND):
                    last = nc.tensor.matmul(b[:, :], w_sl[:, n, k, :], xmix[n][:, k, :], start=(k == 0), stop=(k == ND - 1))
                last.then_inc(full[rj[name][0]], 1)
            for kind, w, src in (("w", w2_sl, lora_w), ("a", a2_sl, lora_a)):
                for d in range(2):
                    name = f"{kind}{d}"
                    b = open_job(pe, rj, name)
                    q = slice(d * LORA, (d + 1) * LORA)
                    nc.tensor.matmul(b[:, :], w[q, :], src[q, :], start=True, stop=True).then_inc(full[rj[name][0]], 1)
            b = open_job(pe, rj, "g")
            nc.tensor.matmul(b[:, :], g2a_sl, gate_a, start=True, stop=False)
            nc.tensor.matmul(b[:, :], g2b_sl[0:GATE - P, :], gate_b[0:GATE - P, :], start=False, stop=True).then_inc(full[rj["g"][0]], 1)
            b = open_job(pe, rj, "kn")
            pe.wait_ge(ksq_ready, 1)
            nc.tensor.matmul(b[:, :], head_ones, kraw, start=True, stop=True).then_inc(full[rj["kn"][0]], 1)

            def turn(name, src):
                b = open_job(pe, rj, name)
                for m in range(NT):
                    last = nc.tensor.transpose(b[:, m * P:(m + 1) * P], src[:, m * P:(m + 1) * P], ident[:, :])
                last.then_inc(full[rj[name][0]], 1)

            job_read(pe, rj, "v")
            turn("vt", vT)
            for d in range(2):
                pe.wait_ge(operands_ready, d + 1)
                turn(f"bt{d}", Bt[d].rearrange("p m j -> p (m j)"))
                turn(f"kt{d}", Kt[d].rearrange("p m j -> p (m j)"))
            for d in range(2):
                for h in range(2):
                    q = slice(h * HEAD, (h + 1) * HEAD)
                    for nm, st in (("LR", Bt[d]), ("L", None), ("MR", Kt[d])):
                        if nm == "L":
                            b = open_job(pe, rj, ("L", d, h))
                            for m in range(NT):
                                last = nc.tensor.matmul(b[:, m * P:(m + 1) * P], AR[d][q, m, 0, :], Bt[d][q, m, :], start=True, stop=True)
                            last.then_inc(full[rj[("L", d, h)][0]], 1)
                            continue
                        for z in range(2):
                            name = (f"{nm}{z}", d, h)
                            b = open_job(pe, rj, name)
                            for y in range(2):
                                m = 2 * z + y
                                last = nc.tensor.matmul(b[:, y * 256:(y + 1) * 256], st[q, m, :],
                                                        AR[d][q, m, :, :].rearrange("p a b -> p (a b)"), start=True, stop=True)
                            last.then_inc(full[rj[name][0]], 1)
                for lv in range(1, LEVELS):
                    for h in range(2):
                        name = ("X", lv, d, h)
                        if lv == 1:
                            job_read(pe, rj, ("LR1", d, h))
                            pe.wait_ge(init_ready, 2 * d + h + 1)
                            pe.wait_ge(ttinit_ready, 2 * d + h + 1)
                        else:
                            job_read(pe, rj, ("TX", lv - 1, d, h))
                        b = open_job(pe, rj, name)
                        for m in range(NT):
                            last = nc.tensor.matmul(b[:, m * P:(m + 1) * P], LTRB[d][h][:, m, 0, :], Tm[h][:, m, :], start=True, stop=True)
                        last.then_inc(full[rj[name][0]], 1)
                    for h in range(2):
                        job_read(pe, rj, ("X", lv, d, h))
                        if lv > 1:
                            job_read(pe, rj, ("XT", lv - 1, d, h))
                        if lv < LEVELS - 1:
                            b = open_job(pe, rj, ("TX", lv, d, h))
                            for m in range(NT):
                                last = nc.tensor.matmul(b[:, m * P:(m + 1) * P], TT[d][h][:, m, :], Xm[h][:, m, :], start=True, stop=True)
                            last.then_inc(full[rj[("TX", lv, d, h)][0]], 1)
                        b = open_job(pe, rj, ("XT", lv, d, h))
                        for m in range(NT):
                            last = nc.tensor.matmul(b[:, m * P:(m + 1) * P], Xm[h][:, m, :], TT[d][h][:, m, :], start=True, stop=True)
                        last.then_inc(full[rj[("XT", lv, d, h)][0]], 1)
            pe.wait_ge(bonus_in, 1)
            b = open_job(pe, rj, "bonus")
            nc.tensor.matmul(b[:, :], head_ones, rk_cols, start=True, stop=True).then_inc(full[rj["bonus"][0]], 1)
            for d in range(2):
                for h in range(2):
                    job_read(pe, rj, ("XT", LEVELS - 1, d, h))
                    job_read(pe, rj, ("MR1", d, h))
            for m in range(NT):
                tile = (m, NT - 1 - m)
                if m:
                    pe.wait_ge(state_ready, m)
                for h in range(2):
                    q = slice(h * HEAD, (h + 1) * HEAD)
                    b = open_job(pe, rj, ("cx", m, h))
                    for d in range(2):
                        o = b[:, d * HEAD:(d + 1) * HEAD]
                        if m:
                            nc.tensor.matmul(o, AR[d][q, tile[d], 0, :], states[m % 2][q, d, :], start=True, stop=False)
                        last = nc.tensor.matmul(o, MTRK[d][h][:, tile[d], 0, :], vtok[:, tile[d], q], start=(m == 0), stop=True)
                    last.then_inc(full[rj[("cx", m, h)][0]], 1)
                b = open_job(pe, rj, ("cu", m))
                for h in range(2):
                    job_read(pe, rj, ("cx", m, h))
                    for d in range(2):
                        last = nc.tensor.matmul(b[:, (2 * h + d) * HEAD:(2 * h + d + 1) * HEAD], TT[d][h][:, tile[d], :],
                                                chain_x[:, h, d, :], start=True, stop=True)
                last.then_inc(full[rj[("cu", m)][0]], 1)
                job_read(pe, rj, ("cu", m))
                if m < NT - 1:
                    b = open_job(pe, rj, ("cs", m))
                    for h in range(2):
                        q = slice(h * HEAD, (h + 1) * HEAD)
                        for d in range(2):
                            o = b[q, d * HEAD:(d + 1) * HEAD]
                            nc.tensor.matmul(o, btok[d][:, tile[d], q], chain_u[:, h, d, :], start=True, stop=False)
                            last = nc.tensor.matmul(o, ktok[d][:, tile[d], q], vtok[:, tile[d], q], start=False, stop=True)
                    last.then_inc(full[rj[("cs", m)][0]], 1)
                for h in range(2):
                    q = slice(h * HEAD, (h + 1) * HEAD)
                    for d in range(2):
                        o = ps[6 + h][:, tile[d] * HEAD:(tile[d] + 1) * HEAD]
                        if m:
                            nc.tensor.matmul(o, AR[d][q, tile[d], 1, :], states[m % 2][q, d, :], start=False, stop=False, skip_group_check=True)
                        nc.tensor.matmul(o, LTRB[d][h][:, tile[d], 1, :], chain_u[:, h, d, :],
                                         start=(m == 0 and d == 0), stop=False, skip_group_check=True)
                        last = nc.tensor.matmul(o, MTRK[d][h][:, tile[d], 1, :], vtok[:, tile[d], q], start=False,
                                                stop=(m == NT - 1), skip_group_check=True)
                    if m == NT - 1:
                        last.then_inc(full[rj[("y", h)][0]], 1)
            pe.wait_ge(ynorm_ready, 1)
            turn("yT", cx)

        def pair_act(act, it):
            for name, dst in (("r", rT), ("k", kT)):
                b = job_full(act, rj, name)
                nc.scalar.copy(dst, b[:, :]).then_inc(free[rj[name][0]], 1)
            act.drain()
            act.wait_ge(cols_ready, 1)
            nc.scalar.activation(kraw, kT, ACT.Square, scale=pc[:, V_KK:V_KK + 1]).then_inc(ksq_ready, 1)
            b = job_full(act, rj, "v")
            nc.scalar.copy(vT, b[:, :]).then_inc(free[rj["v"][0]], 1)
            act.wait_ge(knorm_clamped, 1)
            nc.scalar.activation(cx, cs, ACT.Sqrt).then_inc(knorm_root, 1)
            for kind, dst, s in (("w", tw, decay_in), ("a", ta, iclr_in)):
                for d in range(2):
                    name = f"{kind}{d}"
                    b = job_full(act, rj, name)
                    hc = 2 * (kind == "a") + d
                    nc.scalar.activation(dst[d], b[:, :], ACT.Tanh, bias=half_col[:, hc:hc + 1], scale=0.5).then_inc(free[rj[name][0]], 1)
            b = job_full(act, rj, "g")
            nc.scalar.copy(gT, b[:, :]).then_inc(free[rj["g"][0]], 1)
            b = job_full(act, rj, "vt")
            nc.scalar.copy(vtok.rearrange("p m j -> p (m j)"), b[:, :]).then_inc(free[rj["vt"][0]], 1)
            for d in range(2):
                act.wait_ge(cum_ready, d + 1)
                if d:
                    act.wait_ge(operands_ready, 1)
                nc.scalar.activation(e_inc, cs, ACT.Exp)
                nc.scalar.activation(e_neg, cs, ACT.Exp, scale=-1.0)
                nc.scalar.activation(e_exc, cx, ACT.Exp).then_inc(exps_ready, 1)
            for d in range(2):
                for nm, dst in ((f"bt{d}", btok[d]), (f"kt{d}", ktok[d])):
                    b = job_full(act, rj, nm)
                    nc.scalar.copy(dst.rearrange("p m j -> p (m j)"), b[:, :]).then_inc(free[rj[nm][0]], 1)
            for m in range(NT):
                for h in range(2):
                    b = job_full(act, rj, ("cx", m, h))
                    nc.scalar.copy(chain_x[:, h, :, :].rearrange("p d v -> p (d v)"), b[:, 0:128]).then_inc(free[rj[("cx", m, h)][0]], 1)
                b = job_full(act, rj, ("cu", m))
                nc.scalar.copy(chain_u.rearrange("p h d v -> p (h d v)"), b[:, 0:256]).then_inc(free[rj[("cu", m)][0]], 1)
            for h in range(2):
                b = job_full(act, rj, ("y", h))
                nc.scalar.copy(ytok[:, :, h, :], b[:, 0:256].rearrange("p (t v) -> p t v", t=NT)).then_inc(free[rj[("y", h)][0]], 1)
            act.wait_ge(ycen_ready, 1)
            nc.scalar.activation(ysq, cs, ACT.Square).then_inc(ysq_ready, 1)
            b = job_full(act, rj, "yT")
            nc.scalar.activation(e_inc, b[:, :], ACT.Identity, bias=pc[:, V_GNB:V_GNB + 1],
                                 scale=pc[:, V_GNG:V_GNG + 1]).then_inc(yfeat_ready, 1)

        def pair_pool(pool, it):
            for d in range(2):
                for h in range(2):
                    job_read(pool, rj, ("LR1", d, h))
                    lt = LTRB[d][h][:, :, 0, :]
                    nc.gpsimd.tensor_tensor(TT[d][h], lt, bc(level_mask[:, 0, :].unsqueeze(1), P, NT, P), ALU.mult)
                    pool.drain()
                    nc.gpsimd.tensor_tensor(TT[d][h], TT[d][h], bc(ident[:, :].unsqueeze(1), P, NT, P), ALU.add).then_inc(ttinit_ready, 1)
            pool.wait_ge(yvar_ready, 1)
            nc.gpsimd.tensor_scalar(stat2, stat2, 1.0 / HEAD, GN_EPS, ALU.mult, ALU.add)
            pool.drain()
            nc.gpsimd.tensor_tensor(rstd8, stat2, mhalf[:, 0:8], ALU.pow).then_inc(yrstd_ready, 1)

        def pair_dve(dve, it):
            nc.vector.tensor_copy(pc.unsqueeze(2), cols.rearrange("p (g q) -> p g q", q=ND)[:, :, bass.ds(it, 1)])
            dve.drain()
            nc.vector.tensor_scalar(half_col, pc[:, V_W0:V_W0 + 4], 0.5, None, ALU.mult)
            dve.drain().then_inc(cols_ready, 1)
            job_read(dve, rj, "k")
            nc.vector.tensor_scalar(kkn, kT, pc[:, V_KK:V_KK + 1], None, ALU.mult)
            b = job_full(dve, rj, "kn")
            nc.vector.tensor_scalar(cs, b[:, :], 1e-24, None, ALU.max).then_inc(knorm_clamped, 1)
            dve.wait_ge(knorm_root, 1)
            nc.vector.reciprocal(cs, cx)
            dve.drain()
            nc.vector.tensor_tensor(kkn, kkn, cs, ALU.mult).then_inc(free[rj["kn"][0]], 1)
            dve.drain()
            job_read(dve, rj, "r")
            for d in range(2):
                job_read(dve, rj, f"w{d}")
                nc.vector.tensor_scalar(tw[d], tw[d], 0.5 * DECAY, 0.5 * DECAY, ALU.mult, ALU.add)
                dve.drain()
                if d == 0:
                    nc.vector.tensor_tensor_scan(cs, chunk_start, tw[d], 0.0, ALU.mult, ALU.add)
                else:
                    nc.vector.tensor_tensor_scan(cs[:, ::-1], chunk_start, tw[d][:, ::-1], 0.0, ALU.mult, ALU.add)
                dve.drain()
                nc.vector.tensor_tensor(cx, cs, tw[d], ALU.subtract).then_inc(cum_ready, 1)
                job_read(dve, rj, f"a{d}")
                nc.vector.tensor_scalar(ta[d], ta[d], 0.5, 0.5, ALU.mult, ALU.add)
                dve.drain()
                nc.vector.tensor_scalar(tw[d], ta[d], -1.0, pc[:, V_KA:V_KA + 1], ALU.add, ALU.mult)
                nc.vector.tensor_tensor(ta[d], ta[d], kkn, ALU.mult)
                dve.drain()
                nc.vector.scalar_tensor_tensor(tw[d], tw[d], 1.0, kT, ALU.add, ALU.mult)
                dve.drain()
                dve.wait_ge(exps_ready, d + 1)
                flat = lambda v: v.rearrange("p m j -> p (m j)")
                split = lambda v: v.rearrange("p (m j) -> p m j", m=NT)
                nc.vector.tensor_tensor(AR[d][:, :, 1, :], split(rT), split(e_inc), ALU.mult)
                nc.vector.scalar_tensor_tensor(AR[d][:, :, 0, :], split(kkn), -1.0, split(e_exc), ALU.mult, ALU.mult)
                nc.vector.tensor_tensor(flat(Bt[d]), ta[d], e_neg, ALU.mult)
                nc.vector.tensor_tensor(flat(Kt[d]), tw[d], e_neg, ALU.mult)
                if d == 0:
                    nc.vector.tensor_copy(ksum, tw[d])
                else:
                    nc.vector.tensor_tensor(ksum, ksum, tw[d], ALU.add)
                end = split(e_inc)[:, :, P - 1:P] if d == 0 else split(e_inc)[:, :, 0:1]
                nc.vector.tensor_copy(end_dec[:, d, :].unsqueeze(2), end)
                dve.drain().then_inc(operands_ready, 1)
            nc.vector.scalar_tensor_tensor(rk_cols, ksum, pc[:, V_RK:V_RK + 1], rT, ALU.mult, ALU.mult).then_inc(bonus_in, 1)
            for d in range(2):
                for h in range(2):
                    mk = bc(strict_incl[d].unsqueeze(1), P, 2, 2, P)
                    for z in range(2):
                        b = job_full(dve, rj, (f"LR{z}", d, h))
                        nc.vector.tensor_tensor(LTRB[d][h][:, 2 * z:2 * z + 2], b[:, :].rearrange("p (m a j) -> p m a j", m=2, a=2),
                                                mk, ALU.mult).then_inc(free[rj[(f"LR{z}", d, h)][0]], 1)
                    b = job_full(dve, rj, ("L", d, h))
                    nc.vector.tensor_tensor(Tm[h], b[:, :].rearrange("p (m j) -> p m j", m=NT),
                                            bc(pair_tri[d].unsqueeze(1), P, NT, P), ALU.mult).then_inc(free[rj[("L", d, h)][0]], 1)
                    dve.drain()
                    nc.vector.tensor_tensor(Tm[h], Tm[h], bc(ident[:, :].unsqueeze(1), P, NT, P), ALU.add).then_inc(init_ready, 1)
                    for z in range(2):
                        b = job_full(dve, rj, (f"MR{z}", d, h))
                        nc.vector.tensor_tensor(MTRK[d][h][:, 2 * z:2 * z + 2], b[:, :].rearrange("p (m a j) -> p m a j", m=2, a=2),
                                                mk, ALU.mult).then_inc(free[rj[(f"MR{z}", d, h)][0]], 1)
                for h in range(2):
                    dve.wait_ge(ttinit_ready, 2 * d + h + 1)
                for lv in range(1, LEVELS):
                    for h in range(2):
                        name = ("X", lv, d, h)
                        b = job_full(dve, rj, name)
                        nc.vector.tensor_tensor(Xm[h], b[:, :].rearrange("p (m j) -> p m j", m=NT),
                                                bc(level_mask[:, lv, :].unsqueeze(1), P, NT, P), ALU.mult).then_inc(free[rj[name][0]], 1)
                    for h in range(2):
                        for nm, dst in (("TX", Tm[h]), ("XT", TT[d][h])):
                            if nm == "TX" and lv == LEVELS - 1:
                                continue
                            name = (nm, lv, d, h)
                            b = job_full(dve, rj, name)
                            nc.vector.tensor_tensor(dst, dst, b[:, :].rearrange("p (m j) -> p m j", m=NT), ALU.add).then_inc(free[rj[name][0]], 1)
                    dve.drain()
            for m in range(NT - 1):
                b = job_full(dve, rj, ("cs", m))
                for d in range(2):
                    tile = (m, NT - 1 - m)[d]
                    o = b[:, d * HEAD:(d + 1) * HEAD]
                    if m == 0:
                        nc.vector.tensor_scalar(states[1][:, d, :], o, end_dec[:, d, tile:tile + 1], None, ALU.mult)
                    else:
                        nc.vector.scalar_tensor_tensor(states[(m + 1) % 2][:, d, :], o, end_dec[:, d, tile:tile + 1], state_dec[:, d, :], ALU.mult, ALU.add)
                dve.drain().then_inc(state_ready, 1)
                for d in range(2):
                    nx = (m + 1, NT - 2 - m)[d]
                    nc.vector.tensor_scalar(state_dec[:, d, :], states[(m + 1) % 2][:, d, :], end_dec[:, d, nx:nx + 1], None, ALU.mult)
                dve.drain().then_inc(free[rj[("cs", m)][0]], 1)
            for h in range(2):
                job_read(dve, rj, ("y", h))
            y3 = cs.rearrange("p (g v) -> p g v", v=HEAD)
            nc.vector.tensor_reduce(stat, y3, AX, ALU.add)
            dve.drain()
            nc.vector.tensor_scalar(stat, stat, 1.0 / HEAD, None, ALU.mult)
            dve.drain()
            nc.vector.tensor_tensor(y3, y3, bc(stat.unsqueeze(2), P, 8, HEAD), ALU.subtract).then_inc(ycen_ready, 1)
            dve.wait_ge(ysq_ready, 1)
            nc.vector.tensor_reduce(stat2, ysq.rearrange("p (g v) -> p g v", v=HEAD), AX, ALU.add).then_inc(yvar_ready, 1)
            b = job_full(dve, rj, "bonus")
            nc.vector.tensor_tensor(kraw, b[:, :], vT, ALU.mult).then_inc(free[rj["bonus"][0]], 1)
            dve.wait_ge(yrstd_ready, 1)
            nc.vector.tensor_tensor(cx.rearrange("p (g v) -> p g v", v=HEAD), y3, bc(rstd8.unsqueeze(2), P, 8, HEAD), ALU.mult).then_inc(ynorm_ready, 1)
            dve.wait_ge(yfeat_ready, 1)
            nc.vector.tensor_tensor(e_inc, e_inc, kraw, ALU.add)
            dve.drain()
            nc.vector.tensor_tensor(y_all[:, bass.ds(it, 1), :], e_inc.unsqueeze(1), gT.unsqueeze(1), ALU.mult)

        def pair_loads(sp, it):
            c = bass.ds(it * P, P)
            for n, w in enumerate(("rw_wr", "rw_wk", "rw_wv")):
                sp.dma_start(w_sl[:, n], a[w][0].rearrange("(k p) n -> p k n", p=P)[:, :, c]).then_inc(ld_pair, 16)
            sp.dma_start(w2_sl, a["rw_w2"][0].rearrange("e k n -> (e k) n")[:, c]).then_inc(ld_pair, 16)
            sp.dma_start(a2_sl, a["rw_a2"][0].rearrange("e k n -> (e k) n")[:, c]).then_inc(ld_pair, 16)
            sp.dma_start(g2a_sl, a["rw_g2"][0][0:P, c]).then_inc(ld_pair, 16)
            sp.dma_start(g2b_sl[0:GATE - P, :], a["rw_g2"][0][P:GATE, c]).then_inc(ld_pair, 16)

        oj = Jobs([((t, z), (2 * t + z) % NB) for t in range(NT) for z in range(2)])

        def out_pe(pe, n):
            pe.wait_ge(ld_wo[n], 16)
            for t in range(NT):
                for z in range(2):
                    b = open_job(pe, oj, (t, z))
                    for k in range(ND):
                        last = nc.tensor.matmul(b[:, :], yT[:, k, t * P:(t + 1) * P], wo_sb[:, k, z * 512:(z + 1) * 512],
                                                start=(k == 0), stop=(k == ND - 1))
                    last.then_inc(full[oj[(t, z)][0]], 1)

        def out_dve(dve, n):
            if n == 0:
                dve.wait_ge(ld_x2, 16 * NT)
            for t in range(NT):
                for z in range(2):
                    b = job_full(dve, oj, (t, z))
                    xs = x_sb[:, t, z * 512:(z + 1) * 512]
                    nc.vector.tensor_tensor(xs, xs, b[:, :], ALU.add).then_inc(free[oj[(t, z)][0]], 1)

        def load_x(sp, s):
            v = a["x"][0].rearrange("(t p) d -> p t d", p=P)
            for t in range(NT):
                sp.dma_start(x_sb[:, t, :], v[:, t, :]).then_inc(s, 16)

        def load_gain(sp, n):
            layer, which = divmod(n, 2)
            g = a[("norm_mix_g", "norm_ffn_g")[which]][layer:layer + 1, :]
            sp.dma_start(gain_row, g.to_broadcast([P, D])).then_inc(ld_gain[n], 16)

        route_jobs = Jobs([("lg", 0), ("at", 1), ("st", 2)])

        def route_pe(pe, layer):
            pe.wait_ge(ld_router[layer], 16)
            for t in range(NT):
                for k in range(ND):
                    last = nc.tensor.matmul(ps[0][:, t * NE:(t + 1) * NE], hT[:, k, t * P:(t + 1) * P], router_sb[:, k, :],
                                            start=(k == 0), stop=(k == ND - 1))
            last.then_inc(full[0], 1)
            pe.wait_ge(aff_ready, 1)
            for t in range(NT):
                last = nc.tensor.transpose(ps[1][0:NE, t * P:(t + 1) * P], aff[:, t, 0:NE], ident[:, :])
            last.then_inc(full[1], 1)
            pe.wait_ge(slot_ready, 1)
            for t in range(NT):
                last = nc.tensor.transpose(ps[2][:, t * NE:(t + 1) * NE], cumT[0:NE, t * P:(t + 1) * P], ident[0:NE, 0:NE])
            last.then_inc(full[2], 1)

        def route_act(act):
            act.wait_ge(logit_ready, 1)
            nc.scalar.activation(logit, logit, ACT.Exp).then_inc(exp_ready, 1)

        def route_pool(pool):
            nc.gpsimd.iota(iota_i, [[1, CAP]], base=0, channel_multiplier=0)
            nc.gpsimd.memset(slot[:, :, NE:NE + 2], -1.0)
            nc.gpsimd.memset(aff[:, :, NE:NE + 2], 0.0)
            pool.drain().then_inc(iota_ready, 1)

        def route_dve(dve):
            b = job_full(dve, route_jobs, "lg")
            lg = b[:, 0:NT * NE].rearrange("p (t e) -> p t e", t=NT)
            nc.vector.tensor_reduce(rmax, lg, AX, ALU.max)
            dve.drain()
            nc.vector.tensor_tensor(logit, lg, rmax.unsqueeze(2).to_broadcast([P, NT, NE]), ALU.subtract).then_inc(logit_ready, 1)
            dve.wait_ge(exp_ready, 1)
            nc.vector.tensor_reduce(rsum_t, logit, AX, ALU.add)
            dve.drain()
            nc.vector.reciprocal(rmax, rsum_t)
            dve.drain()
            nc.vector.tensor_tensor(aff[:, :, 0:NE], logit, rmax.unsqueeze(2).to_broadcast([P, NT, NE]), ALU.mult).then_inc(aff_ready, 1)
            b = job_full(dve, route_jobs, "at")
            nc.vector.tensor_copy(workT[0:NE, :], b[0:NE, :])
            for n in range(CAP // 8):
                dve.drain()
                nc.vector.max(top8[0:NE, :], workT[0:NE, :])
                dve.drain()
                nc.vector.match_replace(workT[0:NE, :], top8[0:NE, :], workT[0:NE, :], -1.0)
            dve.drain()
            nc.vector.tensor_scalar(maskT[0:NE, :], workT[0:NE, :], 0.0, None, ALU.is_lt)
            dve.drain()
            nc.vector.tensor_tensor_scan(cumT[0:NE, :], maskT[0:NE, :], maskT[0:NE, :], 0.0, ALU.add, ALU.max)
            dve.drain()
            nc.vector.tensor_tensor(cumT[0:NE, :], cumT[0:NE, :], maskT[0:NE, :], ALU.mult)
            dve.drain()
            nc.vector.tensor_scalar(cumT[0:NE, :], cumT[0:NE, :], -1.0, None, ALU.add).then_inc(slot_ready, 1)
            dve.wait_ge(iota_ready, 1)
            nc.vector.tensor_copy(iota_s, iota_i)
            b = job_full(dve, route_jobs, "st")
            nc.vector.tensor_copy(slot[:, :, 0:NE], b[:, 0:NT * NE].rearrange("p (t e) -> p t e", t=NT))
            dve.drain()
            picks(dve, 0)

        def picks(dve, first):
            for t in range(NT):
                for e in range(2):
                    o = slice(e * CAP, (e + 1) * CAP)
                    at = slot[:, t, bass.ds(first + e, 1)]
                    nc.vector.tensor_scalar(pick[:, t, o], iota_s, at, None, ALU.is_equal)
                    nc.vector.tensor_scalar(pick_gate[:, t, o], iota_s, at, aff[:, t, bass.ds(first + e, 1)], ALU.is_equal, ALU.mult)

        PER = [3, 3, 3, 2, 2, 2, 2, 2]
        comb_banks = [7, 0, 1, 2]

        def used(eng, b, it, n):
            eng.wait_ge(free[b], it * PER[b] + n)

        def filled(eng, b, it, n):
            eng.wait_ge(full[b], it * PER[b] + n)

        def read_out(eng, b, it, n):
            eng.wait_ge(free[b], it * PER[b] + n + 1)

        def moe_pe(pe, it, layer):
            pe.wait_ge(pick_ready, it + 1)
            for z in range(2):
                used(pe, z, it, 1)
                for k in range(4):
                    for t in range(NT):
                        last = nc.tensor.matmul(ps[z][:, k * P:(k + 1) * P], h_tok[:, t, (4 * z + k) * P:(4 * z + k + 1) * P],
                                                pick[:, t, :], start=(t == 0), stop=(t == NT - 1))
                last.then_inc(full[z], 1)
            used(pe, 2, it, 1)
            for t in range(NT):
                last = nc.tensor.transpose(ps[2][:, t * P:(t + 1) * P], pick_gate[:, t, :], ident[:, :])
            last.then_inc(full[2], 1)
            for e in range(2):
                for z in range(2):
                    used(pe, 3 + z, it, e + 1)
                    for g in range(2):
                        c = 6 * e + 2 * z + g
                        pe.wait_ge(ld_chunk[c % RING], (it * 3 + (c // RING + 1 + 24 * layer)) * 16)
                        if e == 0 and z == 0 and g == 0:
                            read_out(pe, 0, it, 1)
                            read_out(pe, 1, it, 1)
                        for f in range(4):
                            for k in range(ND):
                                last = nc.tensor.matmul(ps[3 + z][:, (4 * g + f) * CAP:(4 * g + f + 1) * CAP],
                                                        ring[c % RING][:, k, f * P:(f + 1) * P], xeT[:, k, e * CAP:(e + 1) * CAP],
                                                        start=(k == 0), stop=(k == ND - 1))
                        last.then_inc(chunk_used[layer], 1)
                    pe.drain().then_inc(full[3 + z], 1)
                for z in range(2):
                    c = 6 * e + 4 + z
                    used(pe, 5 + z, it, e + 1)
                    pe.wait_ge(ld_chunk[c % RING], (it * 3 + (c // RING + 1 + 24 * layer)) * 16)
                    pe.wait_ge(hid_ready, it * 4 + (2 * e + 2))
                    for k in range(ND):
                        last = nc.tensor.matmul(ps[5 + z][e * CAP:(e + 1) * CAP, :], hid[e][:, k, :], ring[c % RING][:, k, :],
                                                start=(k == 0), stop=(k == ND - 1))
                    last.then_inc(chunk_used[layer], 1)
                    pe.drain().then_inc(full[5 + z], 1)
            read_out(pe, 2, it, 1)
            read_out(pe, 5, it, 2)
            read_out(pe, 6, it, 2)
            for j in range(8):
                t, z = divmod(j, 2)
                b = comb_banks[j % 4]
                used(pe, b, it, j // 4 + (1 if b == 7 else 2))
                nc.tensor.matmul(ps[b][:, :], combT[:, t * P:(t + 1) * P], ye[:, z * 512:(z + 1) * 512],
                                 start=True, stop=True).then_inc(full[b], 1)

        def moe_act(act, it):
            for z in range(2):
                filled(act, z, it, 1)
                nc.scalar.copy(xeT[:, 4 * z:4 * z + 4, :].rearrange("p k s -> p (k s)"), ps[z][:, :]).then_inc(free[z], 1)
            for e in range(2):
                for z in range(2):
                    filled(act, 3 + z, it, e + 1)
                    nc.scalar.activation(th[z], ps[3 + z][:, 0:4 * CAP], ACT.Tanh, scale=0.5).then_inc(tanh_ready, 1)
                for z in range(2):
                    filled(act, 5 + z, it, e + 1)
                    q = slice(e * CAP, (e + 1) * CAP)
                    nc.scalar.copy(ye[q, z * 512:(z + 1) * 512], ps[5 + z][q, :]).then_inc(free[5 + z], 1)

        def moe_dve(dve, it):
            filled(dve, 2, it, 1)
            nc.vector.tensor_copy(combT, ps[2][:, :]).then_inc(free[2], 1)
            for e in range(2):
                for z in range(2):
                    dve.wait_ge(tanh_ready, it * 4 + (2 * e + z + 1))
                    nc.vector.scalar_tensor_tensor(th[z], th[z], 1.0, ps[3 + z][:, 0:4 * CAP], ALU.add, ALU.mult)
                    dve.drain()
                    nc.vector.scalar_tensor_tensor(hid[e][:, 4 * z:4 * z + 4, :].rearrange("p k s -> p (k s)"), th[z], 0.5,
                                                   ps[3 + z][:, 4 * CAP:8 * CAP], ALU.mult, ALU.mult).then_inc(hid_ready, 1)
                    dve.drain().then_inc(free[3 + z], 1)
                if e == 0:
                    filled(dve, 1, it, 1)
                    picks(dve, it * 2 + 2)
                    dve.drain().then_inc(pick_ready, 1)
            for j in range(8):
                t, z = divmod(j, 2)
                b = comb_banks[j % 4]
                filled(dve, b, it, j // 4 + (1 if b == 7 else 2))
                xs = x_sb[:, t, z * 512:(z + 1) * 512]
                nc.vector.tensor_tensor(xs, xs, ps[b][:, :], ALU.add).then_inc(free[b], 1)

        def load_chunk(sp, layer, pair, c):
            e, r = divmod(c % CPP, 6)
            w, z = (("moe_w_gate", 0), ("moe_w_up", 0), ("moe_w_gate", 1), ("moe_w_up", 1), ("moe_w_down", 0), ("moe_w_down", 1))[r]
            v = a[w][layer].rearrange("(i e) (k p) n -> i e p k n", e=2, p=P)
            pair = pair + c // CPP
            src = v[bass.ds(pair, 1), e, :, :, z * 512:(z + 1) * 512].rearrange("i p k n -> (i p) k n") \
                if not isinstance(pair, int) else v[pair, e, :, :, z * 512:(z + 1) * 512]
            sp.dma_start(ring[c % RING], src).then_inc(ld_chunk[c % RING], 16)

        def load_experts(sp, layer, first=True):
            last = NE // 2 - 1
            for c in range(RING):
                load_chunk(sp, layer, 0, c)
            with sp.Fori(0, last) as it:
                for c in range(CPP):
                    sp.wait_ge(chunk_used[layer], it * CPP + (c + 1))
                    load_chunk(sp, layer, it, c + RING)
            for c in range(CPP - RING):
                sp.wait_ge(chunk_used[layer], last * CPP + c + 1)
                load_chunk(sp, layer, last, c + RING)

        CB = [(t, z) for t in range(NT) for z in range(2)]
        NC = (QL + KVL) // P
        mj = Jobs([(x, n) for n, x in enumerate(CB)] + [("cols", 0)] + [(("cT", j), j + 1) for j in range(NC)])

        def mla_in_pe(pe):
            pe.wait_ge(ld_win, 16)
            for t, z in CB:
                w = 512 if z == 0 else QL + KVL + ROPE - 512
                b = open_job(pe, mj, (t, z))
                for k in range(ND):
                    last = nc.tensor.matmul(b[:, 0:w], hT[:, k, t * P:(t + 1) * P], win_sb[:, k, z * 512:z * 512 + w],
                                            start=(k == 0), stop=(k == ND - 1))
                last.then_inc(full[mj[(t, z)][0]], 1)
            pe.wait_ge(ld_mla, 16 * 5)
            b = open_job(pe, mj, "cols")
            nc.tensor.transpose(b[:, 0:NC], norm_rows[0:NC, :], ident[0:NC, 0:NC]).then_inc(full[0], 1)
            pe.wait_ge(cnorm_ready, 1)
            for j in range(NC):
                b = open_job(pe, mj, ("cT", j))
                for t in range(NT):
                    last = nc.tensor.transpose(b[:, t * P:(t + 1) * P], c_tok[:, t, j * P:(j + 1) * P], ident[:, :])
                last.then_inc(full[j + 1], 1)

        def mla_in_act(act):
            for t, z in CB:
                w = 512 if z == 0 else QL + KVL + ROPE - 512
                b = job_full(act, mj, (t, z))
                nc.scalar.copy(c_tok[:, t, z * 512:z * 512 + w], b[:, 0:w]).then_inc(free[mj[(t, z)][0]], 1)
            act.drain()
            for t in range(NT):
                nc.scalar.activation(prob[0][:, t, 0:QL], c_tok[:, t, 0:QL], ACT.Square, accum_out=ss_c[:, t:t + 1])
                nc.scalar.activation(prob[1][:, t, 0:KVL], c_tok[:, t, QL:QL + KVL], ACT.Square, accum_out=ss_c[:, NT + t:NT + t + 1])
            act.drain().then_inc(css_ready, 1)
            nc.scalar.copy(k_rope, c_tok[:, :, QL + KVL:])
            act.wait_ge(red_ready, 1)
            nc.scalar.activation(sin8.rearrange("p (t h) f -> p t h f", h=2)[:, :, 0, :], red, ACT.Sin)
            nc.scalar.activation(cos8.rearrange("p (t h) f -> p t h f", h=2)[:, :, 0, :], ang, ACT.Sin)
            act.drain()
            for v in (sin8, cos8):
                w = v.rearrange("p (t h) f -> p t h f", h=2)
                nc.scalar.copy(w[:, :, 1, :], w[:, :, 0, :])

        def mla_in_pool(pool):
            for n in range(HALF):
                nc.gpsimd.memset(freq[:, n:n + 1], float(np.float32(THETA) ** np.float32(-2.0 * n / ROPE)))
            pool.drain().then_inc(freq_ready, 1)
            pool.wait_ge(css_ready, 1)
            nc.gpsimd.tensor_scalar(ss_c[:, 0:NT], ss_c[:, 0:NT], 1.0 / QL, NORM_EPS, ALU.mult, ALU.add)
            nc.gpsimd.tensor_scalar(ss_c[:, NT:], ss_c[:, NT:], 1.0 / KVL, NORM_EPS, ALU.mult, ALU.add)
            pool.drain()
            nc.gpsimd.tensor_tensor(rstd_c, ss_c, mhalf[:, 0:8], ALU.pow).then_inc(crstd_ready, 1)

        def mla_in_dve(dve):
            dve.wait_ge(ld_mla, 16 * 5)
            nc.vector.tensor_copy(pos_f, pos_i)
            dve.wait_ge(freq_ready, 1)
            dve.drain()
            nc.vector.tensor_tensor(red, pos_f.unsqueeze(2).to_broadcast([P, NT, HALF]), freq.unsqueeze(1).to_broadcast([P, NT, HALF]), ALU.mult)
            dve.drain()
            nc.vector.tensor_scalar(rnd, red, float(1.0 / (2.0 * np.pi)), 12582912.0, ALU.mult, ALU.add)
            dve.drain()
            nc.vector.tensor_scalar(rnd, rnd, -12582912.0, None, ALU.add)
            dve.drain()
            two_pi = 2.0 * np.pi
            c1 = 6.28125
            c2 = float(np.float32(np.round((two_pi - c1) * 2.0 ** 21) / 2.0 ** 21))
            c3 = two_pi - c1 - c2
            for c in (c1, c2, c3):
                nc.vector.scalar_tensor_tensor(red, rnd, -float(c), red, ALU.mult, ALU.add)
                dve.drain()
            nc.vector.tensor_scalar(red, red, 3.1415925, -3.1415925, ALU.min, ALU.max)
            dve.drain()
            nc.vector.scalar_tensor_tensor(ang, red, -1.0, red, ALU.mult, ALU.max)
            dve.drain()
            nc.vector.tensor_scalar(ang, ang, -1.0, float(np.pi / 2), ALU.mult, ALU.add).then_inc(red_ready, 1)
            job_full(dve, mj, "cols")
            nc.vector.tensor_copy(norm_cols[:, 0:NC], ps[0][:, 0:NC])
            dve.wait_ge(crstd_ready, 1)
            for t in range(NT):
                for lo, hi, s in ((0, QL, t), (QL, QL + KVL, NT + t)):
                    nc.vector.tensor_scalar(c_tok[:, t, lo:hi], c_tok[:, t, lo:hi], rstd_c[:, s:s + 1], None, ALU.mult)
            dve.drain().then_inc(cnorm_ready, 1)
            for j in range(NC):
                b = job_full(dve, mj, ("cT", j))
                nc.vector.tensor_scalar(cT[:, j, :], b[:, :], norm_cols[:, j:j + 1], None, ALU.mult)

        NQ, NKV = QL // P, KVL // P
        names = [("q", 0), ("q", 1), ("kv", 0), ("kv", 1)] + [("T", h, s) for h in range(2) for s in range(2)]
        names += [("S", h, t) for h in range(2) for t in range(NT)]
        for h in range(2):
            names += [("PT", h, t) for t in range(NT)] + [("o", h)]
        aj = Jobs([(x, n % NB) for n, x in enumerate(names)])
        SCALE = QK ** -0.5

        def attn_pe(pe, it):
            pe.wait_ge(ld_pair2, (it + 1) * 32)
            for kind, w, n0, n, width in (("q", wq_sl, 0, NQ, 2 * QK), ("kv", wkv_sl, NQ, NKV, 2 * (NOPE + VH))):
                for z in range(2):
                    b = open_job(pe, aj, (kind, z))
                    for y in range(2):
                        t = 2 * z + y
                        for j in range(n):
                            last = nc.tensor.matmul(b[:, y * width:(y + 1) * width], cT[:, n0 + j, t * P:(t + 1) * P], w[:, j, :],
                                                    start=(j == 0), stop=(j == n - 1))
                    last.then_inc(full[aj[(kind, z)][0]], 1)
            pe.wait_ge(qk_ready, 1)
            for h in range(2):
                for s in range(2):
                    b = open_job(pe, aj, ("T", h, s))
                    for t in range(NT):
                        last = nc.tensor.transpose(b[0:QK, t * P:(t + 1) * P], qk_tok[:, s, 2 * t + h, :], ident[:, :])
                    last.then_inc(full[aj[("T", h, s)][0]], 1)
            for h in range(2):
                job_read(pe, aj, ("T", h, 0))
                job_read(pe, aj, ("T", h, 1))
                for t in range(NT):
                    b = open_job(pe, aj, ("S", h, t))
                    nc.tensor.matmul(b[:, :], qkT[h][0][0:QK, t * P:(t + 1) * P], qkT[h][1][0:QK, :],
                                     start=True, stop=True).then_inc(full[aj[("S", h, t)][0]], 1)
            for h in range(2):
                pe.wait_ge(prob_ready, NT * (h + 1))
                for t in range(NT):
                    b = open_job(pe, aj, ("PT", h, t))
                    for q in range(NT):
                        last = nc.tensor.transpose(b[:, q * P:(q + 1) * P], prob[h][:, q, t * P:(t + 1) * P], ident[:, :])
                    last.then_inc(full[aj[("PT", h, t)][0]], 1)
                b = open_job(pe, aj, ("o", h))
                for t in range(NT):
                    job_read(pe, aj, ("PT", h, t))
                    last = nc.tensor.matmul(b[h * VH:(h + 1) * VH, :], v_tok[:, t, h, :], probT[h][:, t, :],
                                            start=(t == 0), stop=(t == NT - 1))
                last.then_inc(full[aj[("o", h)][0]], 1)

        def attn_act(act, it):
            for z in range(2):
                b = job_full(act, aj, ("q", z))
                nc.scalar.copy(qk_tok[:, 0, 4 * z:4 * z + 4, :].rearrange("p g c -> p (g c)"), b[:, 0:4 * QK]).then_inc(free[aj[("q", z)][0]], 1)
            for z in range(2):
                b = job_full(act, aj, ("kv", z))
                kv = b[:, :].rearrange("p (g c) -> p g c", g=4)
                nc.scalar.copy(qk_tok[:, 1, 4 * z:4 * z + 4, 0:NOPE], kv[:, :, 0:NOPE])
                nc.scalar.copy(v_tok[:, 2 * z:2 * z + 2, :, :].rearrange("p t h v -> p (t h) v"), kv[:, :, NOPE:]).then_inc(free[aj[("kv", z)][0]], 1)
            act.wait_ge(rope_in, 1)
            act.drain()
            nc.scalar.activation(qk_sq.rearrange("p a b c -> p (a b c)"), qk_tok.rearrange("p a b c -> p (a b c)"), ACT.Square).then_inc(qksq_ready, 1)
            for h in range(2):
                b = job_full(act, aj, ("T", h, 0))
                nc.scalar.copy(qkT[h][0][0:QK, :], b[0:QK, :]).then_inc(free[aj[("T", h, 0)][0]], 1)
            for h in range(2):
                for t in range(NT):
                    n = NT * h + t
                    act.wait_ge(max_ready, n + 1)
                    b = job_full(act, aj, ("S", h, t))
                    nc.scalar.activation(prob[h][:, t, :], b[:, :], ACT.Exp, bias=nmx[:, n:n + 1], scale=SCALE,
                                         accum_out=lsum[:, n:n + 1])
                    act.drain().then_inc(free[aj[("S", h, t)][0]], 1)
            for h in range(2):
                for t in (0, 2):
                    b = job_full(act, aj, ("PT", h, t))
                    nc.scalar.copy(probT[h][:, t, :], b[:, :]).then_inc(free[aj[("PT", h, t)][0]], 1)
                b = job_full(act, aj, ("o", h))
                q = slice(h * VH, (h + 1) * VH)
                nc.scalar.copy(hT[q, bass.ds(it, 1), :].rearrange("p a s -> p (a s)"), b[q, :]).then_inc(free[aj[("o", h)][0]], 1)

        def attn_pool(pool, it):
            nc.gpsimd.tensor_copy(qk_tok[:, 1, :, NOPE:].rearrange("p (t h) c -> p t h c", h=2),
                                  k_rope.unsqueeze(2).to_broadcast([P, NT, 2, ROPE])).then_inc(rope_in, 1)
            pool.wait_ge(qkss_ready, 1)
            nc.gpsimd.tensor_scalar(ss16, ss16, 1.0 / QK, NORM_EPS, ALU.mult, ALU.add)
            pool.drain()
            nc.gpsimd.tensor_tensor(rstd16, ss16, mhalf, ALU.pow).then_inc(qkrstd_ready, 1)

        def attn_dve(dve, it):
            dve.wait_ge(qksq_ready, 1)
            nc.vector.tensor_reduce(ss16, qk_sq.rearrange("p a b c -> p (a b) c"), AX, ALU.add).then_inc(qkss_ready, 1)
            dve.drain()
            nc.vector.tensor_tensor(qk_tok, qk_tok, head_gain.unsqueeze(2).to_broadcast([P, 2, 8, QK]), ALU.mult)
            dve.wait_ge(qkrstd_ready, 1)
            dve.drain()
            qkf = qk_tok.rearrange("p a b c -> p (a b) c")
            nc.vector.tensor_tensor(qkf, qkf, rstd16.unsqueeze(2).to_broadcast([P, 16, QK]), ALU.mult)
            dve.drain()
            x1, x2 = qk_tok[:, :, :, NOPE:NOPE + HALF], qk_tok[:, :, :, NOPE + HALF:]
            c, s = (v.unsqueeze(1).to_broadcast([P, 2, 8, HALF]) for v in (cos8, sin8))
            for o, x, y in ((0, x1, c), (1, x2, s), (2, x2, c), (3, x1, s)):
                nc.vector.tensor_tensor(rtmp[o], x, y, ALU.mult)
            dve.drain()
            nc.vector.tensor_tensor(x1, rtmp[0], rtmp[1], ALU.subtract)
            nc.vector.tensor_tensor(x2, rtmp[2], rtmp[3], ALU.add)
            dve.drain().then_inc(qk_ready, 1)
            for h in range(2):
                b = job_full(dve, aj, ("T", h, 1))
                nc.vector.tensor_copy(qkT[h][1][0:QK, :], b[0:QK, :]).then_inc(free[aj[("T", h, 1)][0]], 1)

            def normed(h, t):
                n = NT * h + t
                job_read(dve, aj, ("S", h, t))
                nc.vector.reciprocal(linv[:, n:n + 1], lsum[:, n:n + 1])
                dve.drain()
                nc.vector.tensor_scalar(prob[h][:, t, :], prob[h][:, t, :], linv[:, n:n + 1], None, ALU.mult).then_inc(prob_ready, 1)

            order = [(h, t) for h in range(2) for t in range(NT)]
            for n, (h, t) in enumerate(order):
                b = job_full(dve, aj, ("S", h, t))
                nc.vector.tensor_reduce(mx[:, n:n + 1], b[:, :], AX, ALU.max)
                dve.drain()
                nc.vector.tensor_scalar(nmx[:, n:n + 1], mx[:, n:n + 1], -SCALE, None, ALU.mult).then_inc(max_ready, 1)
                if n >= 2:
                    normed(*order[n - 2])
            normed(*order[-2])
            normed(*order[-1])
            for h in range(2):
                for t in (1, 3):
                    b = job_full(dve, aj, ("PT", h, t))
                    nc.vector.tensor_copy(probT[h][:, t, :], b[:, :]).then_inc(free[aj[("PT", h, t)][0]], 1)

        def attn_loads(sp, it):
            sp.dma_start(wq_sl, a["mla_w_uq"][0].rearrange("(k p) n -> p k n", p=P)[:, :, bass.ds(it * (2 * QK), 2 * QK)]).then_inc(ld_pair2, 16)
            sp.dma_start(wkv_sl, a["mla_w_ukv"][0].rearrange("(k p) n -> p k n", p=P)[:, :, bass.ds(it * (2 * (NOPE + VH)), 2 * (NOPE + VH))]).then_inc(ld_pair2, 16)

        @block.gpsimd
        def _(pool):
            nc.gpsimd.memset(ident[:, :], 0.0)
            nc.gpsimd.memset(mhalf, -0.5)
            pool.drain()
            nc.gpsimd.affine_select(out=ident[:, :], in_=ident[:, :], compare_op=ALU.not_equal, fill=1.0,
                                    base=0, pattern=[[-1, P]], channel_multiplier=1)
            meet_pool(pool)
            norm_pool(pool)
            meet_pool(pool)
            meet_pool(pool, ("pe", "act", "dve", "sp"))
            masks_pool(pool)
            meet_pool(pool)
            with pool.Fori(0, NPAIR) as it:
                pair_pool(pool, it)
                meet_pool(pool, ("pe", "act", "dve", "sp"))
            for layer in range(2):
                if layer == 1:
                    norm_pool(pool)
                    meet_pool(pool)
                    mla_in_pool(pool)
                    meet_pool(pool, ("pe", "act", "dve", "sp"))
                    with pool.Fori(0, NPAIR) as it:
                        attn_pool(pool, it)
                        meet_pool(pool, ("pe", "act", "dve", "sp"))
                else:
                    meet_pool(pool, ("pe", "act", "dve", "sp"))
                meet_pool(pool)
                norm_pool(pool)
                meet_pool(pool)
                route_pool(pool)
                meet_pool(pool, credit=1)
                meet_pool(pool, ("pe", "act", "dve", "sp"))

        @block.tensor
        def _(pe):
            meet(pe, "pe")
            norm_pe(pe)
            meet(pe, "pe")
            pre_pe(pe)
            meet(pe, "pe")
            meet(pe, "pe")
            with pe.Fori(0, NPAIR) as it:
                pair_pe(pe, it)
                meet(pe, "pe")
            for layer in range(2):
                if layer == 1:
                    norm_pe(pe)
                    meet(pe, "pe")
                    mla_in_pe(pe)
                    meet(pe, "pe")
                    with pe.Fori(0, NPAIR) as it:
                        attn_pe(pe, it)
                        meet(pe, "pe")
                else:
                    meet(pe, "pe")
                out_pe(pe, layer)
                meet(pe, "pe")
                norm_pe(pe)
                meet(pe, "pe")
                route_pe(pe, layer)
                meet(pe, "pe")
                with pe.Fori(0, NE // 2) as it:
                    moe_pe(pe, it, layer)
                meet(pe, "pe")

        @block.scalar
        def _(act):
            meet(act, "act")
            norm_act(act, True)
            meet(act, "act")
            pre_act(act)
            meet(act, "act")
            meet(act, "act")
            with act.Fori(0, NPAIR) as it:
                pair_act(act, it)
                meet(act, "act")
            for layer in range(2):
                if layer == 1:
                    norm_act(act, False)
                    meet(act, "act")
                    mla_in_act(act)
                    meet(act, "act")
                    with act.Fori(0, NPAIR) as it:
                        attn_act(act, it)
                        meet(act, "act")
                else:
                    nc.scalar.copy(yT[:, 0:4, :], y_all[:, 0:4, :])
                    meet(act, "act")
                meet(act, "act")
                norm_act(act, False)
                meet(act, "act")
                route_act(act)
                meet(act, "act")
                with act.Fori(0, NE // 2) as it:
                    moe_act(act, it)
                meet(act, "act")

        @block.vector
        def _(dve):
            meet(dve, "dve")
            norm_dve(dve, 0)
            meet(dve, "dve")
            pre_dve(dve)
            meet(dve, "dve")
            masks_dve(dve)
            meet(dve, "dve")
            with dve.Fori(0, NPAIR) as it:
                pair_dve(dve, it)
                meet(dve, "dve")
            for layer in range(2):
                if layer == 1:
                    norm_dve(dve, 2)
                    meet(dve, "dve")
                    mla_in_dve(dve)
                    meet(dve, "dve")
                    with dve.Fori(0, NPAIR) as it:
                        attn_dve(dve, it)
                        meet(dve, "dve")
                else:
                    nc.vector.tensor_copy(yT[:, 4:8, :], y_all[:, 4:8, :])
                    meet(dve, "dve")
                out_dve(dve, layer)
                meet(dve, "dve")
                norm_dve(dve, 2 * layer + 1)
                meet(dve, "dve")
                route_dve(dve)
                meet(dve, "dve")
                dve.sem_inc(pick_ready, 1)
                with dve.Fori(0, NE // 2) as it:
                    moe_dve(dve, it)
                meet(dve, "dve")

        @block.sync
        def _(sp):
            load_x(sp, ld_x)
            load_gain(sp, 0)
            for dst, w in ((w1_sb, "rw_w1"), (a1_sb, "rw_a1")):
                for e in range(2):
                    sp.dma_start(dst[:, :, e * LORA:(e + 1) * LORA], a[w][0, e].rearrange("(k p) n -> p k n", p=P)).then_inc(ld_lora, 16)
            for lo, hi in ((0, GATE // 2), (GATE // 2, GATE)):
                sp.dma_start(g1_sb[:, :, lo:hi], a["rw_g1"][0].rearrange("(k p) n -> p k n", p=P)[:, :, lo:hi]).then_inc(ld_lora, 16)
            rows = [(V_MU, a["rw_mu"][0].rearrange("g (k p) -> (g k) p", p=P), 6), (V_KK, a["rw_kk"][0].rearrange("(k p) -> k p", p=P), 1),
                    (V_KA, a["rw_ka"][0].rearrange("(k p) -> k p", p=P), 1), (V_W0, a["rw_w0"][0].rearrange("g (k p) -> (g k) p", p=P), 2),
                    (V_A0, a["rw_a0"][0].rearrange("g (k p) -> (g k) p", p=P), 2), (V_GNG, a["rw_gn_g"][0].rearrange("(k p) -> k p", p=P), 1),
                    (V_GNB, a["rw_gn_b"][0].rearrange("(k p) -> k p", p=P), 1), (V_RK, a["rw_rk"][0].rearrange("(k u) j -> k (u j)", u=2), 1)]
            for at, src, n in rows:
                sp.dma_start(vec_rows[at * ND:(at + n) * ND, :], src).then_inc(ld_vec, 16)
            meet(sp, "sp")
            pair_loads(sp, 0)
            with sp.Fori(0, NPAIR) as it:
                sp.wait_ge(full[rj["g"][0]], 1)
                pair_loads(sp, (it + 1) & (NPAIR - 1))
                meet(sp, "sp")
            sp.wait_ge(ld_pair, 16 * 7 * (NPAIR + 1))
            meet(sp, "sp")
            load_x(sp, ld_x2)
            wo = [a[w][0].rearrange("(k p) n -> p k n", p=P) for w in ("rw_wo", "mla_w_o")]
            router = [a["moe_router"][n].rearrange("(k p) n -> p k n", p=P) for n in range(2)]
            sp.dma_start(wo_sb, wo[0]).then_inc(ld_wo[0], 16)
            load_gain(sp, 1)
            sp.dma_start(router_sb, router[0]).then_inc(ld_router[0], 16)
            load_experts(sp, 0)
            meet(sp, "sp")
            load_gain(sp, 2)
            sp.dma_start(win_sb, a["mla_w_in"][0].rearrange("(k p) n -> p k n", p=P)).then_inc(ld_win, 16)
            sp.dma_start(norm_rows[0:QL // P, :], a["mla_q_norm_g"][0].rearrange("(k p) -> k p", p=P)).then_inc(ld_mla, 16)
            sp.dma_start(norm_rows[QL // P:(QL + KVL) // P, :], a["mla_kv_norm_g"][0].rearrange("(k p) -> k p", p=P)).then_inc(ld_mla, 16)
            sp.dma_start(head_gain[:, 0, :], a["mla_q_head_g"][0:1, :].to_broadcast([P, QK])).then_inc(ld_mla, 16)
            sp.dma_start(head_gain[:, 1, :], a["mla_k_head_g"][0:1, :].to_broadcast([P, QK])).then_inc(ld_mla, 16)
            sp.dma_start(pos_i, a["positions"][0].rearrange("(t p) -> p t", p=P), allow_slow_non_contiguous=True).then_inc(ld_mla, 16)
            attn_loads(sp, 0)
            meet(sp, "sp")
            sp.dma_start(wo_sb, wo[1]).then_inc(ld_wo[1], 16)
            load_gain(sp, 3)
            sp.dma_start(router_sb, router[1]).then_inc(ld_router[1], 16)
            with sp.Fori(0, NPAIR) as it:
                sp.wait_ge(full[aj[("kv", 1)][0]], aj[("kv", 1)][1])
                attn_loads(sp, (it + 1) & (NPAIR - 1))
                meet(sp, "sp")
            sp.wait_ge(ld_pair2, 32 * (NPAIR + 1))
            load_experts(sp, 1)
            meet(sp, "sp")
            o = a["out"][0].rearrange("(t p) d -> p t d", p=P)
            for t in range(NT):
                sp.dma_start(o[:, t, :], x_sb[:, t, :]).then_inc(stored, 16)
            sp.wait_ge(stored, 16 * NT)


_INS = ['x', 'positions', 'norm_mix_g', 'norm_ffn_g', 'rw_mu', 'rw_wr', 'rw_wk', 'rw_wv', 'rw_wo', 'rw_w0', 'rw_w1',
        'rw_w2', 'rw_a0', 'rw_a1', 'rw_a2', 'rw_g1', 'rw_g2', 'rw_kk', 'rw_ka', 'rw_rk', 'rw_gn_g', 'rw_gn_b',
        'mla_w_in', 'mla_q_norm_g', 'mla_kv_norm_g', 'mla_w_uq', 'mla_w_ukv', 'mla_q_head_g', 'mla_k_head_g',
        'mla_w_o', 'moe_router', 'moe_w_gate', 'moe_w_up', 'moe_w_down']


def kernel(**inputs):
    import concourse.bacc as bacc
    from concourse.bass_utils import run_bass_kernel_spmd

    nc = bacc.Bacc("TRN2", target_bir_lowering=False, num_devices=1)
    arrays, args = {}, {}
    for name in _INS:
        arrays[f"in_{name}"] = np.ascontiguousarray(inputs[name])
        args[name] = nc.dram_tensor(f"in_{name}", arrays[f"in_{name}"].shape, mybir.dt.from_np(arrays[f"in_{name}"].dtype),
                                    kind="ExternalInput").ap()
    args["out"] = nc.dram_tensor("out_dram", (1, S, D), F32, kind="ExternalOutput").ap()
    trunk(nc, args)
    r = run_bass_kernel_spmd(nc, [arrays], core_ids=[0])
    return r.results[0]["out_dram"]
```

```python
from contextlib import ExitStack

import numpy as np

import concourse.bass as bass
from concourse import mybir

F32 = mybir.dt.float32
I32 = mybir.dt.int32
ALU = mybir.AluOpType
ACT = mybir.ActivationFunctionType
AX = mybir.AxisListType.X

P = 128
D = 1024
S = 512
NT = S // P
ND = D // P
NORM_EPS = 1e-6
HEAD = 64
LORA = 64
GATE = 160
GN_EPS = 64e-5
NPAIR = D // (2 * HEAD)
DECAY = -float(np.exp(-0.5))
LEVELS = 7
NOPE = 64
ROPE = 32
VH = 64
QL = 384
KVL = 256
QK = NOPE + ROPE
HALF = ROPE // 2
THETA = 10000.0
NE = 16
FF = 1024
CAP = 2 * S // NE
NB = 8
RING = 6
CHUNK = ND * 512
CPP = 12

V_MU, V_KK, V_KA, V_W0, V_A0, V_GNG, V_GNB, V_RK, V_N = 0, 6, 7, 8, 10, 12, 13, 14, 15


class Jobs:

    def __init__(self, order):
        self.at, self.count = {}, [0] * NB
        for name, bank in order:
            self.count[bank] += 1
            self.at[name] = (bank, self.count[bank])

    def __getitem__(self, name):
        return self.at[name]


def trunk(nc, a):
    with ExitStack() as ctx:
        sem = lambda name: ctx.enter_context(nc.semaphore(name))
        sb = lambda name, shape, dt=F32: ctx.enter_context(nc.sbuf_tensor(name, shape, dt))

        ARENA = 51 * 1024
        arena = sb("arena", [P, ARENA])
        ident = sb("ident", [P, P])
        small = sb("small", [P, 640])
        small_at = [0]

        def tiny(n):
            o = small_at[0]
            small_at[0] += n
            assert small_at[0] <= 640
            return small[:, o:o + n]

        def place(start):
            at = [start]

            def take(*shape):
                n = int(np.prod(shape))
                v = arena[:, at[0]:at[0] + n]
                at[0] += n
                assert at[0] <= ARENA, at[0]
                if len(shape) > 1:
                    names = "abcde"[:len(shape)]
                    v = v.rearrange(f"p ({' '.join(names)}) -> p {' '.join(names)}",
                                    **{c: s for c, s in zip(names, shape)})
                return v
            take.at = at
            return take

        ps = [ctx.enter_context(nc.psum_tensor(f"bank{b}", [P, 512], F32)) for b in range(NB)]

        RING0 = ARENA - RING * CHUNK
        ring = [arena[:, RING0 + s * CHUNK:RING0 + (s + 1) * CHUNK].rearrange("p (k n) -> p k n", k=ND)
                for s in range(RING)]
        common = place(0)
        x_sb = common(NT, D)

        h_tok = common(NT, D)
        hT = common(ND, S)
        AFTER_H = common.at[0]

        pre = place(AFTER_H)
        gain_row = pre(D)
        vec_rows = pre(P)
        w1_sb = pre(ND, 2 * LORA)
        a1_sb = pre(ND, 2 * LORA)
        g1_sb = pre(ND, GATE)
        keep = place(ARENA - (3 * ND * S + 4 * S + NPAIR * S))
        xmix = [keep(ND, S) for _ in range(3)]
        lora_w = keep(S)
        lora_a = keep(S)
        gate_a, gate_b = keep(S), keep(S)
        y_all = keep(NPAIR, S)
        assert pre.at[0] <= ARENA - (3 * ND * S + 4 * S + NPAIR * S)
        shift = h_tok.rearrange("p t d -> p (t d)").rearrange("p (k s) -> p k s", k=ND)

        body = place(0)
        w_sl = body(3, ND, P)
        w2_sl, a2_sl, g2a_sl, g2b_sl = body(P), body(P), body(P), body(P)
        strict_incl = [body(2, P) for _ in range(2)]
        level_mask = body(LEVELS, P)
        head_ones = body(P)
        rT, kT, vT, kkn, kraw, tw, ta, cs, cx, e_neg, rk_cols = (body(S) for _ in range(11))
        Bt = [body(NT, P) for _ in range(2)]
        Kt = [body(NT, P) for _ in range(2)]
        AR = [[body(NT, 2, P) for _ in range(2)] for _ in range(2)]
        btok = [body(NT, P) for _ in range(2)]
        ktok = [body(NT, P) for _ in range(2)]
        vtok = body(NT, P)
        LT = [body(NT, P) for _ in range(2)]
        RB = [[body(NT, P) for _ in range(2)] for _ in range(2)]
        MTRK = [[body(NT, 2, P) for _ in range(2)] for _ in range(2)]
        TT = [[body(NT, P) for _ in range(2)] for _ in range(2)]
        Tm = [body(NT, P) for _ in range(2)]
        Xm = [body(NT, P) for _ in range(2)]
        bonus = [body(S) for _ in range(2)]
        gT, ytok_flat, ysq = body(S), body(S), body(S)
        assert body.at[0] <= ARENA - (3 * ND * S + 4 * S + NPAIR * S), (body.at[0], ARENA - (3 * ND * S + 4 * S + NPAIR * S))
        chain_x = Xm[0].rearrange("p m j -> p (m j)")[:, 0:256].rearrange("p (h d v) -> p h d v", h=2, d=2)
        chain_u = Xm[0].rearrange("p m j -> p (m j)")[:, 256:512].rearrange("p (h d v) -> p h d v", h=2, d=2)
        flat_x1 = Xm[1].rearrange("p m j -> p (m j)")
        states = [flat_x1[:, z * 128:(z + 1) * 128].rearrange("p (d v) -> p d v", d=2) for z in range(2)]
        state_dec = flat_x1[:, 256:384].rearrange("p (d v) -> p d v", d=2)
        ytok = ytok_flat.rearrange("p (t h v) -> p t h v", t=NT, h=2)

        cols = tiny(V_N * ND)
        pc = tiny(V_N)
        half_col = tiny(2 * 2)
        end_dec = [tiny(2 * NT).rearrange("p (d m) -> p d m", d=2) for _ in range(2)]
        stat = tiny(8)
        stat2 = tiny(8)
        rstd8 = tiny(8)
        rstd16 = tiny(16)
        mhalf = tiny(16)
        ssum = tiny(4)
        rstd4 = tiny(4)
        iota_s = tiny(CAP)

        proj = place(AFTER_H + D)
        wo_sb = proj(ND, D)
        assert proj.at[0] <= RING0
        yT = hT

        moe = place(AFTER_H + D)
        xeT = moe(ND, 2 * CAP)
        hidT = [moe(ND, CAP) for _ in range(2)]
        hid_tok = [moe(FF) for _ in range(2)]
        th = [moe(512) for _ in range(2)]
        ye = moe(D)
        combT = moe(S)
        pick = moe(NT, 2 * CAP)
        pick_gate = moe(NT, 2 * CAP)
        aff = moe(NT, NE + 2)
        slot = moe(NT, NE + 2)
        affT, workT, maskT, cumT = moe(S), moe(S), moe(S), moe(S)
        top8 = moe(8)
        logit = moe(NT, NE)
        iota_i = moe(CAP).bitcast(I32)
        assert max(proj.at[0], moe.at[0]) <= RING0 - ND * NE
        router_sb = arena[:, RING0 - ND * NE:RING0].rearrange("p (k n) -> p k n", k=ND)

        hbuf = place(NT * D)
        prob_at = hbuf.at[0] + NT * S
        prob = [hbuf(NT, S) for _ in range(2)]
        inp = place(AFTER_H + D)
        win_sb = inp(ND, QL + KVL + ROPE)
        c_tok = inp(NT, QL + KVL + ROPE)
        mla = place(AFTER_H + D + ND * D)
        assert inp.at[0] <= mla.at[0]
        cT = mla((QL + KVL) // P, S)
        wq_sl = mla(QL // P, 2 * QK)
        wkv_sl = mla(KVL // P, 2 * (NOPE + VH))
        qk_tok = mla(2, NT * 2, QK)
        qk_sq = arena[:, prob_at:prob_at + 2 * NT * 2 * QK].rearrange("p (a b c) -> p a b c", a=2, b=NT * 2)
        v_tok = mla(NT, 2, VH)
        qkT = [[mla(S) for _ in range(2)] for _ in range(2)]
        probT = [mla(NT, S) for _ in range(2)]
        norm_rows = mla(P)
        head_gain = mla(2, QK)
        k_rope = mla(NT, ROPE)
        cos8, sin8 = mla(NT * 2, HALF), mla(NT * 2, HALF)
        ang, red, rnd = mla(NT, HALF), mla(NT, HALF), mla(NT, HALF)
        freq = mla(HALF)
        pos_f = mla(NT)
        pos_i = mla(NT).bitcast(I32)
        rtmp = [qk_sq.rearrange("p a b c -> p (a b c)")[:, z * 256:(z + 1) * 256].rearrange("p (a b c) -> p a b c", a=2, b=8)
                for z in range(4)]
        norm_cols = tiny(8)
        ss_c = tiny(8)
        rstd_c = tiny(8)
        ss16 = tiny(16)
        mx = tiny(8)
        nmx = tiny(8)
        lsum = tiny(8)
        linv = tiny(8)
        rmax = tiny(NT)
        rsum_t = tiny(NT)

        full = [sem(f"bank_full{b}") for b in range(NB)]
        free = [sem(f"bank_free{b}") for b in range(NB)]
        sq_ready = sem("squares_summed")
        rstd_ready = sem("rstd_ready")
        h_ready = sem("h_ready")
        consts_ready = sem("consts_ready")
        mix_ready = sem("mix_ready")
        mix_used = sem("mix_used")
        gate_ready = sem("gate_ready")
        cols_ready = sem("pair_cols_ready")
        ksq_ready = sem("ksq_ready")
        knorm_clamped = sem("knorm_clamped")
        knorm_root = sem("knorm_root")
        cum_ready = sem("cumulated_ready")
        exps_ready = sem("exps_ready")
        operands_ready = sem("operands_ready")
        ydone_ready = sem("y_done")
        ttinit_ready = sem("inverse_t_started")
        state_ready = sem("state_ready")
        ycen_ready = sem("y_centred")
        ysq_ready = sem("y_squares")
        yvar_ready = sem("y_variance")
        yrstd_ready = sem("y_rstd")
        ynorm_ready = sem("y_normed")
        yfeat_ready = sem("y_feature_major")
        moved = sem("moved")
        logit_ready = sem("logit_ready")
        exp_ready = sem("exp_ready")
        aff_ready = sem("aff_ready")
        slot_ready = sem("slot_ready")
        iota_ready = sem("iota_ready")
        pick_ready = sem("pick_ready")
        tanh_ready = sem("tanh_ready")
        hid_ready = sem("hid_ready")
        css_ready = sem("css_ready")
        crstd_ready = sem("crstd_ready")
        cnorm_ready = sem("cnorm_ready")
        red_ready = sem("angles_reduced")
        trig_ready = sem("trig_ready")
        freq_ready = sem("freq_ready")
        rope_in = sem("rope_in")
        qksq_ready = sem("qksq_ready")
        qkss_ready = sem("qkss_ready")
        qkrstd_ready = sem("qkrstd_ready")
        qk_ready = sem("qk_ready")
        max_ready = sem("max_ready")
        prob_exp = sem("prob_exp")
        prob_ready = sem("prob_ready")
        stage_sems = [sq_ready, rstd_ready, h_ready, consts_ready, mix_ready, mix_used, gate_ready,
                      cols_ready, ksq_ready, knorm_clamped, knorm_root, cum_ready,
                      exps_ready, operands_ready, ydone_ready, ttinit_ready, state_ready,
                      ycen_ready, ysq_ready, yvar_ready, yrstd_ready, ynorm_ready, yfeat_ready, moved,
                      logit_ready, exp_ready, aff_ready, slot_ready, iota_ready, pick_ready, tanh_ready, hid_ready,
                      css_ready, crstd_ready, cnorm_ready, red_ready, trig_ready, freq_ready, rope_in,
                      qksq_ready, qkss_ready, qkrstd_ready, qk_ready, max_ready, prob_exp, prob_ready]
        arrive = sem("arrive")
        arrive_sp = sem("arrive_sp")
        go = {e: sem(f"go_{e}") for e in ("pe", "act", "dve", "sp")}
        ld_x = sem("ld_x")
        ld_x2 = sem("ld_x2")
        ld_gain = [sem(f"ld_gain{n}") for n in range(4)]
        ld_vec = sem("ld_vec")
        ld_lora = sem("ld_lora")
        ld_pair = sem("ld_pair")
        ld_gate = sem("ld_gate")
        ld_wo = [sem(f"ld_wo{n}") for n in range(2)]
        ld_router = [sem(f"ld_router{n}") for n in range(2)]
        ld_chunk = [sem(f"ld_chunk{s}") for s in range(RING)]
        ld_win = sem("ld_win")
        ld_mla = sem("ld_mla")
        ld_pair2 = sem("ld_pair2")
        stored = sem("stored")
        waited, waited_sp = sem("waited"), sem("waited_sp")
        chunk_used = [sem(f"chunk_used{n}") for n in range(2)]

        block = ctx.enter_context(nc.Block())

        def meet(eng, name):
            eng.drain().then_inc(arrive_sp if name == "sp" else arrive, 1)
            eng.wait_ge(go[name], 1)
            eng.sem_clear(go[name])

        def meet_pool(pool, names=("pe", "act", "dve"), credit=0):
            pool.drain()
            pool.wait_ge(arrive, 3)
            pool.sem_clear(arrive)
            if "sp" in names:
                pool.wait_ge(arrive_sp, 1)
                pool.sem_clear(arrive_sp)
            for s in full + free + stage_sems:
                pool.sem_clear(s)
            if credit:
                for s in free:
                    pool.sem_inc(s, credit)
            for n in names:
                pool.sem_inc(go[n], 1)

        def open_job(pe, jobs, name):
            b, n = jobs[name]
            if n > 1:
                pe.wait_ge(free[b], n - 1)
            return ps[b]

        def job_full(eng, jobs, name):
            b, n = jobs[name]
            eng.wait_ge(full[b], n)
            return ps[b]

        def job_read(eng, jobs, name):
            b, n = jobs[name]
            eng.wait_ge(free[b], n)

        norm_jobs = Jobs([(k, k) for k in range(ND)])

        def norm_act(act, x_loaded):
            if x_loaded:
                act.wait_ge(ld_x, 16 * NT)
            for t in range(NT):
                nc.scalar.activation(h_tok[:, t, :], x_sb[:, t, :], ACT.Square,
                                     accum_out=ssum[:, t:t + 1]).then_inc(sq_ready, 1)
            for k in range(0, ND, 2):
                b = job_full(act, norm_jobs, k)
                nc.scalar.copy(hT[:, k, :], b[:, :]).then_inc(free[norm_jobs[k][0]], 1)

        def norm_pool(pool):
            pool.wait_ge(sq_ready, NT)
            nc.gpsimd.tensor_scalar(ssum, ssum, 1.0 / D, NORM_EPS, ALU.mult, ALU.add)
            pool.drain()
            nc.gpsimd.tensor_tensor(rstd4, ssum, mhalf[:, 0:4], ALU.pow).then_inc(rstd_ready, 1)

        def norm_dve(dve, n):
            dve.wait_ge(ld_gain[n], 16)
            dve.wait_ge(rstd_ready, 1)
            for t in range(NT):
                nc.vector.scalar_tensor_tensor(h_tok[:, t, :], x_sb[:, t, :], rstd4[:, t:t + 1], gain_row,
                                               ALU.mult, ALU.mult).then_inc(h_ready, 1)
            for k in range(1, ND, 2):
                b = job_full(dve, norm_jobs, k)
                nc.vector.tensor_copy(hT[:, k, :], b[:, :]).then_inc(free[norm_jobs[k][0]], 1)

        def norm_pe(pe):
            pe.wait_ge(h_ready, NT)
            for k in range(ND):
                b = open_job(pe, norm_jobs, k)
                for t in range(NT):
                    last = nc.tensor.transpose(b[:, t * P:(t + 1) * P], h_tok[:, t, k * P:(k + 1) * P], ident[:, :])
                last.then_inc(full[norm_jobs[k][0]], 1)

        MIX = [(1, 0), (4, 1), (5, 2), (0, 0), (2, 1), (3, 2)]
        pre_jobs = Jobs([("cols", 0), ("w", 1), ("a", 2), ("ga", 3), ("gb", 4)])

        def pre_pe(pe):
            pe.wait_ge(ld_vec, 16 * 8)
            nc.tensor.transpose(ps[0][:, 0:V_N * ND], vec_rows[0:V_N * ND, :],
                                ident[0:V_N * ND, 0:V_N * ND]).then_inc(full[0], 1)
            pe.wait_ge(ld_lora, 16 * 6)
            for n, (name, w, m) in enumerate([("w", w1_sb, P), ("a", a1_sb, P), ("ga", g1_sb, P), ("gb", g1_sb, GATE - P)]):
                src = xmix[min(n, 2)]
                pe.wait_ge(mix_ready, ND * (min(n, 2) + 1))
                b = open_job(pe, pre_jobs, name)
                lo = P if name == "gb" else 0
                for k in range(ND):
                    last = nc.tensor.matmul(b[0:m, :], w[:, k, lo:lo + m], src[:, k, :],
                                            start=(k == 0), stop=(k == ND - 1))
                last.then_inc(full[pre_jobs[name][0]], 1)

        def pre_act(act):
            for name, dst, m, f in (("w", lora_w, P, ACT.Tanh), ("a", lora_a, P, ACT.Copy)):
                b = job_full(act, pre_jobs, name)
                nc.scalar.activation(dst[0:m, :], b[0:m, :], f).then_inc(free[pre_jobs[name][0]], 1)
            for name, dst, m in (("ga", gate_a, P), ("gb", gate_b, GATE - P)):
                b = job_full(act, pre_jobs, name)
                nc.scalar.activation(dst[0:m, :], b[0:m, :], ACT.Tanh, scale=0.5).then_inc(gate_ready, 1)

        def pre_dve(dve):
            job_full(dve, pre_jobs, "cols")
            nc.vector.tensor_copy(cols, ps[0][:, 0:V_N * ND])
            nc.vector.tensor_tensor(shift[:, :, 1:S - 1], hT[:, :, 0:S - 2], hT[:, :, 2:S], ALU.add)
            nc.vector.tensor_copy(shift[:, :, 0:1], hT[:, :, 1:2])
            nc.vector.tensor_copy(shift[:, :, S - 1:S], hT[:, :, S - 2:S - 1])
            dve.drain()
            for k in range(ND):
                nc.vector.scalar_tensor_tensor(shift[:, k, :], shift[:, k, :], 0.5, hT[:, k, :], ALU.mult, ALU.subtract)
            dve.drain()
            for n, (row, buf) in enumerate(MIX):
                if n >= 3:
                    dve.wait_ge(full[pre_jobs[("w", "a", "gb")[n - 3]][0]], 1)
                for k in range(ND):
                    nc.vector.scalar_tensor_tensor(xmix[buf][:, k, :], shift[:, k, :],
                                                   cols[:, (V_MU + row) * ND + k:(V_MU + row) * ND + k + 1],
                                                   hT[:, k, :], ALU.mult, ALU.add).then_inc(mix_ready, 1)
            dve.wait_ge(gate_ready, 2)
            nc.vector.tensor_scalar(gate_a, gate_a, 0.5, 0.5, ALU.mult, ALU.add)
            nc.vector.tensor_scalar(gate_b[0:GATE - P, :], gate_b[0:GATE - P, :], 0.5, 0.5, ALU.mult, ALU.add)

        ii, jj = cs.bitcast(I32), cx.bitcast(I32)

        def masks_pool(pool):
            nc.gpsimd.iota(ii[:, 0:P], [[0, P]], base=0, channel_multiplier=1)
            nc.gpsimd.iota(jj[:, 0:P], [[1, P]], base=0, channel_multiplier=0)
            for m in (strict_incl[0], strict_incl[1]):
                nc.gpsimd.memset(m, 1.0)
            pool.drain()
            for d, sgn in ((0, 1), (1, -1)):
                for z in range(2):
                    v = strict_incl[d][:, z, :]
                    nc.gpsimd.affine_select(out=v, in_=v, compare_op=ALU.is_ge, fill=0.0, base=z - 1,
                                            pattern=[[sgn, P]], channel_multiplier=-sgn)
            pool.drain().then_inc(consts_ready, 1)

        def masks_dve(dve):
            dve.wait_ge(consts_ready, 1)
            nc.vector.tensor_tensor(ii[:, P:2 * P], ii[:, 0:P], jj[:, 0:P], ALU.bitwise_xor)
            dve.drain()
            xor = cs[:, 2 * P:3 * P]
            nc.vector.tensor_copy(xor, ii[:, P:2 * P])
            dve.drain()
            nc.vector.tensor_scalar(head_ones, xor, float(HEAD), None, ALU.is_lt)
            for n in range(LEVELS):
                nc.vector.tensor_scalar(cx[:, P:2 * P], xor, float(2 ** (n + 1)), None, ALU.is_lt)
                dve.drain()
                nc.vector.scalar_tensor_tensor(level_mask[:, n, :], xor, float(2 ** n), cx[:, P:2 * P],
                                               ALU.is_ge, ALU.mult)
                dve.drain()

        WITH = {("lv", 0, 1): [("r",)], ("lv", 0, 2): [("k",)], ("lv", 0, 3): [("kn",)], ("lv", 0, 4): [("wa", 0), ("kkn",)],
                ("lv", 0, 5): [("cum", 0)], ("lv", 0, 6): [("rate", 0)],
                ("lv", 1, 1): [("ops", 0)], ("lv", 1, 2): [("wa", 1)], ("lv", 1, 3): [("cum", 1)], ("lv", 1, 4): [("rate", 1)],
                ("lv", 1, 5): [("ops", 1)]}
        ALONE = [("r",), ("k",), ("kn",), ("wa", 0), ("kkn",), ("cum", 0), ("rate", 0), ("ops", 0), ("wa", 1), ("cum", 1),
                 ("rate", 1), ("ops", 1)]
        PREP_BANK = {"r": 6, "k": 7, "kn": 6, "w0": 7, "a0": 6, "w1": 7, "a1": 6}

        def prep_jobs(piece, u):
            names = {"r": ["r"], "k": ["k"], "kn": ["kn"]}.get(piece[0])
            if piece[0] == "wa":
                names = [f"w{piece[1]}", f"a{piece[1]}"]
            return [((x, u), PREP_BANK[x]) for x in names or []]

        order = []
        for u in range(2):
            order += [(("bonus", u), 0), (("vt", u), 1), (("bt0", u), 2), (("kt0", u), 3), (("bt1", u), 4), (("kt1", u), 5)]
            for d in range(2):
                rot = 0
                for nm in ("LR0", "LR1", "MR0", "MR1"):
                    for h in range(2):
                        order.append(((nm, d, h, u), rot % 6))
                        rot += 1
                for h in range(2):
                    order.append((("T0", d, h, u), 3 * h + 2))
                for lv in range(1, LEVELS):
                    for h in range(2):
                        order.append((("X", lv, d, h, u), 3 * h))
                    if u == 1 and d == 0 and lv == 1:
                        order.append((("yT", 0), 7))
                    for piece in WITH.get(("lv", d, lv), []):
                        order += prep_jobs(piece, u)
                    for h in range(2):
                        order.append((("TX", lv, d, h, u), 3 * h + 1))
                    if lv < LEVELS - 1:
                        for h in range(2):
                            order.append((("Tr", lv, d, h, u), 3 * h + 2))
            for m in range(NT):
                order += [(("cx", m, 0, u), 1), (("cx", m, 1, u), 2)]
                order += [(("g", u), 0)] if m == 0 else []
                order += [(("cu", m, u), 3)]
                if m < NT - 1:
                    order += [(("cs", m, u), 4)]
            order += [(("v", u), 5), (("y", 0, u), 6), (("y", 1, u), 7)]
        order += [(("yT", 1), 0)]
        rj = Jobs(order)
        alone = []
        for piece in ALONE:
            alone += prep_jobs(piece, 0)
        pj = Jobs(alone + [(("v", 0), 5)])

        def bc(v, *shape):
            return v.to_broadcast(list(shape))

        flat = lambda v: v.rearrange("p m j -> p (m j)")
        split = lambda v: v.rearrange("p (m j) -> p m j", m=NT)

        def prep_pe(pe, piece, jb, u, loads):
            if piece[0] in ("r", "k"):
                n = {"r": 0, "k": 1}[piece[0]]
                if n == 0:
                    pe.wait_ge(ld_pair, loads * (16 * 5))
                b = open_job(pe, jb, (piece[0], u))
                for k in range(ND):
                    last = nc.tensor.matmul(b[:, :], w_sl[:, n, k, :], xmix[n][:, k, :], start=(k == 0), stop=(k == ND - 1))
                last.then_inc(full[jb[(piece[0], u)][0]], 1)
            if piece[0] == "kn":
                b = open_job(pe, jb, ("kn", u))
                pe.wait_ge(ksq_ready, u + 1)
                nc.tensor.matmul(b[:, :], head_ones, kraw, start=True, stop=True).then_inc(full[jb[("kn", u)][0]], 1)
            if piece[0] == "wa":
                d = piece[1]
                q = slice(d * LORA, (d + 1) * LORA)
                for kind, w, src in (("w", w2_sl, lora_w), ("a", a2_sl, lora_a)):
                    b = open_job(pe, jb, (f"{kind}{d}", u))
                    nc.tensor.matmul(b[:, :], w[q, :], src[q, :], start=True, stop=True).then_inc(full[jb[(f"{kind}{d}", u)][0]], 1)

        def v_piece(pe, jb, u, k):
            b = open_job(pe, jb, ("v", u)) if k == 0 else ps[jb[("v", u)][0]]
            last = nc.tensor.matmul(b[:, :], w_sl[:, 2, k, :], xmix[2][:, k, :], start=(k == 0), stop=(k == ND - 1))
            if k == ND - 1:
                last.then_inc(full[jb[("v", u)][0]], 1)

        def prep_act(act, piece, jb, u):
            if piece[0] == "r":
                b = job_full(act, jb, ("r", u))
                nc.scalar.copy(rT, b[:, :]).then_inc(free[jb[("r", u)][0]], 1)
            if piece[0] == "k":
                b = job_full(act, jb, ("k", u))
                act.wait_ge(cols_ready, u + 1)
                nc.scalar.activation(kraw, b[:, :], ACT.Square, scale=pc[:, V_KK:V_KK + 1]).then_inc(ksq_ready, 1)
                nc.scalar.copy(kT, b[:, :]).then_inc(free[jb[("k", u)][0]], 1)
            if piece[0] == "kkn":
                act.wait_ge(knorm_clamped, u + 1)
                nc.scalar.activation(cx, cs, ACT.Sqrt).then_inc(knorm_root, 1)
            if piece[0] == "wa":
                d = piece[1]
                if d == 1:
                    act.wait_ge(operands_ready, 2 * u + 1)
                for kind, dst, hc in (("w", tw, d), ("a", ta, 2 + d)):
                    b = job_full(act, jb, (f"{kind}{d}", u))
                    nc.scalar.activation(dst, b[:, :], ACT.Tanh, bias=half_col[:, hc:hc + 1], scale=0.5).then_inc(free[jb[(f"{kind}{d}", u)][0]], 1)
            if piece[0] == "cum":
                act.wait_ge(cum_ready, 2 * u + piece[1] + 1)
                nc.scalar.activation(e_neg, cs, ACT.Exp, scale=-1.0)
                nc.scalar.activation(cx, cx, ACT.Exp)
                act.drain()
                nc.scalar.activation(cs, cs, ACT.Exp).then_inc(exps_ready, 1)

        def prep_cols(dve, pair):
            nc.vector.tensor_copy(pc.unsqueeze(2), cols.rearrange("p (g q) -> p g q", q=ND)[:, :, bass.ds(pair, 1)])
            dve.drain()
            nc.vector.tensor_scalar(half_col, pc[:, V_W0:V_W0 + 4], 0.5, None, ALU.mult)
            dve.drain().then_inc(cols_ready, 1)

        def prep_dve(dve, piece, jb, u, par):
            d = piece[1] if len(piece) > 1 else 0
            if piece[0] == "kn":
                job_read(dve, jb, ("k", u))
                nc.vector.tensor_scalar(kkn, kT, pc[:, V_KK:V_KK + 1], None, ALU.mult)
                b = job_full(dve, jb, ("kn", u))
                nc.vector.tensor_scalar(cs, b[:, :], 1e-24, None, ALU.max).then_inc(knorm_clamped, 1)
                dve.drain().then_inc(free[jb[("kn", u)][0]], 1)
            if piece[0] == "kkn":
                dve.wait_ge(knorm_root, u + 1)
                nc.vector.reciprocal(cs, cx)
                dve.drain()
                nc.vector.tensor_tensor(kkn, kkn, cs, ALU.mult)
            if piece[0] == "cum":
                job_read(dve, jb, (f"w{d}", u))
                nc.vector.tensor_scalar(tw, tw, 0.5 * DECAY, 0.5 * DECAY, ALU.mult, ALU.add)
                dve.drain()
                for m in range(NT):
                    o, w = cs[:, m * P:(m + 1) * P], tw[:, m * P:(m + 1) * P]
                    if d == 0:
                        nc.vector.tensor_tensor_scan(o, w, w, 0.0, ALU.add, ALU.min)
                    else:
                        nc.vector.tensor_tensor_scan(o[:, ::-1], w[:, ::-1], w[:, ::-1], 0.0, ALU.add, ALU.min)
                dve.drain()
                nc.vector.tensor_tensor(cx, cs, tw, ALU.subtract).then_inc(cum_ready, 1)
            if piece[0] == "rate":
                job_read(dve, jb, (f"a{d}", u))
                nc.vector.tensor_scalar(ta, ta, 0.5, 0.5, ALU.mult, ALU.add)
                dve.drain()
                nc.vector.tensor_scalar(tw, ta, -1.0, pc[:, V_KA:V_KA + 1], ALU.add, ALU.mult)
                nc.vector.tensor_tensor(ta, ta, kkn, ALU.mult)
                dve.drain()
                nc.vector.scalar_tensor_tensor(tw, tw, 1.0, kT, ALU.add, ALU.mult)
                dve.drain()
            if piece[0] == "ops":
                dve.wait_ge(exps_ready, 2 * u + d + 1)
                job_read(dve, jb, ("r", u))
                nc.vector.tensor_tensor(AR[par][d][:, :, 1, :], split(rT), split(cs), ALU.mult)
                nc.vector.scalar_tensor_tensor(AR[par][d][:, :, 0, :], split(kkn), -1.0, split(cx), ALU.mult, ALU.mult)
                nc.vector.tensor_tensor(flat(Bt[d]), ta, e_neg, ALU.mult)
                nc.vector.tensor_tensor(flat(Kt[d]), tw, e_neg, ALU.mult)
                if d == 0:
                    nc.vector.tensor_copy(rk_cols, tw)
                else:
                    nc.vector.tensor_tensor(rk_cols, rk_cols, tw, ALU.add)
                end = split(cs)[:, :, P - 1:P] if d == 0 else split(cs)[:, :, 0:1]
                nc.vector.tensor_copy(end_dec[par][:, d, :].unsqueeze(2), end)
                if d == 1:
                    dve.drain()
                    nc.vector.scalar_tensor_tensor(rk_cols, rk_cols, pc[:, V_RK:V_RK + 1], rT, ALU.mult, ALU.mult)
                dve.drain().then_inc(operands_ready, 1)

        def first_pe(pe):
            for piece in ALONE:
                prep_pe(pe, piece, pj, 0, 1)
            for k in range(ND):
                v_piece(pe, pj, 0, k)

        def first_act(act):
            for piece in ALONE:
                prep_act(act, piece, pj, 0)
            b = job_full(act, pj, ("v", 0))
            nc.scalar.copy(vT, b[:, :])

        def first_dve(dve):
            prep_cols(dve, 0)
            for piece in ALONE:
                prep_dve(dve, piece, pj, 0, 0)

        def turn(pe, name, src):
            b = open_job(pe, rj, name)
            for m in range(NT):
                last = nc.tensor.transpose(b[:, m * P:(m + 1) * P], src[:, m * P:(m + 1) * P], ident[:, :])
            last.then_inc(full[rj[name][0]], 1)

        def pairs_pe(pe, it):
            for u in range(2):
                if u:
                    pe.wait_ge(operands_ready, 2)
                    job_read(pe, rj, ("v", 0))
                b = open_job(pe, rj, ("bonus", u))
                nc.tensor.matmul(b[:, :], head_ones, rk_cols, start=True, stop=True).then_inc(full[rj[("bonus", u)][0]], 1)
                turn(pe, ("vt", u), vT)
                for d in range(2):
                    turn(pe, (f"bt{d}", u), flat(Bt[d]))
                    turn(pe, (f"kt{d}", u), flat(Kt[d]))
                for d in range(2):
                    ar = AR[u][d]
                    for nm, st in (("LR", Bt[d]), ("MR", Kt[d])):
                        for z in range(2):
                            bs = [open_job(pe, rj, (f"{nm}{z}", d, h, u)) for h in range(2)]
                            for y in range(2):
                                m = 2 * z + y
                                last = []
                                for h in range(2):
                                    q = slice(h * HEAD, (h + 1) * HEAD)
                                    last.append(nc.tensor.matmul(bs[h][:, y * 256:(y + 1) * 256], st[q, m, :],
                                                                 ar[q, m, :, :].rearrange("p a b -> p (a b)"), start=True, stop=True))
                            for h in range(2):
                                last[h].then_inc(full[rj[(f"{nm}{z}", d, h, u)][0]], 1)

                    def turn_inverse(kind, src, lv=None):
                        for h in range(2):
                            name = (kind, d, h, u) if lv is None else (kind, lv, d, h, u)
                            if lv is None:
                                pe.wait_ge(ttinit_ready, 4 * u + 2 * d + h + 1)
                            else:
                                job_read(pe, rj, ("TX", lv, d, h, u))
                            turn(pe, name, flat(src[h]))

                    turn_inverse("T0", TT[d])
                    for lv in range(1, LEVELS):
                        for h in range(2):
                            name = ("X", lv, d, h, u)
                            job_read(pe, rj, ("T0", d, h, u) if lv == 1 else ("TX", lv - 1, d, h, u))
                            b = open_job(pe, rj, name)
                            for m in range(NT):
                                last = nc.tensor.matmul(b[:, m * P:(m + 1) * P], LT[h][:, m, :], Tm[h][:, m, :], start=True, stop=True)
                            last.then_inc(full[rj[name][0]], 1)
                        if u == 1 and d == 0 and lv == 1:
                            pe.wait_ge(ynorm_ready, 1)
                            turn(pe, ("yT", 0), ysq)
                        for piece in WITH.get(("lv", d, lv), []):
                            prep_pe(pe, piece, rj, u, it * 2 + (u + 2))
                        for h in range(2):
                            name = ("TX", lv, d, h, u)
                            job_read(pe, rj, ("X", lv, d, h, u))
                            if lv > 1:
                                job_read(pe, rj, ("Tr", lv - 1, d, h, u))
                            b = open_job(pe, rj, name)
                            for m in range(NT):
                                st, mv = (TT[d][h], Xm[h]) if lv < LEVELS - 1 else (Xm[h], TT[d][h])
                                last = nc.tensor.matmul(b[:, m * P:(m + 1) * P], st[:, m, :], mv[:, m, :], start=True, stop=True)
                            last.then_inc(full[rj[name][0]], 1)
                        if lv < LEVELS - 1:
                            turn_inverse("Tr", Tm, lv)
                for d in range(2):
                    for h in range(2):
                        job_read(pe, rj, ("TX", LEVELS - 1, d, h, u))
                        job_read(pe, rj, ("MR1", d, h, u))
                for x in ("vt", "bt0", "kt0", "bt1", "kt1"):
                    job_read(pe, rj, (x, u))
                for m in range(NT):
                    tile = (m, NT - 1 - m)
                    if m:
                        pe.wait_ge(state_ready, (NT - 1) * u + m)
                    bs = [open_job(pe, rj, ("cx", m, h, u)) for h in range(2)]
                    for d in range(2):
                        if m:
                            for h in range(2):
                                q = slice(h * HEAD, (h + 1) * HEAD)
                                nc.tensor.matmul(bs[h][:, d * HEAD:(d + 1) * HEAD], AR[u][d][q, tile[d], 0, :], states[m % 2][q, d, :],
                                                 start=True, stop=False)
                        for h in range(2):
                            q = slice(h * HEAD, (h + 1) * HEAD)
                            last = nc.tensor.matmul(bs[h][:, d * HEAD:(d + 1) * HEAD], MTRK[d][h][:, tile[d], 0, :], vtok[:, tile[d], q],
                                                    start=(m == 0), stop=True)
                            if d == 1:
                                last.then_inc(full[rj[("cx", m, h, u)][0]], 1)
                    if m == 0:
                        pe.wait_ge(ld_gate, it * 64 + (u + 1) * 32)
                        b = open_job(pe, rj, ("g", u))
                        nc.tensor.matmul(b[:, :], g2a_sl, gate_a, start=True, stop=False)
                        nc.tensor.matmul(b[:, :], g2b_sl[0:GATE - P, :], gate_b[0:GATE - P, :], start=False, stop=True).then_inc(full[rj[("g", u)][0]], 1)
                    v_piece(pe, rj, u, 2 * m)
                    b = open_job(pe, rj, ("cu", m, u))
                    for h in range(2):
                        job_read(pe, rj, ("cx", m, h, u))
                        for d in range(2):
                            last = nc.tensor.matmul(b[:, (2 * h + d) * HEAD:(2 * h + d + 1) * HEAD], TT[d][h][:, tile[d], :],
                                                    chain_x[:, h, d, :], start=True, stop=True)
                    last.then_inc(full[rj[("cu", m, u)][0]], 1)
                    v_piece(pe, rj, u, 2 * m + 1)
                    job_read(pe, rj, ("cu", m, u))
                    if m < NT - 1:
                        b = open_job(pe, rj, ("cs", m, u))
                        for h in range(2):
                            q = slice(h * HEAD, (h + 1) * HEAD)
                            for d in range(2):
                                o = b[q, d * HEAD:(d + 1) * HEAD]
                                nc.tensor.matmul(o, btok[d][:, tile[d], q], chain_u[:, h, d, :], start=True, stop=False)
                                last = nc.tensor.matmul(o, ktok[d][:, tile[d], q], vtok[:, tile[d], q], start=False, stop=True)
                        last.then_inc(full[rj[("cs", m, u)][0]], 1)
                    if m == 0:
                        for h in range(2):
                            open_job(pe, rj, ("y", h, u))
                    for d in range(2):
                        os = [ps[6 + h][:, tile[d] * HEAD:(tile[d] + 1) * HEAD] for h in range(2)]
                        for h in range(2):
                            q = slice(h * HEAD, (h + 1) * HEAD)
                            nc.tensor.matmul(os[h], MTRK[d][h][:, tile[d], 1, :], vtok[:, tile[d], q],
                                             start=(m == 0 and d == 0), stop=False, skip_group_check=True)
                        if m:
                            for h in range(2):
                                q = slice(h * HEAD, (h + 1) * HEAD)
                                nc.tensor.matmul(os[h], AR[u][d][q, tile[d], 1, :], states[m % 2][q, d, :],
                                                 start=False, stop=False, skip_group_check=True)
                        for h in range(2):
                            last = nc.tensor.matmul(os[h], RB[d][h][:, tile[d], :], chain_u[:, h, d, :], start=False,
                                                    stop=(m == NT - 1), skip_group_check=True)
                            if m == NT - 1 and d == 1:
                                last.then_inc(full[rj[("y", h, u)][0]], 1)
            pe.wait_ge(ynorm_ready, 2)
            turn(pe, ("yT", 1), ysq)

        def pairs_act(act, it):
            def y_square(u):
                act.wait_ge(ycen_ready, u + 1)
                nc.scalar.activation(ysq, ytok_flat, ACT.Square).then_inc(ysq_ready, 1)

            def y_feature(u):
                b = job_full(act, rj, ("yT", u))
                nc.scalar.activation(ytok_flat, b[:, :], ACT.Identity, bias=cols[:, bass.ds(it * 2 + (V_GNB * ND + u), 1)],
                                     scale=cols[:, bass.ds(it * 2 + (V_GNG * ND + u), 1)]).then_inc(free[rj[("yT", u)][0]], 1)

            for u in range(2):
                for nm, dst in (("vt", vtok), ("bt0", btok[0]), ("kt0", ktok[0]), ("bt1", btok[1]), ("kt1", ktok[1])):
                    b = job_full(act, rj, (nm, u))
                    nc.scalar.copy(flat(dst), b[:, :]).then_inc(free[rj[(nm, u)][0]], 1)
                if u == 1:
                    y_square(0)
                for d in range(2):
                    for h in range(2):
                        name = ("T0", d, h, u)
                        b = job_full(act, rj, name)
                        nc.scalar.copy(flat(Tm[h]), b[:, :]).then_inc(free[rj[name][0]], 1)
                    for lv in range(1, LEVELS):
                        if u == 1 and d == 0 and lv == 1:
                            y_feature(0)
                        for piece in WITH.get(("lv", d, lv), []):
                            prep_act(act, piece, rj, u)
                        if lv < LEVELS - 1:
                            for h in range(2):
                                name = ("Tr", lv, d, h, u)
                                b = job_full(act, rj, name)
                                nc.scalar.copy(flat(TT[d][h]), b[:, :]).then_inc(free[rj[name][0]], 1)
                for m in range(NT):
                    for h in range(2):
                        b = job_full(act, rj, ("cx", m, h, u))
                        nc.scalar.copy(chain_x[:, h, :, :].rearrange("p d v -> p (d v)"), b[:, 0:128]).then_inc(free[rj[("cx", m, h, u)][0]], 1)
                    if m == 1:
                        b = job_full(act, rj, ("g", u))
                        if u:
                            act.wait_ge(ydone_ready, 1)
                        nc.scalar.copy(gT, b[:, :]).then_inc(free[rj[("g", u)][0]], 1)
                    b = job_full(act, rj, ("cu", m, u))
                    nc.scalar.copy(chain_u.rearrange("p h d v -> p (h d v)"), b[:, 0:256]).then_inc(free[rj[("cu", m, u)][0]], 1)
                b = job_full(act, rj, ("v", u))
                job_read(act, rj, ("bonus", u))
                nc.scalar.copy(vT, b[:, :]).then_inc(free[rj[("v", u)][0]], 1)
                for h in range(2):
                    b = job_full(act, rj, ("y", h, u))
                    nc.scalar.copy(ytok[:, :, h, :], b[:, 0:256].rearrange("p (t v) -> p t v", t=NT)).then_inc(free[rj[("y", h, u)][0]], 1)
            y_square(1)
            y_feature(1)

        def pairs_pool(pool, it):
            def y_rstd(u):
                pool.wait_ge(yvar_ready, u + 1)
                nc.gpsimd.tensor_scalar(stat2, stat2, 1.0 / HEAD, GN_EPS, ALU.mult, ALU.add)
                pool.drain()
                nc.gpsimd.tensor_tensor(rstd8, stat2, mhalf[:, 0:8], ALU.pow).then_inc(yrstd_ready, 1)

            for u in range(2):
                if u:
                    y_rstd(0)
                for d in range(2):
                    for h in range(2):
                        job_read(pool, rj, ("LR1", d, h, u))
                        nc.gpsimd.tensor_tensor(TT[d][h], LT[h], bc(level_mask[:, 0, :].unsqueeze(1), P, NT, P), ALU.mult)
                        pool.drain()
                        nc.gpsimd.tensor_tensor(TT[d][h], TT[d][h], bc(ident[:, :].unsqueeze(1), P, NT, P), ALU.add).then_inc(ttinit_ready, 1)
            y_rstd(1)

        def pairs_dve(dve, it):
            y3 = ytok_flat.rearrange("p (g v) -> p g v", v=HEAD)

            def y_centre(u):
                for h in range(2):
                    job_read(dve, rj, ("y", h, u))
                nc.vector.tensor_reduce(stat, y3, AX, ALU.add)
                dve.drain()
                nc.vector.tensor_scalar(stat, stat, 1.0 / HEAD, None, ALU.mult)
                dve.drain()
                nc.vector.tensor_tensor(y3, y3, bc(stat.unsqueeze(2), P, 8, HEAD), ALU.subtract).then_inc(ycen_ready, 1)

            def y_variance(u):
                dve.wait_ge(ysq_ready, u + 1)
                nc.vector.tensor_reduce(stat2, ysq.rearrange("p (g v) -> p g v", v=HEAD), AX, ALU.add).then_inc(yvar_ready, 1)

            def y_scale(u):
                dve.wait_ge(yrstd_ready, u + 1)
                nc.vector.tensor_tensor(ysq.rearrange("p (g v) -> p g v", v=HEAD), y3, bc(rstd8.unsqueeze(2), P, 8, HEAD), ALU.mult).then_inc(ynorm_ready, 1)

            def y_finish(u):
                job_read(dve, rj, ("yT", u))
                nc.vector.tensor_tensor(ytok_flat, ytok_flat, bonus[u], ALU.add)
                dve.drain()
                nc.vector.tensor_tensor(y_all[:, bass.ds(it * 2 + u, 1), :], ytok_flat.unsqueeze(1), gT.unsqueeze(1), ALU.mult).then_inc(ydone_ready, 1)

            for u in range(2):
                prep_cols(dve, (it * 2 + (u + 1)) & (NPAIR - 1))
                b = job_full(dve, rj, ("bonus", u))
                nc.vector.tensor_tensor(bonus[u], b[:, :], vT, ALU.mult).then_inc(free[rj[("bonus", u)][0]], 1)
                if u:
                    y_centre(0)
                for d in range(2):
                    mk = bc(strict_incl[d].unsqueeze(1), P, 2, 2, P)
                    for z in range(2):
                        for h in range(2):
                            name = (f"LR{z}", d, h, u)
                            b = job_full(dve, rj, name)
                            v = b[:, :].rearrange("p (m a j) -> p m a j", m=2, a=2)
                            for x, dst in ((0, LT[h]), (1, RB[d][h])):
                                last = nc.vector.tensor_tensor(dst[:, 2 * z:2 * z + 2, :], v[:, :, x, :],
                                                               bc(strict_incl[d][:, x, :].unsqueeze(1), P, 2, P), ALU.mult)
                            last.then_inc(free[rj[name][0]], 1)
                    if u == 1 and d == 0:
                        y_variance(0)
                    for z in range(2):
                        for h in range(2):
                            name = (f"MR{z}", d, h, u)
                            b = job_full(dve, rj, name)
                            nc.vector.tensor_tensor(MTRK[d][h][:, 2 * z:2 * z + 2], b[:, :].rearrange("p (m a j) -> p m a j", m=2, a=2),
                                                    mk, ALU.mult).then_inc(free[rj[name][0]], 1)
                    if u == 1 and d == 0:
                        y_scale(0)
                    for lv in range(1, LEVELS):
                        for h in range(2):
                            name = ("X", lv, d, h, u)
                            b = job_full(dve, rj, name)
                            nc.vector.tensor_tensor(Xm[h], b[:, :].rearrange("p (m j) -> p m j", m=NT),
                                                    bc(level_mask[:, lv, :].unsqueeze(1), P, NT, P), ALU.mult).then_inc(free[rj[name][0]], 1)
                        if u == 1 and d == 0 and lv == 2:
                            y_finish(0)
                        for piece in WITH.get(("lv", d, lv), []):
                            prep_dve(dve, piece, rj, u, 1 - u)
                        for h in range(2):
                            name = ("TX", lv, d, h, u)
                            b = job_full(dve, rj, name)
                            dst = Tm[h] if lv < LEVELS - 1 else TT[d][h]
                            nc.vector.tensor_tensor(dst, dst, b[:, :].rearrange("p (m j) -> p m j", m=NT), ALU.add).then_inc(free[rj[name][0]], 1)
                        dve.drain()
                for m in range(NT - 1):
                    b = job_full(dve, rj, ("cs", m, u))
                    for d in range(2):
                        tile = (m, NT - 1 - m)[d]
                        o = b[:, d * HEAD:(d + 1) * HEAD]
                        dec = end_dec[u][:, d, tile:tile + 1]
                        if m == 0:
                            nc.vector.tensor_scalar(states[1][:, d, :], o, dec, None, ALU.mult)
                        else:
                            nc.vector.scalar_tensor_tensor(states[(m + 1) % 2][:, d, :], o, dec, state_dec[:, d, :], ALU.mult, ALU.add)
                    dve.drain().then_inc(state_ready, 1)
                    for d in range(2):
                        nx = (m + 1, NT - 2 - m)[d]
                        nc.vector.tensor_scalar(state_dec[:, d, :], states[(m + 1) % 2][:, d, :], end_dec[u][:, d, nx:nx + 1], None, ALU.mult)
                    dve.drain().then_inc(free[rj[("cs", m, u)][0]], 1)
            y_centre(1)
            y_variance(1)
            y_scale(1)
            y_finish(1)

        def pair_loads(sp, pair):
            c = bass.ds(pair * P, P)
            for n, w in enumerate(("rw_wr", "rw_wk", "rw_wv")):
                sp.dma_start(w_sl[:, n], a[w][0].rearrange("(k p) n -> p k n", p=P)[:, :, c]).then_inc(ld_pair, 16)
            sp.dma_start(w2_sl, a["rw_w2"][0].rearrange("e k n -> (e k) n")[:, c]).then_inc(ld_pair, 16)
            sp.dma_start(a2_sl, a["rw_a2"][0].rearrange("e k n -> (e k) n")[:, c]).then_inc(ld_pair, 16)

        def gate_loads(sp, pair):
            c = bass.ds(pair * P, P)
            sp.dma_start(g2a_sl, a["rw_g2"][0][0:P, c]).then_inc(ld_gate, 16)
            sp.dma_start(g2b_sl[0:GATE - P, :], a["rw_g2"][0][P:GATE, c]).then_inc(ld_gate, 16)

        oj = Jobs([((t, z), (2 * t + z) % NB) for t in range(NT) for z in range(2)])

        def out_pe(pe, n):
            pe.wait_ge(ld_wo[n], 16)
            for t in range(NT):
                for z in range(2):
                    b = open_job(pe, oj, (t, z))
                    for k in range(ND):
                        last = nc.tensor.matmul(b[:, :], yT[:, k, t * P:(t + 1) * P], wo_sb[:, k, z * 512:(z + 1) * 512],
                                                start=(k == 0), stop=(k == ND - 1))
                    last.then_inc(full[oj[(t, z)][0]], 1)

        def out_dve(dve, n):
            if n == 0:
                dve.wait_ge(ld_x2, 16 * NT)
            for t in range(NT):
                for z in range(2):
                    b = job_full(dve, oj, (t, z))
                    xs = x_sb[:, t, z * 512:(z + 1) * 512]
                    nc.vector.tensor_tensor(xs, xs, b[:, :], ALU.add).then_inc(free[oj[(t, z)][0]], 1)

        def load_x(sp, s):
            v = a["x"][0].rearrange("(t p) d -> p t d", p=P)
            for t in range(NT):
                sp.dma_start(x_sb[:, t, :], v[:, t, :]).then_inc(s, 16)

        def load_gain(sp, n):
            layer, which = divmod(n, 2)
            g = a[("norm_mix_g", "norm_ffn_g")[which]][layer:layer + 1, :]
            sp.dma_start(gain_row, g.to_broadcast([P, D])).then_inc(ld_gain[n], 16)

        route_jobs = Jobs([("lg", 0), ("at", 1), ("st", 2)])

        def route_pe(pe, layer):
            pe.wait_ge(ld_router[layer], 16)
            for t in range(NT):
                for k in range(ND):
                    last = nc.tensor.matmul(ps[0][:, t * NE:(t + 1) * NE], hT[:, k, t * P:(t + 1) * P], router_sb[:, k, :],
                                            start=(k == 0), stop=(k == ND - 1))
            last.then_inc(full[0], 1)
            pe.wait_ge(aff_ready, 1)
            for t in range(NT):
                last = nc.tensor.transpose(ps[1][0:NE, t * P:(t + 1) * P], aff[:, t, 0:NE], ident[:, :])
            last.then_inc(full[1], 1)
            pe.wait_ge(slot_ready, 1)
            for t in range(NT):
                last = nc.tensor.transpose(ps[2][:, t * NE:(t + 1) * NE], cumT[0:NE, t * P:(t + 1) * P], ident[0:NE, 0:NE])
            last.then_inc(full[2], 1)

        def route_act(act):
            act.wait_ge(logit_ready, 1)
            nc.scalar.activation(logit, logit, ACT.Exp).then_inc(exp_ready, 1)

        def route_pool(pool):
            nc.gpsimd.iota(iota_i, [[1, CAP]], base=0, channel_multiplier=0)
            nc.gpsimd.memset(slot[:, :, NE:NE + 2], -1.0)
            nc.gpsimd.memset(aff[:, :, NE:NE + 2], 0.0)
            pool.drain().then_inc(iota_ready, 1)

        def route_dve(dve):
            b = job_full(dve, route_jobs, "lg")
            lg = b[:, 0:NT * NE].rearrange("p (t e) -> p t e", t=NT)
            nc.vector.tensor_reduce(rmax, lg, AX, ALU.max)
            dve.drain()
            nc.vector.tensor_tensor(logit, lg, rmax.unsqueeze(2).to_broadcast([P, NT, NE]), ALU.subtract).then_inc(logit_ready, 1)
            dve.wait_ge(exp_ready, 1)
            nc.vector.tensor_reduce(rsum_t, logit, AX, ALU.add)
            dve.drain()
            nc.vector.reciprocal(rmax, rsum_t)
            dve.drain()
            nc.vector.tensor_tensor(aff[:, :, 0:NE], logit, rmax.unsqueeze(2).to_broadcast([P, NT, NE]), ALU.mult).then_inc(aff_ready, 1)
            b = job_full(dve, route_jobs, "at")
            nc.vector.tensor_copy(workT[0:NE, :], b[0:NE, :])
            for n in range(CAP // 8):
                dve.drain()
                nc.vector.max(top8[0:NE, :], workT[0:NE, :])
                dve.drain()
                nc.vector.match_replace(workT[0:NE, :], top8[0:NE, :], workT[0:NE, :], -1.0)
            dve.drain()
            nc.vector.tensor_scalar(maskT[0:NE, :], workT[0:NE, :], 0.0, None, ALU.is_lt)
            dve.drain()
            nc.vector.tensor_tensor_scan(cumT[0:NE, :], maskT[0:NE, :], maskT[0:NE, :], 0.0, ALU.add, ALU.max)
            dve.drain()
            nc.vector.tensor_tensor(cumT[0:NE, :], cumT[0:NE, :], maskT[0:NE, :], ALU.mult)
            dve.drain()
            nc.vector.tensor_scalar(cumT[0:NE, :], cumT[0:NE, :], -1.0, None, ALU.add).then_inc(slot_ready, 1)
            dve.wait_ge(iota_ready, 1)
            nc.vector.tensor_copy(iota_s, iota_i)
            b = job_full(dve, route_jobs, "st")
            nc.vector.tensor_copy(slot[:, :, 0:NE], b[:, 0:NT * NE].rearrange("p (t e) -> p t e", t=NT))
            dve.drain()
            picks(dve, 0)

        def picks(dve, first):
            for t in range(NT):
                for e in range(2):
                    o = slice(e * CAP, (e + 1) * CAP)
                    at = slot[:, t, bass.ds(first + e, 1)]
                    nc.vector.tensor_scalar(pick[:, t, o], iota_s, at, None, ALU.is_equal)
                    nc.vector.tensor_scalar(pick_gate[:, t, o], iota_s, at, aff[:, t, bass.ds(first + e, 1)], ALU.is_equal, ALU.mult)

        PER = [3, 3, 3, 2, 2, 1, 1, 4]
        comb_banks = [7, 0, 1, 2]

        def used(eng, b, it, n):
            eng.wait_ge(free[b], it * PER[b] + n)

        def filled(eng, b, it, n):
            eng.wait_ge(full[b], it * PER[b] + n)

        def read_out(eng, b, it, n):
            eng.wait_ge(free[b], it * PER[b] + n + 1)

        def arrived(pe, layer, it, c):
            pe.wait_ge(ld_chunk[c % RING], (it * (CPP // RING) + (c // RING + 1 + CPP // RING * (NE // 2) * layer)) * 16)

        def moe_pe(pe, it, layer):
            pe.wait_ge(pick_ready, it + 1)
            for z in range(2):
                used(pe, z, it, 1)
                for k in range(4):
                    for t in range(NT):
                        last = nc.tensor.matmul(ps[z][:, k * P:(k + 1) * P], h_tok[:, t, (4 * z + k) * P:(4 * z + k + 1) * P],
                                                pick[:, t, :], start=(t == 0), stop=(t == NT - 1))
                last.then_inc(full[z], 1)
            used(pe, 2, it, 1)
            for t in range(NT):
                last = nc.tensor.transpose(ps[2][:, t * P:(t + 1) * P], pick_gate[:, t, :], ident[:, :])
            last.then_inc(full[2], 1)
            read_out(pe, 0, it, 1)
            read_out(pe, 1, it, 1)

            def gate_up(e, z):
                used(pe, 3 + z, it, e + 1)
                c = 4 * e + 2 * z
                arrived(pe, layer, it, c)
                arrived(pe, layer, it, c + 1)
                for k in range(ND):
                    for g in range(2):
                        last = nc.tensor.matmul(ps[3 + z][g * CAP:(g + 1) * CAP, :], xeT[:, k, e * CAP:(e + 1) * CAP],
                                                ring[(c + g) % RING][:, k, :], start=(k == 0), stop=(k == ND - 1))
                pe.drain().then_inc(full[3 + z], 1)
                pe.sem_inc(chunk_used[layer], 2)

            def turn_hidden(e):
                pe.wait_ge(hid_ready, it * 4 + (2 * e + 2))
                used(pe, 7, it, e + 1)
                pe.sem_inc(waited, 1)
                for k in range(ND):
                    last = nc.tensor.transpose(ps[7][:, k * CAP:(k + 1) * CAP], hid_tok[e][0:CAP, k * P:(k + 1) * P], ident[0:CAP, 0:CAP])
                last.then_inc(full[7], 1)

            def down(e):
                used(pe, 5 + e, it, 1)
                read_out(pe, 7, it, e + 1)
                c = 8 + 2 * e
                arrived(pe, layer, it, c)
                arrived(pe, layer, it, c + 1)
                for k in range(ND):
                    for z in range(2):
                        last = nc.tensor.matmul(ps[5 + e][z * CAP:(z + 1) * CAP, :], hidT[e][:, k, :],
                                                ring[(c + z) % RING][:, k, :], start=(k == 0), stop=(k == ND - 1))
                pe.drain().then_inc(full[5 + e], 1)
                pe.sem_inc(chunk_used[layer], 2)

            gate_up(0, 0)
            gate_up(0, 1)
            gate_up(1, 0)
            turn_hidden(0)
            gate_up(1, 1)
            down(0)
            turn_hidden(1)
            down(1)
            read_out(pe, 2, it, 1)
            read_out(pe, 5, it, 1)
            read_out(pe, 6, it, 1)
            for j in range(8):
                t, z = divmod(j, 2)
                b = comb_banks[j % 4]
                used(pe, b, it, j // 4 + (3 if b == 7 else 2))
                nc.tensor.matmul(ps[b][:, :], combT[:, t * P:(t + 1) * P], ye[:, z * 512:(z + 1) * 512],
                                 start=True, stop=True).then_inc(full[b], 1)

        def moe_act(act, it):
            for z in range(2):
                filled(act, z, it, 1)
                nc.scalar.copy(xeT[:, 4 * z:4 * z + 4, :].rearrange("p k s -> p (k s)"), ps[z][:, :]).then_inc(free[z], 1)

            def half_tanh(e, z):
                filled(act, 3 + z, it, e + 1)
                nc.scalar.activation(th[z][0:CAP, :], ps[3 + z][0:CAP, :], ACT.Tanh, scale=0.5).then_inc(tanh_ready, 1)

            def hidden(e):
                filled(act, 7, it, e + 1)
                nc.scalar.copy(hidT[e].rearrange("p k s -> p (k s)"), ps[7][:, :]).then_inc(free[7], 1)

            def outputs(e):
                filled(act, 5 + e, it, 1)
                for z in range(2):
                    nc.scalar.copy(ye[e * CAP:(e + 1) * CAP, z * 512:(z + 1) * 512], ps[5 + e][z * CAP:(z + 1) * CAP, :])
                act.drain().then_inc(free[5 + e], 1)

            half_tanh(0, 0)
            half_tanh(0, 1)
            half_tanh(1, 0)
            hidden(0)
            half_tanh(1, 1)
            outputs(0)
            hidden(1)
            outputs(1)

        def moe_dve(dve, it):
            filled(dve, 2, it, 1)
            nc.vector.tensor_copy(combT, ps[2][:, :]).then_inc(free[2], 1)
            for e in range(2):
                for z in range(2):
                    dve.wait_ge(tanh_ready, it * 4 + (2 * e + z + 1))
                    nc.vector.scalar_tensor_tensor(th[z][0:CAP, :], th[z][0:CAP, :], 1.0, ps[3 + z][0:CAP, :], ALU.add, ALU.mult)
                    dve.drain()
                    nc.vector.scalar_tensor_tensor(hid_tok[e][0:CAP, z * 512:(z + 1) * 512], th[z][0:CAP, :], 0.5,
                                                   ps[3 + z][CAP:2 * CAP, :], ALU.mult, ALU.mult)
                    dve.drain().then_inc(free[3 + z], 1)
                    dve.sem_inc(hid_ready, 1)
                if e == 0:
                    filled(dve, 1, it, 1)
                    picks(dve, it * 2 + 2)
                    dve.drain().then_inc(pick_ready, 1)
            for j in range(8):
                t, z = divmod(j, 2)
                b = comb_banks[j % 4]
                filled(dve, b, it, j // 4 + (3 if b == 7 else 2))
                xs = x_sb[:, t, z * 512:(z + 1) * 512]
                nc.vector.tensor_tensor(xs, xs, ps[b][:, :], ALU.add).then_inc(free[b], 1)

        def load_chunk(sp, layer, pair, c):
            pair = pair + c // CPP
            c = c % CPP
            e, r = divmod(c, 4) if c < 8 else ((c - 8) // 2, 4 + c % 2)
            w, z = (("moe_w_gate", 0), ("moe_w_up", 0), ("moe_w_gate", 1), ("moe_w_up", 1), ("moe_w_down", 0), ("moe_w_down", 1))[r]
            v = a[w][layer].rearrange("(i e) (k p) n -> i e p k n", e=2, p=P)
            src = v[bass.ds(pair, 1), e, :, :, z * 512:(z + 1) * 512].rearrange("i p k n -> (i p) k n") \
                if not isinstance(pair, int) else v[pair, e, :, :, z * 512:(z + 1) * 512]
            sp.dma_start(ring[c % RING], src).then_inc(ld_chunk[c % RING], 16)

        def load_experts(sp, layer):
            last = NE // 2 - 1
            for c in range(RING):
                load_chunk(sp, layer, 0, c)
            with sp.Fori(0, last) as it:
                for c in range(CPP):
                    sp.wait_ge(chunk_used[layer], it * CPP + (c + 1))
                    sp.sem_inc(waited_sp, 1)
                    load_chunk(sp, layer, it, c + RING)
            for c in range(CPP - RING):
                sp.wait_ge(chunk_used[layer], last * CPP + c + 1)
                load_chunk(sp, layer, last, c + RING)

        CB = [(t, z) for t in range(NT) for z in range(2)]
        NC = (QL + KVL) // P
        mj = Jobs([(x, n) for n, x in enumerate(CB)] + [("cols", 0)] + [(("cT", j), j + 1) for j in range(NC)])

        def mla_in_pe(pe):
            pe.wait_ge(ld_win, 16)
            for t, z in CB:
                w = 512 if z == 0 else QL + KVL + ROPE - 512
                b = open_job(pe, mj, (t, z))
                for k in range(ND):
                    last = nc.tensor.matmul(b[:, 0:w], hT[:, k, t * P:(t + 1) * P], win_sb[:, k, z * 512:z * 512 + w],
                                            start=(k == 0), stop=(k == ND - 1))
                last.then_inc(full[mj[(t, z)][0]], 1)
            pe.wait_ge(ld_mla, 16 * 5)
            b = open_job(pe, mj, "cols")
            nc.tensor.transpose(b[:, 0:NC], norm_rows[0:NC, :], ident[0:NC, 0:NC]).then_inc(full[0], 1)
            pe.wait_ge(cnorm_ready, 1)
            for j in range(NC):
                b = open_job(pe, mj, ("cT", j))
                for t in range(NT):
                    last = nc.tensor.transpose(b[:, t * P:(t + 1) * P], c_tok[:, t, j * P:(j + 1) * P], ident[:, :])
                last.then_inc(full[j + 1], 1)

        def mla_in_act(act):
            for t, z in CB:
                w = 512 if z == 0 else QL + KVL + ROPE - 512
                b = job_full(act, mj, (t, z))
                nc.scalar.copy(c_tok[:, t, z * 512:z * 512 + w], b[:, 0:w]).then_inc(free[mj[(t, z)][0]], 1)
            act.drain()
            for t in range(NT):
                nc.scalar.activation(prob[0][:, t, 0:QL], c_tok[:, t, 0:QL], ACT.Square, accum_out=ss_c[:, t:t + 1])
                nc.scalar.activation(prob[1][:, t, 0:KVL], c_tok[:, t, QL:QL + KVL], ACT.Square, accum_out=ss_c[:, NT + t:NT + t + 1])
            act.drain().then_inc(css_ready, 1)
            nc.scalar.copy(k_rope, c_tok[:, :, QL + KVL:])
            act.wait_ge(red_ready, 1)
            nc.scalar.activation(sin8.rearrange("p (t h) f -> p t h f", h=2)[:, :, 0, :], red, ACT.Sin)
            nc.scalar.activation(cos8.rearrange("p (t h) f -> p t h f", h=2)[:, :, 0, :], ang, ACT.Sin)
            act.drain()
            for v in (sin8, cos8):
                w = v.rearrange("p (t h) f -> p t h f", h=2)
                nc.scalar.copy(w[:, :, 1, :], w[:, :, 0, :])

        def mla_in_pool(pool):
            for n in range(HALF):
                nc.gpsimd.memset(freq[:, n:n + 1], float(np.float32(THETA) ** np.float32(-2.0 * n / ROPE)))
            pool.drain().then_inc(freq_ready, 1)
            pool.wait_ge(css_ready, 1)
            nc.gpsimd.tensor_scalar(ss_c[:, 0:NT], ss_c[:, 0:NT], 1.0 / QL, NORM_EPS, ALU.mult, ALU.add)
            nc.gpsimd.tensor_scalar(ss_c[:, NT:], ss_c[:, NT:], 1.0 / KVL, NORM_EPS, ALU.mult, ALU.add)
            pool.drain()
            nc.gpsimd.tensor_tensor(rstd_c, ss_c, mhalf[:, 0:8], ALU.pow).then_inc(crstd_ready, 1)

        def mla_in_dve(dve):
            dve.wait_ge(ld_mla, 16 * 5)
            nc.vector.tensor_copy(pos_f, pos_i)
            dve.wait_ge(freq_ready, 1)
            dve.drain()
            nc.vector.tensor_tensor(red, pos_f.unsqueeze(2).to_broadcast([P, NT, HALF]), freq.unsqueeze(1).to_broadcast([P, NT, HALF]), ALU.mult)
            dve.drain()
            nc.vector.tensor_scalar(rnd, red, float(1.0 / (2.0 * np.pi)), 12582912.0, ALU.mult, ALU.add)
            dve.drain()
            nc.vector.tensor_scalar(rnd, rnd, -12582912.0, None, ALU.add)
            dve.drain()
            two_pi = 2.0 * np.pi
            c1 = 6.28125
            c2 = float(np.float32(np.round((two_pi - c1) * 2.0 ** 21) / 2.0 ** 21))
            c3 = two_pi - c1 - c2
            for c in (c1, c2, c3):
                nc.vector.scalar_tensor_tensor(red, rnd, -float(c), red, ALU.mult, ALU.add)
                dve.drain()
            nc.vector.tensor_scalar(red, red, 3.1415925, -3.1415925, ALU.min, ALU.max)
            dve.drain()
            nc.vector.scalar_tensor_tensor(ang, red, -1.0, red, ALU.mult, ALU.max)
            dve.drain()
            nc.vector.tensor_scalar(ang, ang, -1.0, float(np.pi / 2), ALU.mult, ALU.add).then_inc(red_ready, 1)
            job_full(dve, mj, "cols")
            nc.vector.tensor_copy(norm_cols[:, 0:NC], ps[0][:, 0:NC])
            dve.wait_ge(crstd_ready, 1)
            for t in range(NT):
                for lo, hi, s in ((0, QL, t), (QL, QL + KVL, NT + t)):
                    nc.vector.tensor_scalar(c_tok[:, t, lo:hi], c_tok[:, t, lo:hi], rstd_c[:, s:s + 1], None, ALU.mult)
            dve.drain().then_inc(cnorm_ready, 1)
            for j in range(NC):
                b = job_full(dve, mj, ("cT", j))
                nc.vector.tensor_scalar(cT[:, j, :], b[:, :], norm_cols[:, j:j + 1], None, ALU.mult)

        NQ, NKV = QL // P, KVL // P
        names = [("q", 0), ("q", 1), ("kv", 0), ("kv", 1)] + [("T", h, s) for h in range(2) for s in range(2)]
        names += [("S", h, t) for h in range(2) for t in range(NT)]
        for h in range(2):
            names += [("PT", h, t) for t in range(NT)] + [("o", h)]
        aj = Jobs([(x, n % NB) for n, x in enumerate(names)])
        SCALE = QK ** -0.5

        def attn_pe(pe, it):
            pe.wait_ge(ld_pair2, (it + 1) * 32)
            for kind, w, n0, n, width in (("q", wq_sl, 0, NQ, 2 * QK), ("kv", wkv_sl, NQ, NKV, 2 * (NOPE + VH))):
                for z in range(2):
                    b = open_job(pe, aj, (kind, z))
                    for y in range(2):
                        t = 2 * z + y
                        for j in range(n):
                            last = nc.tensor.matmul(b[:, y * width:(y + 1) * width], cT[:, n0 + j, t * P:(t + 1) * P], w[:, j, :],
                                                    start=(j == 0), stop=(j == n - 1))
                    last.then_inc(full[aj[(kind, z)][0]], 1)
            pe.wait_ge(qk_ready, 1)
            for h in range(2):
                for s in range(2):
                    b = open_job(pe, aj, ("T", h, s))
                    for t in range(NT):
                        last = nc.tensor.transpose(b[0:QK, t * P:(t + 1) * P], qk_tok[:, s, 2 * t + h, :], ident[:, :])
                    last.then_inc(full[aj[("T", h, s)][0]], 1)
            for h in range(2):
                job_read(pe, aj, ("T", h, 0))
                job_read(pe, aj, ("T", h, 1))
                for t in range(NT):
                    b = open_job(pe, aj, ("S", h, t))
                    nc.tensor.matmul(b[:, :], qkT[h][0][0:QK, t * P:(t + 1) * P], qkT[h][1][0:QK, :],
                                     start=True, stop=True).then_inc(full[aj[("S", h, t)][0]], 1)
            for h in range(2):
                pe.wait_ge(prob_ready, NT * (h + 1))
                for t in range(NT):
                    b = open_job(pe, aj, ("PT", h, t))
                    for q in range(NT):
                        last = nc.tensor.transpose(b[:, q * P:(q + 1) * P], prob[h][:, q, t * P:(t + 1) * P], ident[:, :])
                    last.then_inc(full[aj[("PT", h, t)][0]], 1)
                b = open_job(pe, aj, ("o", h))
                for t in range(NT):
                    job_read(pe, aj, ("PT", h, t))
                    last = nc.tensor.matmul(b[h * VH:(h + 1) * VH, :], v_tok[:, t, h, :], probT[h][:, t, :],
                                            start=(t == 0), stop=(t == NT - 1))
                last.then_inc(full[aj[("o", h)][0]], 1)

        def attn_act(act, it):
            for z in range(2):
                b = job_full(act, aj, ("q", z))
                nc.scalar.copy(qk_tok[:, 0, 4 * z:4 * z + 4, :].rearrange("p g c -> p (g c)"), b[:, 0:4 * QK]).then_inc(free[aj[("q", z)][0]], 1)
            for z in range(2):
                b = job_full(act, aj, ("kv", z))
                kv = b[:, :].rearrange("p (g c) -> p g c", g=4)
                nc.scalar.copy(qk_tok[:, 1, 4 * z:4 * z + 4, 0:NOPE], kv[:, :, 0:NOPE])
                nc.scalar.copy(v_tok[:, 2 * z:2 * z + 2, :, :].rearrange("p t h v -> p (t h) v"), kv[:, :, NOPE:]).then_inc(free[aj[("kv", z)][0]], 1)
            act.wait_ge(rope_in, 1)
            act.drain()
            nc.scalar.activation(qk_sq.rearrange("p a b c -> p (a b c)"), qk_tok.rearrange("p a b c -> p (a b c)"), ACT.Square).then_inc(qksq_ready, 1)
            for h in range(2):
                b = job_full(act, aj, ("T", h, 0))
                nc.scalar.copy(qkT[h][0][0:QK, :], b[0:QK, :]).then_inc(free[aj[("T", h, 0)][0]], 1)
            for h in range(2):
                for t in range(NT):
                    n = NT * h + t
                    act.wait_ge(max_ready, n + 1)
                    b = job_full(act, aj, ("S", h, t))
                    nc.scalar.activation(prob[h][:, t, :], b[:, :], ACT.Exp, bias=nmx[:, n:n + 1], scale=SCALE,
                                         accum_out=lsum[:, n:n + 1])
                    act.drain().then_inc(free[aj[("S", h, t)][0]], 1)
            for h in range(2):
                for t in (0, 2):
                    b = job_full(act, aj, ("PT", h, t))
                    nc.scalar.copy(probT[h][:, t, :], b[:, :]).then_inc(free[aj[("PT", h, t)][0]], 1)
                b = job_full(act, aj, ("o", h))
                q = slice(h * VH, (h + 1) * VH)
                nc.scalar.copy(hT[q, bass.ds(it, 1), :].rearrange("p a s -> p (a s)"), b[q, :]).then_inc(free[aj[("o", h)][0]], 1)

        def attn_pool(pool, it):
            nc.gpsimd.tensor_copy(qk_tok[:, 1, :, NOPE:].rearrange("p (t h) c -> p t h c", h=2),
                                  k_rope.unsqueeze(2).to_broadcast([P, NT, 2, ROPE])).then_inc(rope_in, 1)
            pool.wait_ge(qkss_ready, 1)
            nc.gpsimd.tensor_scalar(ss16, ss16, 1.0 / QK, NORM_EPS, ALU.mult, ALU.add)
            pool.drain()
            nc.gpsimd.tensor_tensor(rstd16, ss16, mhalf, ALU.pow).then_inc(qkrstd_ready, 1)

        def attn_dve(dve, it):
            dve.wait_ge(qksq_ready, 1)
            nc.vector.tensor_reduce(ss16, qk_sq.rearrange("p a b c -> p (a b) c"), AX, ALU.add).then_inc(qkss_ready, 1)
            dve.drain()
            nc.vector.tensor_tensor(qk_tok, qk_tok, head_gain.unsqueeze(2).to_broadcast([P, 2, 8, QK]), ALU.mult)
            dve.wait_ge(qkrstd_ready, 1)
            dve.drain()
            qkf = qk_tok.rearrange("p a b c -> p (a b) c")
            nc.vector.tensor_tensor(qkf, qkf, rstd16.unsqueeze(2).to_broadcast([P, 16, QK]), ALU.mult)
            dve.drain()
            x1, x2 = qk_tok[:, :, :, NOPE:NOPE + HALF], qk_tok[:, :, :, NOPE + HALF:]
            c, s = (v.unsqueeze(1).to_broadcast([P, 2, 8, HALF]) for v in (cos8, sin8))
            for o, x, y in ((0, x1, c), (1, x2, s), (2, x2, c), (3, x1, s)):
                nc.vector.tensor_tensor(rtmp[o], x, y, ALU.mult)
            dve.drain()
            nc.vector.tensor_tensor(x1, rtmp[0], rtmp[1], ALU.subtract)
            nc.vector.tensor_tensor(x2, rtmp[2], rtmp[3], ALU.add)
            dve.drain().then_inc(qk_ready, 1)
            for h in range(2):
                b = job_full(dve, aj, ("T", h, 1))
                nc.vector.tensor_copy(qkT[h][1][0:QK, :], b[0:QK, :]).then_inc(free[aj[("T", h, 1)][0]], 1)

            def normed(h, t):
                n = NT * h + t
                job_read(dve, aj, ("S", h, t))
                nc.vector.reciprocal(linv[:, n:n + 1], lsum[:, n:n + 1])
                dve.drain()
                nc.vector.tensor_scalar(prob[h][:, t, :], prob[h][:, t, :], linv[:, n:n + 1], None, ALU.mult).then_inc(prob_ready, 1)

            order = [(h, t) for h in range(2) for t in range(NT)]
            for n, (h, t) in enumerate(order):
                b = job_full(dve, aj, ("S", h, t))
                nc.vector.tensor_reduce(mx[:, n:n + 1], b[:, :], AX, ALU.max)
                dve.drain()
                nc.vector.tensor_scalar(nmx[:, n:n + 1], mx[:, n:n + 1], -SCALE, None, ALU.mult).then_inc(max_ready, 1)
                if n >= 2:
                    normed(*order[n - 2])
            normed(*order[-2])
            normed(*order[-1])
            for h in range(2):
                for t in (1, 3):
                    b = job_full(dve, aj, ("PT", h, t))
                    nc.vector.tensor_copy(probT[h][:, t, :], b[:, :]).then_inc(free[aj[("PT", h, t)][0]], 1)

        def attn_loads(sp, it):
            sp.dma_start(wq_sl, a["mla_w_uq"][0].rearrange("(k p) n -> p k n", p=P)[:, :, bass.ds(it * (2 * QK), 2 * QK)]).then_inc(ld_pair2, 16)
            sp.dma_start(wkv_sl, a["mla_w_ukv"][0].rearrange("(k p) n -> p k n", p=P)[:, :, bass.ds(it * (2 * (NOPE + VH)), 2 * (NOPE + VH))]).then_inc(ld_pair2, 16)

        @block.gpsimd
        def _(pool):
            nc.gpsimd.memset(ident[:, :], 0.0)
            nc.gpsimd.memset(mhalf, -0.5)
            pool.drain()
            nc.gpsimd.affine_select(out=ident[:, :], in_=ident[:, :], compare_op=ALU.not_equal, fill=1.0,
                                    base=0, pattern=[[-1, P]], channel_multiplier=1)
            meet_pool(pool)
            norm_pool(pool)
            meet_pool(pool)
            meet_pool(pool, ("pe", "act", "dve", "sp"))
            masks_pool(pool)
            meet_pool(pool)
            meet_pool(pool, ("pe", "act", "dve", "sp"))
            with pool.Fori(0, NPAIR // 2) as it:
                pairs_pool(pool, it)
                meet_pool(pool, ("pe", "act", "dve", "sp"))
            for layer in range(2):
                if layer == 1:
                    norm_pool(pool)
                    meet_pool(pool)
                    mla_in_pool(pool)
                    meet_pool(pool, ("pe", "act", "dve", "sp"))
                    with pool.Fori(0, NPAIR) as it:
                        attn_pool(pool, it)
                        meet_pool(pool, ("pe", "act", "dve", "sp"))
                else:
                    meet_pool(pool, ("pe", "act", "dve", "sp"))
                meet_pool(pool)
                norm_pool(pool)
                meet_pool(pool)
                route_pool(pool)
                meet_pool(pool, credit=1)
                meet_pool(pool, ("pe", "act", "dve", "sp"))

        @block.tensor
        def _(pe):
            meet(pe, "pe")
            norm_pe(pe)
            meet(pe, "pe")
            pre_pe(pe)
            meet(pe, "pe")
            meet(pe, "pe")
            first_pe(pe)
            meet(pe, "pe")
            with pe.Fori(0, NPAIR // 2) as it:
                pairs_pe(pe, it)
                meet(pe, "pe")
            for layer in range(2):
                if layer == 1:
                    norm_pe(pe)
                    meet(pe, "pe")
                    mla_in_pe(pe)
                    meet(pe, "pe")
                    with pe.Fori(0, NPAIR) as it:
                        attn_pe(pe, it)
                        meet(pe, "pe")
                else:
                    meet(pe, "pe")
                out_pe(pe, layer)
                meet(pe, "pe")
                norm_pe(pe)
                meet(pe, "pe")
                route_pe(pe, layer)
                meet(pe, "pe")
                with pe.Fori(0, NE // 2) as it:
                    moe_pe(pe, it, layer)
                meet(pe, "pe")

        @block.scalar
        def _(act):
            meet(act, "act")
            norm_act(act, True)
            meet(act, "act")
            pre_act(act)
            meet(act, "act")
            meet(act, "act")
            first_act(act)
            meet(act, "act")
            with act.Fori(0, NPAIR // 2) as it:
                pairs_act(act, it)
                meet(act, "act")
            for layer in range(2):
                if layer == 1:
                    norm_act(act, False)
                    meet(act, "act")
                    mla_in_act(act)
                    meet(act, "act")
                    with act.Fori(0, NPAIR) as it:
                        attn_act(act, it)
                        meet(act, "act")
                else:
                    nc.scalar.copy(yT[:, 0:4, :], y_all[:, 0:4, :])
                    meet(act, "act")
                meet(act, "act")
                norm_act(act, False)
                meet(act, "act")
                route_act(act)
                meet(act, "act")
                with act.Fori(0, NE // 2) as it:
                    moe_act(act, it)
                meet(act, "act")

        @block.vector
        def _(dve):
            meet(dve, "dve")
            norm_dve(dve, 0)
            meet(dve, "dve")
            pre_dve(dve)
            meet(dve, "dve")
            masks_dve(dve)
            meet(dve, "dve")
            first_dve(dve)
            meet(dve, "dve")
            with dve.Fori(0, NPAIR // 2) as it:
                pairs_dve(dve, it)
                meet(dve, "dve")
            for layer in range(2):
                if layer == 1:
                    norm_dve(dve, 2)
                    meet(dve, "dve")
                    mla_in_dve(dve)
                    meet(dve, "dve")
                    with dve.Fori(0, NPAIR) as it:
                        attn_dve(dve, it)
                        meet(dve, "dve")
                else:
                    nc.vector.tensor_copy(yT[:, 4:8, :], y_all[:, 4:8, :])
                    meet(dve, "dve")
                out_dve(dve, layer)
                meet(dve, "dve")
                norm_dve(dve, 2 * layer + 1)
                meet(dve, "dve")
                route_dve(dve)
                meet(dve, "dve")
                dve.sem_inc(pick_ready, 1)
                with dve.Fori(0, NE // 2) as it:
                    moe_dve(dve, it)
                meet(dve, "dve")

        @block.sync
        def _(sp):
            load_x(sp, ld_x)
            load_gain(sp, 0)
            for dst, w in ((w1_sb, "rw_w1"), (a1_sb, "rw_a1")):
                for e in range(2):
                    sp.dma_start(dst[:, :, e * LORA:(e + 1) * LORA], a[w][0, e].rearrange("(k p) n -> p k n", p=P)).then_inc(ld_lora, 16)
            for lo, hi in ((0, GATE // 2), (GATE // 2, GATE)):
                sp.dma_start(g1_sb[:, :, lo:hi], a["rw_g1"][0].rearrange("(k p) n -> p k n", p=P)[:, :, lo:hi]).then_inc(ld_lora, 16)
            rows = [(V_MU, a["rw_mu"][0].rearrange("g (k p) -> (g k) p", p=P), 6), (V_KK, a["rw_kk"][0].rearrange("(k p) -> k p", p=P), 1),
                    (V_KA, a["rw_ka"][0].rearrange("(k p) -> k p", p=P), 1), (V_W0, a["rw_w0"][0].rearrange("g (k p) -> (g k) p", p=P), 2),
                    (V_A0, a["rw_a0"][0].rearrange("g (k p) -> (g k) p", p=P), 2), (V_GNG, a["rw_gn_g"][0].rearrange("(k p) -> k p", p=P), 1),
                    (V_GNB, a["rw_gn_b"][0].rearrange("(k p) -> k p", p=P), 1), (V_RK, a["rw_rk"][0].rearrange("(k u) j -> k (u j)", u=2), 1)]
            for at, src, n in rows:
                sp.dma_start(vec_rows[at * ND:(at + n) * ND, :], src).then_inc(ld_vec, 16)
            meet(sp, "sp")
            pair_loads(sp, 0)
            gate_loads(sp, 0)
            meet(sp, "sp")
            pair_loads(sp, 1)
            with sp.Fori(0, NPAIR // 2) as it:
                for u in range(2):
                    for x in ("g", "v"):
                        sp.wait_ge(full[rj[(x, u)][0]], rj[(x, u)][1])
                    gate_loads(sp, (it * 2 + (u + 1)) & (NPAIR - 1))
                    pair_loads(sp, (it * 2 + (u + 2)) & (NPAIR - 1))
                meet(sp, "sp")
            sp.wait_ge(ld_pair, 16 * 5 * (NPAIR + 2))
            sp.wait_ge(ld_gate, 16 * 2 * (NPAIR + 1))
            meet(sp, "sp")
            load_x(sp, ld_x2)
            wo = [a[w][0].rearrange("(k p) n -> p k n", p=P) for w in ("rw_wo", "mla_w_o")]
            router = [a["moe_router"][n].rearrange("(k p) n -> p k n", p=P) for n in range(2)]
            sp.dma_start(wo_sb, wo[0]).then_inc(ld_wo[0], 16)
            load_gain(sp, 1)
            sp.dma_start(router_sb, router[0]).then_inc(ld_router[0], 16)
            load_experts(sp, 0)
            meet(sp, "sp")
            load_gain(sp, 2)
            sp.dma_start(win_sb, a["mla_w_in"][0].rearrange("(k p) n -> p k n", p=P)).then_inc(ld_win, 16)
            sp.dma_start(norm_rows[0:QL // P, :], a["mla_q_norm_g"][0].rearrange("(k p) -> k p", p=P)).then_inc(ld_mla, 16)
            sp.dma_start(norm_rows[QL // P:(QL + KVL) // P, :], a["mla_kv_norm_g"][0].rearrange("(k p) -> k p", p=P)).then_inc(ld_mla, 16)
            sp.dma_start(head_gain[:, 0, :], a["mla_q_head_g"][0:1, :].to_broadcast([P, QK])).then_inc(ld_mla, 16)
            sp.dma_start(head_gain[:, 1, :], a["mla_k_head_g"][0:1, :].to_broadcast([P, QK])).then_inc(ld_mla, 16)
            sp.dma_start(pos_i, a["positions"][0].rearrange("(t p) -> p t", p=P), allow_slow_non_contiguous=True).then_inc(ld_mla, 16)
            attn_loads(sp, 0)
            meet(sp, "sp")
            sp.dma_start(wo_sb, wo[1]).then_inc(ld_wo[1], 16)
            load_gain(sp, 3)
            with sp.Fori(0, NPAIR) as it:
                sp.wait_ge(full[aj[("kv", 1)][0]], aj[("kv", 1)][1])
                attn_loads(sp, (it + 1) & (NPAIR - 1))
                meet(sp, "sp")
            sp.wait_ge(ld_pair2, 32 * (NPAIR + 1))
            sp.dma_start(router_sb, router[1]).then_inc(ld_router[1], 16)
            load_experts(sp, 1)
            meet(sp, "sp")
            o = a["out"][0].rearrange("(t p) d -> p t d", p=P)
            for t in range(NT):
                sp.dma_start(o[:, t, :], x_sb[:, t, :]).then_inc(stored, 16)
            sp.wait_ge(stored, 16 * NT)


_INS = ['x', 'positions', 'norm_mix_g', 'norm_ffn_g', 'rw_mu', 'rw_wr', 'rw_wk', 'rw_wv', 'rw_wo', 'rw_w0', 'rw_w1',
        'rw_w2', 'rw_a0', 'rw_a1', 'rw_a2', 'rw_g1', 'rw_g2', 'rw_kk', 'rw_ka', 'rw_rk', 'rw_gn_g', 'rw_gn_b',
        'mla_w_in', 'mla_q_norm_g', 'mla_kv_norm_g', 'mla_w_uq', 'mla_w_ukv', 'mla_q_head_g', 'mla_k_head_g',
        'mla_w_o', 'moe_router', 'moe_w_gate', 'moe_w_up', 'moe_w_down']


def kernel(**inputs):
    import concourse.bacc as bacc
    from concourse.bass_utils import run_bass_kernel_spmd

    nc = bacc.Bacc("TRN2", target_bir_lowering=False, num_devices=1)
    arrays, args = {}, {}
    for name in _INS:
        arrays[f"in_{name}"] = np.ascontiguousarray(inputs[name])
        args[name] = nc.dram_tensor(f"in_{name}", arrays[f"in_{name}"].shape, mybir.dt.from_np(arrays[f"in_{name}"].dtype),
                                    kind="ExternalInput").ap()
    args["out"] = nc.dram_tensor("out_dram", (1, S, D), F32, kind="ExternalOutput").ap()
    trunk(nc, args)
    r = run_bass_kernel_spmd(nc, [arrays], core_ids=[0])
    return r.results[0]["out_dram"]
```

```python
from contextlib import ExitStack

import numpy as np

import concourse.bass as bass
from concourse import mybir

F32 = mybir.dt.float32
I32 = mybir.dt.int32
ALU = mybir.AluOpType
ACT = mybir.ActivationFunctionType
AX = mybir.AxisListType.X

P = 128
D = 1024
S = 512
NT = S // P
ND = D // P
NORM_EPS = 1e-6
HEAD = 64
LORA = 64
GATE = 160
GN_EPS = 64e-5
NPAIR = D // (2 * HEAD)
DECAY = -float(np.exp(-0.5))
LEVELS = 7
NOPE = 64
ROPE = 32
VH = 64
QL = 384
KVL = 256
QK = NOPE + ROPE
HALF = ROPE // 2
THETA = 10000.0
NE = 16
FF = 1024
CAP = 2 * S // NE
NB = 8
RING = 6
CHUNK = ND * 512
CPP = 12

V_MU, V_KK, V_KA, V_W0, V_A0, V_GNG, V_GNB, V_RK, V_N = 0, 6, 7, 8, 10, 12, 13, 14, 15


class Jobs:

    def __init__(self, order):
        self.at, self.count = {}, [0] * NB
        for name, bank in order:
            self.count[bank] += 1
            self.at[name] = (bank, self.count[bank])

    def __getitem__(self, name):
        return self.at[name]


def trunk(nc, a):
    with ExitStack() as ctx:
        sem = lambda name: ctx.enter_context(nc.semaphore(name))
        sb = lambda name, shape, dt=F32: ctx.enter_context(nc.sbuf_tensor(name, shape, dt))

        ARENA = 51 * 1024
        arena = sb("arena", [P, ARENA])
        ident = sb("ident", [P, P])
        small = sb("small", [P, 640])
        small_at = [0]

        def tiny(n):
            o = small_at[0]
            small_at[0] += n
            assert small_at[0] <= 640
            return small[:, o:o + n]

        def place(start):
            at = [start]

            def take(*shape):
                n = int(np.prod(shape))
                v = arena[:, at[0]:at[0] + n]
                at[0] += n
                assert at[0] <= ARENA, at[0]
                if len(shape) > 1:
                    names = "abcde"[:len(shape)]
                    v = v.rearrange(f"p ({' '.join(names)}) -> p {' '.join(names)}",
                                    **{c: s for c, s in zip(names, shape)})
                return v
            take.at = at
            return take

        ps = [ctx.enter_context(nc.psum_tensor(f"bank{b}", [P, 512], F32)) for b in range(NB)]

        RING0 = ARENA - RING * CHUNK
        ring = [arena[:, RING0 + s * CHUNK:RING0 + (s + 1) * CHUNK].rearrange("p (k n) -> p k n", k=ND)
                for s in range(RING)]
        common = place(0)
        x_sb = common(NT, D)

        h_tok = common(NT, D)
        hT = common(ND, S)
        AFTER_H = common.at[0]

        pre = place(AFTER_H)
        gain_row = pre(D)
        vec_rows = pre(P)
        w1_sb = pre(ND, 2 * LORA)
        a1_sb = pre(ND, 2 * LORA)
        g1_sb = pre(ND, GATE)
        keep = place(ARENA - (3 * ND * S + 4 * S))
        xmix = [keep(ND, S) for _ in range(3)]
        lora_w = keep(S)
        lora_a = keep(S)
        gate_a, gate_b = keep(S), keep(S)
        assert pre.at[0] <= ARENA - (3 * ND * S + 4 * S)
        shift = h_tok.rearrange("p t d -> p (t d)").rearrange("p (k s) -> p k s", k=ND)

        body = place(0)
        w_sl = body(3, ND, P)
        w2_sl, a2_sl, g2a_sl, g2b_sl = body(P), body(P), body(P), body(P)
        strict_incl = [body(2, P) for _ in range(2)]
        level_mask = body(LEVELS, P)
        head_ones = body(P)
        rT, kT, vT, kkn, kraw, tw, ta, cs, cx, rk_cols = (body(S) for _ in range(10))
        e_neg = kraw
        Bt = [body(NT, P) for _ in range(2)]
        Kt = [body(NT, P) for _ in range(2)]
        AR = [[body(NT, 2, P) for _ in range(2)] for _ in range(2)]
        btok = [body(NT, P) for _ in range(2)]
        ktok = [body(NT, P) for _ in range(2)]
        vtok = body(NT, P)
        LTRB = [[body(NT, 2, P) for _ in range(2)] for _ in range(2)]
        MTRK = [[body(NT, 2, P) for _ in range(2)] for _ in range(2)]
        TT = [body(2, NT, P) for _ in range(2)]
        Tm = [body(2, NT, P) for _ in range(2)]
        Xm = [body(2, NT, P) for _ in range(2)]
        bonus = [body(S) for _ in range(2)]
        gT, ytok_flat, ysq = body(S), body(S), body(S)
        y_out = [body(S) for _ in range(2)]
        assert body.at[0] <= ARENA - (3 * ND * S + 4 * S), (body.at[0], ARENA - (3 * ND * S + 4 * S))
        chain_x = Xm[0].rearrange("p h m j -> p (h m j)")[:, 0:256].rearrange("p (h d v) -> p h d v", h=2, d=2)
        chain_u = Xm[0].rearrange("p h m j -> p (h m j)")[:, 256:512].rearrange("p (h d v) -> p h d v", h=2, d=2)
        flat_x1 = Xm[1].rearrange("p h m j -> p (h m j)")
        states = [flat_x1[:, z * 128:(z + 1) * 128].rearrange("p (d v) -> p d v", d=2) for z in range(2)]
        state_dec = flat_x1[:, 256:384].rearrange("p (d v) -> p d v", d=2)
        ytok = ytok_flat.rearrange("p (t h v) -> p t h v", t=NT, h=2)

        cols = tiny(V_N * ND)
        pc = tiny(V_N)
        half_col = tiny(2 * 2)
        end_dec = [tiny(2 * NT).rearrange("p (d m) -> p d m", d=2) for _ in range(2)]
        stat = tiny(8)
        stat2 = tiny(8)
        rstd8 = tiny(8)
        mhalf = tiny(16)
        ssum = tiny(4)
        rstd4 = tiny(4)
        iota_s = tiny(CAP)

        proj = place(AFTER_H + D)
        wo_sb = proj(ND, D)
        assert proj.at[0] <= RING0
        yT = hT
        y_dram = a["out"][0].rearrange("(k q) (c s) -> k (q c) s", k=NPAIR, c=2)

        moe = place(AFTER_H + D)
        xeT = moe(ND, 2 * CAP)
        hidT = [moe(ND, CAP) for _ in range(2)]
        hid_tok = [moe(FF) for _ in range(2)]
        th = [moe(512) for _ in range(2)]
        ye = moe(D)
        combT = moe(S)
        pick = moe(NT, 2 * CAP)
        pick_gate = moe(NT, 2 * CAP)
        aff = moe(NT, NE + 2)
        slot = moe(NT, NE + 2)
        affT, workT, maskT, cumT = moe(S), moe(S), moe(S), moe(S)
        top8 = moe(8)
        logit = moe(NT, NE)
        iota_i = moe(CAP).bitcast(I32)
        assert max(proj.at[0], moe.at[0]) <= RING0 - ND * NE
        router_sb = arena[:, RING0 - ND * NE:RING0].rearrange("p (k n) -> p k n", k=ND)

        hbuf = place(NT * D)
        prob = [hbuf(NT, S) for _ in range(2)]
        inp = place(AFTER_H + D)
        win_sb = inp(ND, QL + KVL + ROPE)
        c_tok = inp(NT, QL + KVL + ROPE)
        mla = place(AFTER_H + D + ND * D)
        assert inp.at[0] <= mla.at[0]
        cT = mla((QL + KVL) // P, S)
        wq_sl = mla(QL // P, 2 * QK)
        wkv_sl = mla(KVL // P, 2 * (NOPE + VH))
        q_tok, k_tok = mla(NT * 2, QK), mla(NT * 2, QK)
        q_sq, k_sq = mla(NT * 2, QK), mla(NT * 2, NOPE)
        v_tok = [mla(NT, 2, VH) for _ in range(2)]
        qkT = [[mla(S) for _ in range(2)] for _ in range(2)]
        probT = [mla(NT, S) for _ in range(2)]
        norm_rows = mla(P)
        head_gain = mla(2, QK)
        k_rope = mla(NT, ROPE)
        cos8, sin8 = mla(NT * 2, HALF), mla(NT * 2, HALF)
        ang, red, rnd = mla(NT, HALF), mla(NT, HALF), mla(NT, HALF)
        freq = mla(HALF)
        pos_f = mla(NT)
        pos_i = mla(NT).bitcast(I32)
        rtmp = [mla(NT * 2, HALF) for _ in range(4)]
        gain_cols = tiny(2)
        krope_ss = tiny(NT)
        kss, krstd, qss = tiny(8), tiny(8), tiny(8)
        q_scale = [tiny(8) for _ in range(2)]
        q_scale_neg = [tiny(8) for _ in range(2)]
        norm_cols = tiny(8)
        ss_c = tiny(8)
        rstd_c = tiny(8)
        mx = tiny(8)
        nmx = tiny(8)
        lsum = tiny(8)
        linv = tiny(8)
        rmax = tiny(NT)
        rsum_t = tiny(NT)

        full = [sem(f"bank_full{b}") for b in range(NB)]
        free = [sem(f"bank_free{b}") for b in range(NB)]
        sq_ready = sem("squares_summed")
        rstd_ready = sem("rstd_ready")
        h_ready = sem("h_ready")
        consts_ready = sem("consts_ready")
        mix_ready = sem("mix_ready")
        gate_ready = sem("gate_ready")
        cols_ready = sem("pair_cols_ready")
        ksq_ready = sem("ksq_ready")
        knorm_clamped = sem("knorm_clamped")
        knorm_root = sem("knorm_root")
        cum_ready = sem("cumulated_ready")
        exps_ready = sem("exps_ready")
        operands_ready = sem("operands_ready")
        ydone_ready = sem("y_done")
        ttinit_ready = sem("inverse_t_started")
        state_ready = sem("state_ready")
        ycen_ready = sem("y_centred")
        ysq_ready = sem("y_squares")
        yvar_ready = sem("y_variance")
        yrstd_ready = sem("y_rstd")
        ynorm_ready = sem("y_normed")
        logit_ready = sem("logit_ready")
        exp_ready = sem("exp_ready")
        aff_ready = sem("aff_ready")
        slot_ready = sem("slot_ready")
        iota_ready = sem("iota_ready")
        pick_ready = sem("pick_ready")
        tanh_ready = sem("tanh_ready")
        hid_ready = sem("hid_ready")
        css_ready = sem("css_ready")
        crstd_ready = sem("crstd_ready")
        cnorm_ready = sem("cnorm_ready")
        red_ready = sem("angles_reduced")
        trig_ready = sem("trig_ready")
        freq_ready = sem("freq_ready")
        krstd_ready = sem("krstd_ready")
        k_ready = sem("k_ready")
        qksq_ready = sem("qksq_ready")
        qkss_ready = sem("qkss_ready")
        qkrstd_ready = sem("qkrstd_ready")
        qk_ready = sem("qk_ready")
        max_ready = sem("max_ready")
        prob_ready = sem("prob_ready")
        banks = full + free
        norm_sems = banks + [sq_ready, rstd_ready, h_ready]
        inputs_sems = banks + [mix_ready, gate_ready]
        prep_sems = banks + [cols_ready, ksq_ready, knorm_clamped, knorm_root, cum_ready, exps_ready, operands_ready]
        y_sems = [ycen_ready, ysq_ready, yvar_ready, yrstd_ready, ynorm_ready, ydone_ready]
        pairs_sems = prep_sems + y_sems + [ttinit_ready, state_ready]
        route_sems = banks + [logit_ready, exp_ready, aff_ready, slot_ready, iota_ready]
        moe_sems = banks + [pick_ready, tanh_ready, hid_ready]
        mla_in_sems = banks + [css_ready, crstd_ready, cnorm_ready, red_ready, trig_ready, freq_ready]
        heads_sems = banks + [ksq_ready, qkss_ready, krstd_ready, k_ready, qksq_ready, qkrstd_ready, qk_ready]
        attn_sems = heads_sems + [max_ready, prob_ready]
        arrive = sem("arrive")
        arrive_sp = sem("arrive_sp")
        go = {e: sem(f"go_{e}") for e in ("pe", "act", "dve", "sp")}
        ld_x = sem("ld_x")
        ld_x2 = sem("ld_x2")
        ld_gain = [sem(f"ld_gain{n}") for n in range(4)]
        ld_vec = sem("ld_vec")
        ld_lora = sem("ld_lora")
        ld_pair = sem("ld_pair")
        ld_gate = sem("ld_gate")
        y_stored, ld_y = sem("y_stored"), sem("ld_y")
        ld_wo = [sem(f"ld_wo{n}") for n in range(2)]
        ld_router = [sem(f"ld_router{n}") for n in range(2)]
        ld_chunk = [sem(f"ld_chunk{s}") for s in range(RING)]
        ld_win = sem("ld_win")
        ld_mla = sem("ld_mla")
        ld_pair2 = sem("ld_pair2")
        stored = sem("stored")
        waited, waited_sp = sem("waited"), sem("waited_sp")
        chunk_used = [sem(f"chunk_used{n}") for n in range(2)]

        block = ctx.enter_context(nc.Block())

        def meet(eng, name):
            eng.drain().then_inc(arrive_sp if name == "sp" else arrive, 1)
            eng.wait_ge(go[name], 1)
            eng.sem_clear(go[name])

        def meet_pool(pool, used, names=("pe", "act", "dve"), credit=0):
            pool.drain()
            pool.wait_ge(arrive, 3)
            pool.sem_clear(arrive)
            if "sp" in names:
                pool.wait_ge(arrive_sp, 1)
                pool.sem_clear(arrive_sp)
            for s in used:
                pool.sem_clear(s)
            if credit:
                for s in free:
                    pool.sem_inc(s, credit)
            for n in names:
                pool.sem_inc(go[n], 1)

        def open_job(pe, jobs, name):
            b, n = jobs[name]
            if n > 1:
                pe.wait_ge(free[b], n - 1)
            return ps[b]

        def job_full(eng, jobs, name):
            b, n = jobs[name]
            eng.wait_ge(full[b], n)
            return ps[b]

        def job_read(eng, jobs, name):
            b, n = jobs[name]
            eng.wait_ge(free[b], n)

        norm_jobs = Jobs([(k, k) for k in range(ND)])

        def norm_act(act, x_loaded):
            if x_loaded:
                act.wait_ge(ld_x, 16 * NT)
            for t in range(NT):
                nc.scalar.activation(h_tok[:, t, :], x_sb[:, t, :], ACT.Square,
                                     accum_out=ssum[:, t:t + 1]).then_inc(sq_ready, 1)
            for k in range(0, ND, 2):
                b = job_full(act, norm_jobs, k)
                nc.scalar.copy(hT[:, k, :], b[:, :]).then_inc(free[norm_jobs[k][0]], 1)

        def norm_pool(pool):
            pool.wait_ge(sq_ready, NT)
            nc.gpsimd.tensor_scalar(ssum, ssum, 1.0 / D, NORM_EPS, ALU.mult, ALU.add)
            pool.drain()
            nc.gpsimd.tensor_tensor(rstd4, ssum, mhalf[:, 0:4], ALU.pow).then_inc(rstd_ready, 1)

        def norm_dve(dve, n):
            dve.wait_ge(ld_gain[n], 16)
            dve.wait_ge(rstd_ready, 1)
            for t in range(NT):
                nc.vector.scalar_tensor_tensor(h_tok[:, t, :], x_sb[:, t, :], rstd4[:, t:t + 1], gain_row,
                                               ALU.mult, ALU.mult).then_inc(h_ready, 1)
            for k in range(1, ND, 2):
                b = job_full(dve, norm_jobs, k)
                nc.vector.tensor_copy(hT[:, k, :], b[:, :]).then_inc(free[norm_jobs[k][0]], 1)

        def norm_pe(pe):
            pe.wait_ge(h_ready, NT)
            for k in range(ND):
                b = open_job(pe, norm_jobs, k)
                for t in range(NT):
                    last = nc.tensor.transpose(b[:, t * P:(t + 1) * P], h_tok[:, t, k * P:(k + 1) * P], ident[:, :])
                last.then_inc(full[norm_jobs[k][0]], 1)

        MIX = [(1, 0), (4, 1), (5, 2), (0, 0), (2, 1), (3, 2)]
        pre_jobs = Jobs([("cols", 0), ("w", 1), ("a", 2), ("ga", 3), ("gb", 4)])

        def pre_pe(pe):
            pe.wait_ge(ld_vec, 16 * 8)
            nc.tensor.transpose(ps[0][:, 0:V_N * ND], vec_rows[0:V_N * ND, :],
                                ident[0:V_N * ND, 0:V_N * ND]).then_inc(full[0], 1)
            pe.wait_ge(ld_lora, 16 * 6)
            for n, (name, w, m) in enumerate([("w", w1_sb, P), ("a", a1_sb, P), ("ga", g1_sb, P), ("gb", g1_sb, GATE - P)]):
                src = xmix[min(n, 2)]
                pe.wait_ge(mix_ready, ND * (min(n, 2) + 1))
                b = open_job(pe, pre_jobs, name)
                lo = P if name == "gb" else 0
                for k in range(ND):
                    last = nc.tensor.matmul(b[0:m, :], w[:, k, lo:lo + m], src[:, k, :],
                                            start=(k == 0), stop=(k == ND - 1))
                last.then_inc(full[pre_jobs[name][0]], 1)

        def pre_act(act):
            for name, dst, m, f in (("w", lora_w, P, ACT.Tanh), ("a", lora_a, P, ACT.Copy)):
                b = job_full(act, pre_jobs, name)
                nc.scalar.activation(dst[0:m, :], b[0:m, :], f).then_inc(free[pre_jobs[name][0]], 1)
            for name, dst, m in (("ga", gate_a, P), ("gb", gate_b, GATE - P)):
                b = job_full(act, pre_jobs, name)
                nc.scalar.activation(dst[0:m, :], b[0:m, :], ACT.Tanh, scale=0.5).then_inc(gate_ready, 1)

        def pre_dve(dve):
            job_full(dve, pre_jobs, "cols")
            nc.vector.tensor_copy(cols, ps[0][:, 0:V_N * ND])
            nc.vector.tensor_tensor(shift[:, :, 1:S - 1], hT[:, :, 0:S - 2], hT[:, :, 2:S], ALU.add)
            nc.vector.tensor_copy(shift[:, :, 0:1], hT[:, :, 1:2])
            nc.vector.tensor_copy(shift[:, :, S - 1:S], hT[:, :, S - 2:S - 1])
            dve.drain()
            for k in range(ND):
                nc.vector.scalar_tensor_tensor(shift[:, k, :], shift[:, k, :], 0.5, hT[:, k, :], ALU.mult, ALU.subtract)
            dve.drain()
            for n, (row, buf) in enumerate(MIX):
                if n >= 3:
                    dve.wait_ge(full[pre_jobs[("w", "a", "gb")[n - 3]][0]], 1)
                for k in range(ND):
                    nc.vector.scalar_tensor_tensor(xmix[buf][:, k, :], shift[:, k, :],
                                                   cols[:, (V_MU + row) * ND + k:(V_MU + row) * ND + k + 1],
                                                   hT[:, k, :], ALU.mult, ALU.add).then_inc(mix_ready, 1)
            dve.wait_ge(gate_ready, 2)
            nc.vector.tensor_scalar(gate_a, gate_a, 0.5, 0.5, ALU.mult, ALU.add)
            nc.vector.tensor_scalar(gate_b[0:GATE - P, :], gate_b[0:GATE - P, :], 0.5, 0.5, ALU.mult, ALU.add)

        ii, jj = cs.bitcast(I32), cx.bitcast(I32)

        def masks_pool(pool):
            nc.gpsimd.iota(ii[:, 0:P], [[0, P]], base=0, channel_multiplier=1)
            nc.gpsimd.iota(jj[:, 0:P], [[1, P]], base=0, channel_multiplier=0)
            for m in (strict_incl[0], strict_incl[1]):
                nc.gpsimd.memset(m, 1.0)
            pool.drain()
            for d, sgn in ((0, 1), (1, -1)):
                for z in range(2):
                    v = strict_incl[d][:, z, :]
                    nc.gpsimd.affine_select(out=v, in_=v, compare_op=ALU.is_ge, fill=0.0, base=z - 1,
                                            pattern=[[sgn, P]], channel_multiplier=-sgn)
            pool.drain().then_inc(consts_ready, 1)

        def masks_dve(dve):
            for v in (ytok_flat, gT, bonus[1]):
                nc.vector.memset(v, 0.0)
            dve.wait_ge(consts_ready, 1)
            nc.vector.tensor_tensor(ii[:, P:2 * P], ii[:, 0:P], jj[:, 0:P], ALU.bitwise_xor)
            dve.drain()
            xor = cs[:, 2 * P:3 * P]
            nc.vector.tensor_copy(xor, ii[:, P:2 * P])
            dve.drain()
            nc.vector.tensor_scalar(head_ones, xor, float(HEAD), None, ALU.is_lt)
            for n in range(LEVELS):
                nc.vector.tensor_scalar(cx[:, P:2 * P], xor, float(2 ** (n + 1)), None, ALU.is_lt)
                dve.drain()
                nc.vector.scalar_tensor_tensor(level_mask[:, n, :], xor, float(2 ** n), cx[:, P:2 * P],
                                               ALU.is_ge, ALU.mult)
                dve.drain()

        PE_WITH = {0: [("r",)], 1: [("k",)], 2: [("kn",)], 3: [("wa", 0)], 6: [("wa", 1)]}
        ACT_WITH = {0: [("r",)], 1: [("k",)], 2: [("kkn",)], 3: [("wa", 0)], 4: [("cum", 0)], 6: [("wa", 1)]}
        DVE_WITH = {2: [("kn",)], 3: [("kkn",)], 4: [("cum", 0)], 5: [("rate", 0), ("ops", 0)]}
        DVE_CHAIN = {0: [("cum", 1)], 1: [("rate", 1)], 2: [("ops", 1)]}
        ACT_CHAIN = {1: [("cum", 1)]}
        ALONE = [("r",), ("k",), ("kn",), ("wa", 0), ("kkn",), ("cum", 0), ("rate", 0), ("ops", 0), ("wa", 1), ("cum", 1),
                 ("rate", 1), ("ops", 1)]
        PREP_BANK = {"r": 6, "k": 7, "kn": 6, "w0": 7, "a0": 6, "w1": 7, "a1": 6}

        def prep_jobs(piece, u):
            names = {"r": ["r"], "k": ["k"], "kn": ["kn"]}.get(piece[0])
            if piece[0] == "wa":
                names = [f"w{piece[1]}", f"a{piece[1]}"]
            return [((x, u), PREP_BANK[x]) for x in names or []]

        CHAINS = [(d, h) for d in range(2) for h in range(2)]
        order = []
        for u in range(2):
            order += [(("bonus", u), 0), (("vt", u), 1), (("bt0", u), 2), (("kt0", u), 3), (("bt1", u), 4), (("kt1", u), 5)]
            rot = 0
            for nm in ("LR", "MR"):
                for d in range(2):
                    for z in range(2):
                        for h in range(2):
                            order.append(((f"{nm}{z}", d, h, u), rot % 6))
                            rot += 1
            for piece in PE_WITH[0]:
                order += prep_jobs(piece, u)
            order += [(("T0", d, h, u), 4 + h) for d, h in CHAINS]
            for lv in range(1, LEVELS):
                order += [(("X", lv, d, h, u), 2 * d + h) for d, h in CHAINS]
                if lv == 2:
                    order.append((("yT", u), 7))
                for piece in PE_WITH.get(lv, []):
                    order += prep_jobs(piece, u)
                order += [(("TX", lv, d, h, u), 2 * d + h) for d, h in CHAINS]
                if lv < LEVELS - 1:
                    order += [(("Tr", lv, d, h, u), 4 + h) for d, h in CHAINS]
            for m in range(NT):
                order += [(("cx", m, 0, u), 1), (("cx", m, 1, u), 2)]
                order += [(("g", u), 0)] if m == 0 else []
                order += [(("cu", m, u), 3)]
                if m < NT - 1:
                    order += [(("cs", m, u), 4)]
            order += [(("v", u), 5), (("y", 0, u), 6), (("y", 1, u), 7)]
        rj = Jobs(order)
        alone = []
        for piece in ALONE:
            alone += prep_jobs(piece, 0)
        pj = Jobs(alone + [(("v", 0), 5)])

        def bc(v, *shape):
            return v.to_broadcast(list(shape))

        flat = lambda v: v.rearrange("p m j -> p (m j)")
        split = lambda v: v.rearrange("p (m j) -> p m j", m=NT)

        def prep_pe(pe, piece, jb, u, loads):
            if piece[0] in ("r", "k"):
                n = {"r": 0, "k": 1}[piece[0]]
                if n == 0:
                    pe.wait_ge(ld_pair, loads * (16 * 5))
                b = open_job(pe, jb, (piece[0], u))
                for k in range(ND):
                    last = nc.tensor.matmul(b[:, :], w_sl[:, n, k, :], xmix[n][:, k, :], start=(k == 0), stop=(k == ND - 1))
                last.then_inc(full[jb[(piece[0], u)][0]], 1)
            if piece[0] == "kn":
                b = open_job(pe, jb, ("kn", u))
                pe.wait_ge(ksq_ready, u + 1)
                nc.tensor.matmul(b[:, :], head_ones, kraw, start=True, stop=True).then_inc(full[jb[("kn", u)][0]], 1)
            if piece[0] == "wa":
                d = piece[1]
                q = slice(d * LORA, (d + 1) * LORA)
                for kind, w, src in (("w", w2_sl, lora_w), ("a", a2_sl, lora_a)):
                    b = open_job(pe, jb, (f"{kind}{d}", u))
                    nc.tensor.matmul(b[:, :], w[q, :], src[q, :], start=True, stop=True).then_inc(full[jb[(f"{kind}{d}", u)][0]], 1)

        def v_piece(pe, jb, u, k):
            b = open_job(pe, jb, ("v", u)) if k == 0 else ps[jb[("v", u)][0]]
            last = nc.tensor.matmul(b[:, :], w_sl[:, 2, k, :], xmix[2][:, k, :], start=(k == 0), stop=(k == ND - 1))
            if k == ND - 1:
                last.then_inc(full[jb[("v", u)][0]], 1)

        def prep_act(act, piece, jb, u):
            if piece[0] == "r":
                b = job_full(act, jb, ("r", u))
                nc.scalar.copy(rT, b[:, :]).then_inc(free[jb[("r", u)][0]], 1)
            if piece[0] == "k":
                b = job_full(act, jb, ("k", u))
                act.wait_ge(cols_ready, u + 1)
                nc.scalar.activation(kraw, b[:, :], ACT.Square, scale=pc[:, V_KK:V_KK + 1]).then_inc(ksq_ready, 1)
                nc.scalar.copy(kT, b[:, :]).then_inc(free[jb[("k", u)][0]], 1)
            if piece[0] == "kkn":
                act.wait_ge(knorm_clamped, u + 1)
                nc.scalar.activation(cx, cs, ACT.Sqrt).then_inc(knorm_root, 1)
            if piece[0] == "wa":
                d = piece[1]
                if d == 1:
                    act.wait_ge(operands_ready, 2 * u + 1)
                for kind, dst, hc in (("w", tw, d), ("a", ta, 2 + d)):
                    b = job_full(act, jb, (f"{kind}{d}", u))
                    nc.scalar.activation(dst, b[:, :], ACT.Tanh, bias=half_col[:, hc:hc + 1], scale=0.5).then_inc(free[jb[(f"{kind}{d}", u)][0]], 1)
            if piece[0] == "cum":
                act.wait_ge(cum_ready, 2 * u + piece[1] + 1)
                nc.scalar.activation(e_neg, cs, ACT.Exp, scale=-1.0)
                nc.scalar.activation(cx, cx, ACT.Exp)
                act.drain()
                nc.scalar.activation(cs, cs, ACT.Exp).then_inc(exps_ready, 1)

        def prep_cols(dve, pair):
            nc.vector.tensor_copy(pc.unsqueeze(2), cols.rearrange("p (g q) -> p g q", q=ND)[:, :, bass.ds(pair, 1)])
            dve.drain()
            nc.vector.tensor_scalar(half_col, pc[:, V_W0:V_W0 + 4], 0.5, None, ALU.mult)
            dve.drain().then_inc(cols_ready, 1)

        def prep_dve(dve, piece, jb, u, par):
            d = piece[1] if len(piece) > 1 else 0
            if piece[0] == "kn":
                job_read(dve, jb, ("k", u))
                nc.vector.tensor_scalar(kkn, kT, pc[:, V_KK:V_KK + 1], None, ALU.mult)
                b = job_full(dve, jb, ("kn", u))
                nc.vector.tensor_scalar(cs, b[:, :], 1e-24, None, ALU.max).then_inc(knorm_clamped, 1)
                dve.drain().then_inc(free[jb[("kn", u)][0]], 1)
            if piece[0] == "kkn":
                dve.wait_ge(knorm_root, u + 1)
                nc.vector.reciprocal(cs, cx)
                dve.drain()
                nc.vector.tensor_tensor(kkn, kkn, cs, ALU.mult)
            if piece[0] == "cum":
                job_read(dve, jb, (f"w{d}", u))
                nc.vector.tensor_scalar(tw, tw, 0.5 * DECAY, 0.5 * DECAY, ALU.mult, ALU.add)
                dve.drain()
                for m in range(NT):
                    o, w = cs[:, m * P:(m + 1) * P], tw[:, m * P:(m + 1) * P]
                    if d == 0:
                        nc.vector.tensor_tensor_scan(o, w, w, 0.0, ALU.add, ALU.min)
                    else:
                        nc.vector.tensor_tensor_scan(o[:, ::-1], w[:, ::-1], w[:, ::-1], 0.0, ALU.add, ALU.min)
                dve.drain()
                nc.vector.tensor_tensor(cx, cs, tw, ALU.subtract).then_inc(cum_ready, 1)
            if piece[0] == "rate":
                job_read(dve, jb, (f"a{d}", u))
                nc.vector.tensor_scalar(ta, ta, 0.5, 0.5, ALU.mult, ALU.add)
                dve.drain()
                nc.vector.tensor_scalar(tw, ta, -1.0, pc[:, V_KA:V_KA + 1], ALU.add, ALU.mult)
                nc.vector.tensor_tensor(ta, ta, kkn, ALU.mult)
                dve.drain()
                nc.vector.scalar_tensor_tensor(tw, tw, 1.0, kT, ALU.add, ALU.mult)
                dve.drain()
            if piece[0] == "ops":
                dve.wait_ge(exps_ready, 2 * u + d + 1)
                job_read(dve, jb, ("r", u))
                nc.vector.tensor_tensor(AR[par][d][:, :, 1, :], split(rT), split(cs), ALU.mult)
                nc.vector.scalar_tensor_tensor(AR[par][d][:, :, 0, :], split(kkn), -1.0, split(cx), ALU.mult, ALU.mult)
                nc.vector.tensor_tensor(flat(Bt[d]), ta, e_neg, ALU.mult)
                nc.vector.tensor_tensor(flat(Kt[d]), tw, e_neg, ALU.mult)
                if d == 0:
                    nc.vector.tensor_copy(rk_cols, tw)
                else:
                    nc.vector.tensor_tensor(rk_cols, rk_cols, tw, ALU.add)
                end = split(cs)[:, :, P - 1:P] if d == 0 else split(cs)[:, :, 0:1]
                nc.vector.tensor_copy(end_dec[par][:, d, :].unsqueeze(2), end)
                if d == 1:
                    dve.drain()
                    nc.vector.scalar_tensor_tensor(rk_cols, rk_cols, pc[:, V_RK:V_RK + 1], rT, ALU.mult, ALU.mult)
                dve.drain().then_inc(operands_ready, 1)

        def first_pe(pe):
            for piece in ALONE:
                prep_pe(pe, piece, pj, 0, 1)
            for k in range(ND):
                v_piece(pe, pj, 0, k)

        def first_act(act):
            for piece in ALONE:
                prep_act(act, piece, pj, 0)
            b = job_full(act, pj, ("v", 0))
            nc.scalar.copy(vT, b[:, :])

        def first_dve(dve):
            prep_cols(dve, 0)
            for piece in ALONE:
                prep_dve(dve, piece, pj, 0, 0)

        def turn(pe, name, src):
            b = open_job(pe, rj, name)
            for m in range(NT):
                last = nc.tensor.transpose(b[:, m * P:(m + 1) * P], src[:, m * P:(m + 1) * P], ident[:, :])
            last.then_inc(full[rj[name][0]], 1)

        def products(pe, name, st, mv):
            b = open_job(pe, rj, name)
            for m in range(NT):
                last = nc.tensor.matmul(b[:, m * P:(m + 1) * P], st[:, m, :], mv[:, m, :], start=True, stop=True)
            last.then_inc(full[rj[name][0]], 1)

        def pairs_pe(pe, it):
            for u in range(2):
                if u:
                    pe.wait_ge(operands_ready, 2)
                    job_read(pe, rj, ("v", 0))
                b = open_job(pe, rj, ("bonus", u))
                nc.tensor.matmul(b[:, :], head_ones, rk_cols, start=True, stop=True).then_inc(full[rj[("bonus", u)][0]], 1)
                turn(pe, ("vt", u), vT)
                for d in range(2):
                    turn(pe, (f"bt{d}", u), flat(Bt[d]))
                    turn(pe, (f"kt{d}", u), flat(Kt[d]))
                for nm, sts in (("LR", Bt), ("MR", Kt)):
                    for d in range(2):
                        for z in range(2):
                            bs = [open_job(pe, rj, (f"{nm}{z}", d, h, u)) for h in range(2)]
                            for y in range(2):
                                m = 2 * z + y
                                last = []
                                for h in range(2):
                                    q = slice(h * HEAD, (h + 1) * HEAD)
                                    last.append(nc.tensor.matmul(bs[h][:, y * 256:(y + 1) * 256], sts[d][q, m, :],
                                                                 AR[u][d][q, m, :, :].rearrange("p a b -> p (a b)"), start=True, stop=True))
                            for h in range(2):
                                last[h].then_inc(full[rj[(f"{nm}{z}", d, h, u)][0]], 1)
                for piece in PE_WITH[0]:
                    prep_pe(pe, piece, rj, u, it * 2 + (u + 2))
                for n, (d, h) in enumerate(CHAINS):
                    pe.wait_ge(ttinit_ready, 4 * u + n + 1)
                    turn(pe, ("T0", d, h, u), TT[d][:, h].rearrange("p m j -> p (m j)"))
                for lv in range(1, LEVELS):
                    for d, h in CHAINS:
                        job_read(pe, rj, ("T0", d, h, u) if lv == 1 else ("TX", lv - 1, d, h, u))
                        products(pe, ("X", lv, d, h, u), LTRB[d][h][:, :, 0, :], Tm[d][:, h])
                    if lv == 2:
                        pe.wait_ge(ynorm_ready, u + 1)
                        turn(pe, ("yT", u), ysq)
                    for piece in PE_WITH.get(lv, []):
                        prep_pe(pe, piece, rj, u, it * 2 + (u + 2))
                    for d, h in CHAINS:
                        job_read(pe, rj, ("X", lv, d, h, u))
                        if lv > 1:
                            job_read(pe, rj, ("Tr", lv - 1, d, h, u))
                        st, mv = (TT[d], Xm[d]) if lv < LEVELS - 1 else (Xm[d], TT[d])
                        products(pe, ("TX", lv, d, h, u), st[:, h], mv[:, h])
                    if lv < LEVELS - 1:
                        for d, h in CHAINS:
                            job_read(pe, rj, ("TX", lv, d, h, u))
                            turn(pe, ("Tr", lv, d, h, u), Tm[d][:, h].rearrange("p m j -> p (m j)"))
                for d in range(2):
                    for h in range(2):
                        job_read(pe, rj, ("TX", LEVELS - 1, d, h, u))
                        job_read(pe, rj, ("MR1", d, h, u))
                for x in ("vt", "bt0", "kt0", "bt1", "kt1"):
                    job_read(pe, rj, (x, u))
                for m in range(NT):
                    tile = (m, NT - 1 - m)
                    if m:
                        pe.wait_ge(state_ready, (NT - 1) * u + m)
                    bs = [open_job(pe, rj, ("cx", m, h, u)) for h in range(2)]
                    for d in range(2):
                        if m:
                            for h in range(2):
                                q = slice(h * HEAD, (h + 1) * HEAD)
                                nc.tensor.matmul(bs[h][:, d * HEAD:(d + 1) * HEAD], AR[u][d][q, tile[d], 0, :], states[m % 2][q, d, :],
                                                 start=True, stop=False)
                        for h in range(2):
                            q = slice(h * HEAD, (h + 1) * HEAD)
                            last = nc.tensor.matmul(bs[h][:, d * HEAD:(d + 1) * HEAD], MTRK[d][h][:, tile[d], 0, :], vtok[:, tile[d], q],
                                                    start=(m == 0), stop=True)
                            if d == 1:
                                last.then_inc(full[rj[("cx", m, h, u)][0]], 1)
                    if m == 0:
                        pe.wait_ge(ld_gate, it * 64 + (u + 1) * 32)
                        b = open_job(pe, rj, ("g", u))
                        nc.tensor.matmul(b[:, :], g2a_sl, gate_a, start=True, stop=False)
                        nc.tensor.matmul(b[:, :], g2b_sl[0:GATE - P, :], gate_b[0:GATE - P, :], start=False, stop=True).then_inc(full[rj[("g", u)][0]], 1)
                    v_piece(pe, rj, u, 2 * m)
                    b = open_job(pe, rj, ("cu", m, u))
                    for h in range(2):
                        job_read(pe, rj, ("cx", m, h, u))
                        for d in range(2):
                            last = nc.tensor.matmul(b[:, (2 * h + d) * HEAD:(2 * h + d + 1) * HEAD], TT[d][:, h, tile[d], :],
                                                    chain_x[:, h, d, :], start=True, stop=True)
                    last.then_inc(full[rj[("cu", m, u)][0]], 1)
                    v_piece(pe, rj, u, 2 * m + 1)
                    job_read(pe, rj, ("cu", m, u))
                    if m < NT - 1:
                        b = open_job(pe, rj, ("cs", m, u))
                        for h in range(2):
                            q = slice(h * HEAD, (h + 1) * HEAD)
                            for d in range(2):
                                o = b[q, d * HEAD:(d + 1) * HEAD]
                                nc.tensor.matmul(o, btok[d][:, tile[d], q], chain_u[:, h, d, :], start=True, stop=False)
                                last = nc.tensor.matmul(o, ktok[d][:, tile[d], q], vtok[:, tile[d], q], start=False, stop=True)
                        last.then_inc(full[rj[("cs", m, u)][0]], 1)
                    if m == 0:
                        for h in range(2):
                            open_job(pe, rj, ("y", h, u))
                    for d in range(2):
                        os = [ps[6 + h][:, tile[d] * HEAD:(tile[d] + 1) * HEAD] for h in range(2)]
                        for h in range(2):
                            q = slice(h * HEAD, (h + 1) * HEAD)
                            nc.tensor.matmul(os[h], MTRK[d][h][:, tile[d], 1, :], vtok[:, tile[d], q],
                                             start=(m == 0 and d == 0), stop=False, skip_group_check=True)
                        if m:
                            for h in range(2):
                                q = slice(h * HEAD, (h + 1) * HEAD)
                                nc.tensor.matmul(os[h], AR[u][d][q, tile[d], 1, :], states[m % 2][q, d, :],
                                                 start=False, stop=False, skip_group_check=True)
                        for h in range(2):
                            last = nc.tensor.matmul(os[h], LTRB[d][h][:, tile[d], 1, :], chain_u[:, h, d, :], start=False,
                                                    stop=(m == NT - 1), skip_group_check=True)
                            if m == NT - 1 and d == 1:
                                last.then_inc(full[rj[("y", h, u)][0]], 1)

        def last_y_pe(pe):
            pe.wait_ge(ynorm_ready, 1)
            for t in range(NT):
                last = nc.tensor.transpose(ps[0][:, t * P:(t + 1) * P], ysq[:, t * P:(t + 1) * P], ident[:, :])
            last.then_inc(full[0], 1)

        def y_square(act, n):
            act.wait_ge(ycen_ready, n)
            nc.scalar.activation(ysq, ytok_flat, ACT.Square).then_inc(ysq_ready, 1)

        def y_feature(act, bank, n, pair):
            act.wait_ge(full[bank], n)
            nc.scalar.activation(ytok_flat, ps[bank][:, :], ACT.Identity, bias=cols[:, bass.ds(pair + V_GNB * ND, 1)],
                                 scale=cols[:, bass.ds(pair + V_GNG * ND, 1)]).then_inc(free[bank], 1)

        def last_y_act(act):
            y_square(act, 1)
            y_feature(act, 0, 1, NPAIR - 1)

        def pairs_act(act, it):
            for u in range(2):
                for nm, dst in (("vt", vtok), ("bt0", btok[0]), ("kt0", ktok[0]), ("bt1", btok[1]), ("kt1", ktok[1])):
                    b = job_full(act, rj, (nm, u))
                    nc.scalar.copy(flat(dst), b[:, :]).then_inc(free[rj[(nm, u)][0]], 1)
                y_square(act, u + 1)
                for piece in ACT_WITH[0]:
                    prep_act(act, piece, rj, u)
                for d, h in CHAINS:
                    name = ("T0", d, h, u)
                    b = job_full(act, rj, name)
                    nc.scalar.copy(Tm[d][:, h].rearrange("p m j -> p (m j)"), b[:, :]).then_inc(free[rj[name][0]], 1)
                for lv in range(1, LEVELS):
                    if lv == 2:
                        y_feature(act, *rj[("yT", u)], (it * 2 + (u + NPAIR - 1)) & (NPAIR - 1))
                    if lv < LEVELS - 1:
                        for d, h in CHAINS:
                            name = ("Tr", lv, d, h, u)
                            b = job_full(act, rj, name)
                            nc.scalar.copy(TT[d][:, h].rearrange("p m j -> p (m j)"), b[:, :]).then_inc(free[rj[name][0]], 1)
                    for piece in ACT_WITH.get(lv, []):
                        prep_act(act, piece, rj, u)
                for m in range(NT):
                    for h in range(2):
                        b = job_full(act, rj, ("cx", m, h, u))
                        nc.scalar.copy(chain_x[:, h, :, :].rearrange("p d v -> p (d v)"), b[:, 0:128]).then_inc(free[rj[("cx", m, h, u)][0]], 1)
                    if m == 1:
                        b = job_full(act, rj, ("g", u))
                        act.wait_ge(ydone_ready, u + 1)
                        nc.scalar.copy(gT, b[:, :]).then_inc(free[rj[("g", u)][0]], 1)
                    b = job_full(act, rj, ("cu", m, u))
                    nc.scalar.copy(chain_u.rearrange("p h d v -> p (h d v)"), b[:, 0:256]).then_inc(free[rj[("cu", m, u)][0]], 1)
                    for piece in ACT_CHAIN.get(m, []):
                        prep_act(act, piece, rj, u)
                b = job_full(act, rj, ("v", u))
                job_read(act, rj, ("bonus", u))
                nc.scalar.copy(vT, b[:, :]).then_inc(free[rj[("v", u)][0]], 1)
                for h in range(2):
                    b = job_full(act, rj, ("y", h, u))
                    nc.scalar.copy(ytok[:, :, h, :], b[:, 0:256].rearrange("p (t v) -> p t v", t=NT)).then_inc(free[rj[("y", h, u)][0]], 1)

        def y_rstd(pool, n):
            pool.wait_ge(yvar_ready, n)
            nc.gpsimd.tensor_scalar(stat2, stat2, 1.0 / HEAD, GN_EPS, ALU.mult, ALU.add)
            pool.drain()
            nc.gpsimd.tensor_tensor(rstd8, stat2, mhalf[:, 0:8], ALU.pow).then_inc(yrstd_ready, 1)

        def pairs_pool(pool, it):
            for u in range(2):
                for d in range(2):
                    for h in range(2):
                        v = TT[d][:, h, :, :]
                        job_read(pool, rj, ("LR1", d, h, u))
                        nc.gpsimd.tensor_tensor(v, LTRB[d][h][:, :, 0, :], bc(level_mask[:, 0, :].unsqueeze(1), P, NT, P), ALU.mult)
                        pool.drain()
                        nc.gpsimd.tensor_tensor(v, v, bc(ident[:, :].unsqueeze(1), P, NT, P), ALU.add).then_inc(ttinit_ready, 1)
                y_rstd(pool, u + 1)

        y3 = ytok_flat.rearrange("p (g v) -> p g v", v=HEAD)

        def y_centre(dve):
            nc.vector.tensor_reduce(stat, y3, AX, ALU.add)
            dve.drain()
            nc.vector.tensor_scalar(stat, stat, 1.0 / HEAD, None, ALU.mult)
            dve.drain()
            nc.vector.tensor_tensor(y3, y3, bc(stat.unsqueeze(2), P, 8, HEAD), ALU.subtract).then_inc(ycen_ready, 1)

        def y_variance(dve, n):
            dve.wait_ge(ysq_ready, n)
            nc.vector.tensor_reduce(stat2, ysq.rearrange("p (g v) -> p g v", v=HEAD), AX, ALU.add).then_inc(yvar_ready, 1)

        def y_scale(dve, n):
            dve.wait_ge(yrstd_ready, n)
            nc.vector.tensor_tensor(ysq.rearrange("p (g v) -> p g v", v=HEAD), y3, bc(rstd8.unsqueeze(2), P, 8, HEAD), ALU.mult).then_inc(ynorm_ready, 1)

        def y_finish(dve, bank, n, parity, dst):
            dve.wait_ge(free[bank], n)
            nc.vector.tensor_tensor(ytok_flat, ytok_flat, bonus[parity], ALU.add)
            dve.drain()
            nc.vector.tensor_tensor(dst, ytok_flat, gT, ALU.mult).then_inc(ydone_ready, 1)

        def last_y_dve(dve):
            y_centre(dve)
            y_variance(dve, 1)
            y_scale(dve, 1)
            y_finish(dve, 0, 1, 1, yT[:, NPAIR - 1, :])

        def pairs_dve(dve, it):
            for u in range(2):
                prep_cols(dve, (it * 2 + (u + 1)) & (NPAIR - 1))
                b = job_full(dve, rj, ("bonus", u))
                nc.vector.tensor_tensor(bonus[u], b[:, :], vT, ALU.mult).then_inc(free[rj[("bonus", u)][0]], 1)
                for nm, dsts in (("LR", LTRB), ("MR", MTRK)):
                    for d in range(2):
                        mk = bc(strict_incl[d].unsqueeze(1), P, 2, 2, P)
                        for z in range(2):
                            for h in range(2):
                                name = (f"{nm}{z}", d, h, u)
                                b = job_full(dve, rj, name)
                                nc.vector.tensor_tensor(dsts[d][h][:, 2 * z:2 * z + 2], b[:, :].rearrange("p (m a j) -> p m a j", m=2, a=2),
                                                        mk, ALU.mult).then_inc(free[rj[name][0]], 1)
                    if nm == "LR":
                        if u:
                            for h in range(2):
                                job_read(dve, rj, ("y", h, u - 1))
                        y_centre(dve)
                    else:
                        y_variance(dve, u + 1)
                for lv in range(1, LEVELS):
                    for d, h in CHAINS:
                        name = ("X", lv, d, h, u)
                        b = job_full(dve, rj, name)
                        nc.vector.tensor_tensor(Xm[d][:, h], b[:, :].rearrange("p (m j) -> p m j", m=NT),
                                                bc(level_mask[:, lv, :].unsqueeze(1), P, NT, P), ALU.mult).then_inc(free[rj[name][0]], 1)
                    for d, h in CHAINS:
                        name = ("TX", lv, d, h, u)
                        b = job_full(dve, rj, name)
                        dst = Tm[d][:, h] if lv < LEVELS - 1 else TT[d][:, h]
                        nc.vector.tensor_tensor(dst, dst, b[:, :].rearrange("p (m j) -> p m j", m=NT), ALU.add).then_inc(free[rj[name][0]], 1)
                    dve.drain()
                    if lv == 1:
                        y_scale(dve, u + 1)
                    if lv == 3:
                        y_finish(dve, *rj[("yT", u)], 1 - u, y_out[u])
                    for piece in DVE_WITH.get(lv, []):
                        prep_dve(dve, piece, rj, u, 1 - u)
                for m in range(NT - 1):
                    b = job_full(dve, rj, ("cs", m, u))
                    for d in range(2):
                        tile = (m, NT - 1 - m)[d]
                        o = b[:, d * HEAD:(d + 1) * HEAD]
                        dec = end_dec[u][:, d, tile:tile + 1]
                        if m == 0:
                            nc.vector.tensor_scalar(states[1][:, d, :], o, dec, None, ALU.mult)
                        else:
                            nc.vector.scalar_tensor_tensor(states[(m + 1) % 2][:, d, :], o, dec, state_dec[:, d, :], ALU.mult, ALU.add)
                    dve.drain().then_inc(state_ready, 1)
                    for d in range(2):
                        nx = (m + 1, NT - 2 - m)[d]
                        nc.vector.tensor_scalar(state_dec[:, d, :], states[(m + 1) % 2][:, d, :], end_dec[u][:, d, nx:nx + 1], None, ALU.mult)
                    dve.drain().then_inc(free[rj[("cs", m, u)][0]], 1)
                    for piece in DVE_CHAIN[m]:
                        prep_dve(dve, piece, rj, u, 1 - u)

        def pair_loads(sp, pair):
            c = bass.ds(pair * P, P)
            for n, w in enumerate(("rw_wr", "rw_wk", "rw_wv")):
                sp.dma_start(w_sl[:, n], a[w][0].rearrange("(k p) n -> p k n", p=P)[:, :, c]).then_inc(ld_pair, 16)
            sp.dma_start(w2_sl, a["rw_w2"][0].rearrange("e k n -> (e k) n")[:, c]).then_inc(ld_pair, 16)
            sp.dma_start(a2_sl, a["rw_a2"][0].rearrange("e k n -> (e k) n")[:, c]).then_inc(ld_pair, 16)

        def gate_loads(sp, pair):
            c = bass.ds(pair * P, P)
            sp.dma_start(g2a_sl, a["rw_g2"][0][0:P, c]).then_inc(ld_gate, 16)
            sp.dma_start(g2b_sl[0:GATE - P, :], a["rw_g2"][0][P:GATE, c]).then_inc(ld_gate, 16)

        oj = Jobs([((t, z), (2 * t + z) % NB) for t in range(NT) for z in range(2)])

        def out_pe(pe, n):
            pe.wait_ge(ld_wo[n], 16)
            if n == 0:
                pe.wait_ge(ld_y, 16)
            for t in range(NT):
                for z in range(2):
                    b = open_job(pe, oj, (t, z))
                    for k in range(ND):
                        last = nc.tensor.matmul(b[:, :], yT[:, k, t * P:(t + 1) * P], wo_sb[:, k, z * 512:(z + 1) * 512],
                                                start=(k == 0), stop=(k == ND - 1))
                    last.then_inc(full[oj[(t, z)][0]], 1)

        def out_dve(dve, n):
            if n == 0:
                dve.wait_ge(ld_x2, 16 * NT)
            for t in range(NT):
                for z in range(2):
                    b = job_full(dve, oj, (t, z))
                    xs = x_sb[:, t, z * 512:(z + 1) * 512]
                    nc.vector.tensor_tensor(xs, xs, b[:, :], ALU.add).then_inc(free[oj[(t, z)][0]], 1)

        def load_x(sp, s):
            v = a["x"][0].rearrange("(t p) d -> p t d", p=P)
            for t in range(NT):
                sp.dma_start(x_sb[:, t, :], v[:, t, :]).then_inc(s, 16)

        def load_gain(sp, n):
            layer, which = divmod(n, 2)
            g = a[("norm_mix_g", "norm_ffn_g")[which]][layer:layer + 1, :]
            sp.dma_start(gain_row, g.to_broadcast([P, D])).then_inc(ld_gain[n], 16)

        route_jobs = Jobs([("lg", 0), ("at", 1), ("st", 2)])

        def route_pe(pe, layer):
            pe.wait_ge(ld_router[layer], 16)
            for t in range(NT):
                for k in range(ND):
                    last = nc.tensor.matmul(ps[0][:, t * NE:(t + 1) * NE], hT[:, k, t * P:(t + 1) * P], router_sb[:, k, :],
                                            start=(k == 0), stop=(k == ND - 1))
            last.then_inc(full[0], 1)
            pe.wait_ge(aff_ready, 1)
            for t in range(NT):
                last = nc.tensor.transpose(ps[1][0:NE, t * P:(t + 1) * P], aff[:, t, 0:NE], ident[:, :])
            last.then_inc(full[1], 1)
            pe.wait_ge(slot_ready, 1)
            for t in range(NT):
                last = nc.tensor.transpose(ps[2][:, t * NE:(t + 1) * NE], cumT[0:NE, t * P:(t + 1) * P], ident[0:NE, 0:NE])
            last.then_inc(full[2], 1)

        def route_act(act):
            act.wait_ge(logit_ready, 1)
            nc.scalar.activation(logit, logit, ACT.Exp).then_inc(exp_ready, 1)

        def route_pool(pool):
            nc.gpsimd.iota(iota_i, [[1, CAP]], base=0, channel_multiplier=0)
            nc.gpsimd.memset(slot[:, :, NE:NE + 2], -1.0)
            nc.gpsimd.memset(aff[:, :, NE:NE + 2], 0.0)
            pool.drain().then_inc(iota_ready, 1)

        def route_dve(dve):
            b = job_full(dve, route_jobs, "lg")
            lg = b[:, 0:NT * NE].rearrange("p (t e) -> p t e", t=NT)
            nc.vector.tensor_reduce(rmax, lg, AX, ALU.max)
            dve.drain()
            nc.vector.tensor_tensor(logit, lg, rmax.unsqueeze(2).to_broadcast([P, NT, NE]), ALU.subtract).then_inc(logit_ready, 1)
            dve.wait_ge(exp_ready, 1)
            nc.vector.tensor_reduce(rsum_t, logit, AX, ALU.add)
            dve.drain()
            nc.vector.reciprocal(rmax, rsum_t)
            dve.drain()
            nc.vector.tensor_tensor(aff[:, :, 0:NE], logit, rmax.unsqueeze(2).to_broadcast([P, NT, NE]), ALU.mult).then_inc(aff_ready, 1)
            b = job_full(dve, route_jobs, "at")
            nc.vector.tensor_copy(workT[0:NE, :], b[0:NE, :])
            for n in range(CAP // 8):
                dve.drain()
                nc.vector.max(top8[0:NE, :], workT[0:NE, :])
                dve.drain()
                nc.vector.match_replace(workT[0:NE, :], top8[0:NE, :], workT[0:NE, :], -1.0)
            dve.drain()
            nc.vector.tensor_scalar(maskT[0:NE, :], workT[0:NE, :], 0.0, None, ALU.is_lt)
            dve.drain()
            nc.vector.tensor_tensor_scan(cumT[0:NE, :], maskT[0:NE, :], maskT[0:NE, :], 0.0, ALU.add, ALU.max)
            dve.drain()
            nc.vector.tensor_tensor(cumT[0:NE, :], cumT[0:NE, :], maskT[0:NE, :], ALU.mult)
            dve.drain()
            nc.vector.tensor_scalar(cumT[0:NE, :], cumT[0:NE, :], -1.0, None, ALU.add).then_inc(slot_ready, 1)
            dve.wait_ge(iota_ready, 1)
            nc.vector.tensor_copy(iota_s, iota_i)
            b = job_full(dve, route_jobs, "st")
            nc.vector.tensor_copy(slot[:, :, 0:NE], b[:, 0:NT * NE].rearrange("p (t e) -> p t e", t=NT))
            dve.drain()
            picks(dve, 0)

        def picks(dve, first):
            for t in range(NT):
                for e in range(2):
                    o = slice(e * CAP, (e + 1) * CAP)
                    at = slot[:, t, bass.ds(first + e, 1)]
                    nc.vector.tensor_scalar(pick[:, t, o], iota_s, at, None, ALU.is_equal)
                    nc.vector.tensor_scalar(pick_gate[:, t, o], iota_s, at, aff[:, t, bass.ds(first + e, 1)], ALU.is_equal, ALU.mult)

        PER = [3, 3, 3, 2, 2, 1, 1, 4]
        comb_banks = [7, 0, 1, 2]

        def used(eng, b, it, n):
            eng.wait_ge(free[b], it * PER[b] + n)

        def filled(eng, b, it, n):
            eng.wait_ge(full[b], it * PER[b] + n)

        def read_out(eng, b, it, n):
            eng.wait_ge(free[b], it * PER[b] + n + 1)

        def arrived(pe, layer, it, c):
            pe.wait_ge(ld_chunk[c % RING], (it * (CPP // RING) + (c // RING + 1 + CPP // RING * (NE // 2) * layer)) * 16)

        def moe_pe(pe, it, layer):
            pe.wait_ge(pick_ready, it + 1)
            for z in range(2):
                used(pe, z, it, 1)
                for k in range(4):
                    for t in range(NT):
                        last = nc.tensor.matmul(ps[z][:, k * P:(k + 1) * P], h_tok[:, t, (4 * z + k) * P:(4 * z + k + 1) * P],
                                                pick[:, t, :], start=(t == 0), stop=(t == NT - 1))
                last.then_inc(full[z], 1)
            used(pe, 2, it, 1)
            for t in range(NT):
                last = nc.tensor.transpose(ps[2][:, t * P:(t + 1) * P], pick_gate[:, t, :], ident[:, :])
            last.then_inc(full[2], 1)
            read_out(pe, 0, it, 1)
            read_out(pe, 1, it, 1)

            def gate_up(e, z):
                used(pe, 3 + z, it, e + 1)
                c = 4 * e + 2 * z
                arrived(pe, layer, it, c)
                arrived(pe, layer, it, c + 1)
                for k in range(ND):
                    for g in range(2):
                        last = nc.tensor.matmul(ps[3 + z][g * CAP:(g + 1) * CAP, :], xeT[:, k, e * CAP:(e + 1) * CAP],
                                                ring[(c + g) % RING][:, k, :], start=(k == 0), stop=(k == ND - 1))
                pe.drain().then_inc(full[3 + z], 1)
                pe.sem_inc(chunk_used[layer], 2)

            def turn_hidden(e):
                pe.wait_ge(hid_ready, it * 4 + (2 * e + 2))
                used(pe, 7, it, e + 1)
                pe.sem_inc(waited, 1)
                for k in range(ND):
                    last = nc.tensor.transpose(ps[7][:, k * CAP:(k + 1) * CAP], hid_tok[e][0:CAP, k * P:(k + 1) * P], ident[0:CAP, 0:CAP])
                last.then_inc(full[7], 1)

            def down(e):
                used(pe, 5 + e, it, 1)
                read_out(pe, 7, it, e + 1)
                c = 8 + 2 * e
                arrived(pe, layer, it, c)
                arrived(pe, layer, it, c + 1)
                for k in range(ND):
                    for z in range(2):
                        last = nc.tensor.matmul(ps[5 + e][z * CAP:(z + 1) * CAP, :], hidT[e][:, k, :],
                                                ring[(c + z) % RING][:, k, :], start=(k == 0), stop=(k == ND - 1))
                pe.drain().then_inc(full[5 + e], 1)
                pe.sem_inc(chunk_used[layer], 2)

            gate_up(0, 0)
            gate_up(0, 1)
            gate_up(1, 0)
            turn_hidden(0)
            gate_up(1, 1)
            down(0)
            turn_hidden(1)
            down(1)
            read_out(pe, 2, it, 1)
            read_out(pe, 5, it, 1)
            read_out(pe, 6, it, 1)
            for j in range(8):
                t, z = divmod(j, 2)
                b = comb_banks[j % 4]
                used(pe, b, it, j // 4 + (3 if b == 7 else 2))
                nc.tensor.matmul(ps[b][:, :], combT[:, t * P:(t + 1) * P], ye[:, z * 512:(z + 1) * 512],
                                 start=True, stop=True).then_inc(full[b], 1)

        def moe_act(act, it):
            for z in range(2):
                filled(act, z, it, 1)
                nc.scalar.copy(xeT[:, 4 * z:4 * z + 4, :].rearrange("p k s -> p (k s)"), ps[z][:, :]).then_inc(free[z], 1)

            def half_tanh(e, z):
                filled(act, 3 + z, it, e + 1)
                nc.scalar.activation(th[z][0:CAP, :], ps[3 + z][0:CAP, :], ACT.Tanh, scale=0.5).then_inc(tanh_ready, 1)

            def hidden(e):
                filled(act, 7, it, e + 1)
                nc.scalar.copy(hidT[e].rearrange("p k s -> p (k s)"), ps[7][:, :]).then_inc(free[7], 1)

            def outputs(e):
                filled(act, 5 + e, it, 1)
                for z in range(2):
                    nc.scalar.copy(ye[e * CAP:(e + 1) * CAP, z * 512:(z + 1) * 512], ps[5 + e][z * CAP:(z + 1) * CAP, :])
                act.drain().then_inc(free[5 + e], 1)

            half_tanh(0, 0)
            half_tanh(0, 1)
            half_tanh(1, 0)
            hidden(0)
            half_tanh(1, 1)
            outputs(0)
            hidden(1)
            outputs(1)

        def moe_dve(dve, it):
            filled(dve, 2, it, 1)
            nc.vector.tensor_copy(combT, ps[2][:, :]).then_inc(free[2], 1)
            for e in range(2):
                for z in range(2):
                    dve.wait_ge(tanh_ready, it * 4 + (2 * e + z + 1))
                    nc.vector.scalar_tensor_tensor(th[z][0:CAP, :], th[z][0:CAP, :], 1.0, ps[3 + z][0:CAP, :], ALU.add, ALU.mult)
                    dve.drain()
                    nc.vector.scalar_tensor_tensor(hid_tok[e][0:CAP, z * 512:(z + 1) * 512], th[z][0:CAP, :], 0.5,
                                                   ps[3 + z][CAP:2 * CAP, :], ALU.mult, ALU.mult)
                    dve.drain().then_inc(free[3 + z], 1)
                    dve.sem_inc(hid_ready, 1)
                if e == 0:
                    filled(dve, 1, it, 1)
                    picks(dve, it * 2 + 2)
                    dve.drain().then_inc(pick_ready, 1)
            for j in range(8):
                t, z = divmod(j, 2)
                b = comb_banks[j % 4]
                filled(dve, b, it, j // 4 + (3 if b == 7 else 2))
                xs = x_sb[:, t, z * 512:(z + 1) * 512]
                nc.vector.tensor_tensor(xs, xs, ps[b][:, :], ALU.add).then_inc(free[b], 1)

        def load_chunk(sp, layer, pair, c):
            pair = pair + c // CPP
            c = c % CPP
            e, r = divmod(c, 4) if c < 8 else ((c - 8) // 2, 4 + c % 2)
            w, z = (("moe_w_gate", 0), ("moe_w_up", 0), ("moe_w_gate", 1), ("moe_w_up", 1), ("moe_w_down", 0), ("moe_w_down", 1))[r]
            v = a[w][layer].rearrange("(i e) (k p) n -> i e p k n", e=2, p=P)
            src = v[bass.ds(pair, 1), e, :, :, z * 512:(z + 1) * 512].rearrange("i p k n -> (i p) k n") \
                if not isinstance(pair, int) else v[pair, e, :, :, z * 512:(z + 1) * 512]
            sp.dma_start(ring[c % RING], src).then_inc(ld_chunk[c % RING], 16)

        def load_experts(sp, layer):
            last = NE // 2 - 1
            for c in range(RING):
                load_chunk(sp, layer, 0, c)
            with sp.Fori(0, last) as it:
                for c in range(CPP):
                    sp.wait_ge(chunk_used[layer], it * CPP + (c + 1))
                    sp.sem_inc(waited_sp, 1)
                    load_chunk(sp, layer, it, c + RING)
            for c in range(CPP - RING):
                sp.wait_ge(chunk_used[layer], last * CPP + c + 1)
                load_chunk(sp, layer, last, c + RING)

        CB = [(t, z) for t in range(NT) for z in range(2)]
        NC = (QL + KVL) // P
        mj = Jobs([(x, n) for n, x in enumerate(CB)] + [("cols", 0)] + [(("cT", j), j + 1) for j in range(NC)])

        def mla_in_pe(pe):
            pe.wait_ge(ld_win, 16)
            for t, z in CB:
                w = 512 if z == 0 else QL + KVL + ROPE - 512
                b = open_job(pe, mj, (t, z))
                for k in range(ND):
                    last = nc.tensor.matmul(b[:, 0:w], hT[:, k, t * P:(t + 1) * P], win_sb[:, k, z * 512:z * 512 + w],
                                            start=(k == 0), stop=(k == ND - 1))
                last.then_inc(full[mj[(t, z)][0]], 1)
            pe.wait_ge(ld_mla, 16 * 7)
            b = open_job(pe, mj, "cols")
            nc.tensor.transpose(b[:, 0:NC], norm_rows[0:NC, :], ident[0:NC, 0:NC]).then_inc(full[0], 1)
            pe.wait_ge(cnorm_ready, 1)
            for j in range(NC):
                b = open_job(pe, mj, ("cT", j))
                for t in range(NT):
                    last = nc.tensor.transpose(b[:, t * P:(t + 1) * P], c_tok[:, t, j * P:(j + 1) * P], ident[:, :])
                last.then_inc(full[j + 1], 1)

        def mla_in_act(act):
            for t, z in CB:
                w = 512 if z == 0 else QL + KVL + ROPE - 512
                b = job_full(act, mj, (t, z))
                nc.scalar.copy(c_tok[:, t, z * 512:z * 512 + w], b[:, 0:w]).then_inc(free[mj[(t, z)][0]], 1)
            act.drain()
            for t in range(NT):
                nc.scalar.activation(prob[0][:, t, 0:QL], c_tok[:, t, 0:QL], ACT.Square, accum_out=ss_c[:, t:t + 1])
                nc.scalar.activation(prob[1][:, t, 0:KVL], c_tok[:, t, QL:QL + KVL], ACT.Square, accum_out=ss_c[:, NT + t:NT + t + 1])
            act.drain().then_inc(css_ready, 1)
            act.wait_ge(red_ready, 1)
            nc.scalar.activation(sin8.rearrange("p (t h) f -> p t h f", h=2)[:, :, 0, :], red, ACT.Sin)
            nc.scalar.activation(cos8.rearrange("p (t h) f -> p t h f", h=2)[:, :, 0, :], ang, ACT.Sin)
            act.drain()
            for v in (sin8, cos8):
                w = v.rearrange("p (t h) f -> p t h f", h=2)
                nc.scalar.copy(w[:, :, 1, :], w[:, :, 0, :])
            act.drain().then_inc(trig_ready, 1)

        def mla_in_pool(pool):
            for n in range(HALF):
                nc.gpsimd.memset(freq[:, n:n + 1], float(np.float32(THETA) ** np.float32(-2.0 * n / ROPE)))
            pool.drain()
            nc.gpsimd.memset(gain_cols[NOPE:QK, :], 1.0)
            pool.drain().then_inc(freq_ready, 1)
            pool.wait_ge(css_ready, 1)
            nc.gpsimd.tensor_scalar(ss_c[:, 0:NT], ss_c[:, 0:NT], 1.0 / QL, NORM_EPS, ALU.mult, ALU.add)
            nc.gpsimd.tensor_scalar(ss_c[:, NT:], ss_c[:, NT:], 1.0 / KVL, NORM_EPS, ALU.mult, ALU.add)
            pool.drain()
            nc.gpsimd.tensor_tensor(rstd_c, ss_c, mhalf[:, 0:8], ALU.pow).then_inc(crstd_ready, 1)

        def mla_in_dve(dve):
            dve.wait_ge(ld_mla, 16 * 7)
            nc.vector.tensor_copy(pos_f, pos_i)
            dve.wait_ge(freq_ready, 1)
            dve.drain()
            nc.vector.tensor_tensor(red, pos_f.unsqueeze(2).to_broadcast([P, NT, HALF]), freq.unsqueeze(1).to_broadcast([P, NT, HALF]), ALU.mult)
            dve.drain()
            nc.vector.tensor_scalar(rnd, red, float(1.0 / (2.0 * np.pi)), 12582912.0, ALU.mult, ALU.add)
            dve.drain()
            nc.vector.tensor_scalar(rnd, rnd, -12582912.0, None, ALU.add)
            dve.drain()
            two_pi = 2.0 * np.pi
            c1 = 6.28125
            c2 = float(np.float32(np.round((two_pi - c1) * 2.0 ** 21) / 2.0 ** 21))
            c3 = two_pi - c1 - c2
            for c in (c1, c2, c3):
                nc.vector.scalar_tensor_tensor(red, rnd, -float(c), red, ALU.mult, ALU.add)
                dve.drain()
            nc.vector.tensor_scalar(red, red, 3.1415925, -3.1415925, ALU.min, ALU.max)
            dve.drain()
            nc.vector.scalar_tensor_tensor(ang, red, -1.0, red, ALU.mult, ALU.max)
            dve.drain()
            nc.vector.tensor_scalar(ang, ang, -1.0, float(np.pi / 2), ALU.mult, ALU.add).then_inc(red_ready, 1)
            job_full(dve, mj, "cols")
            nc.vector.tensor_copy(norm_cols[:, 0:NC], ps[0][:, 0:NC])
            dve.wait_ge(crstd_ready, 1)
            for t in range(NT):
                for lo, hi, s in ((0, QL, t), (QL, QL + KVL, NT + t)):
                    nc.vector.tensor_scalar(c_tok[:, t, lo:hi], c_tok[:, t, lo:hi], rstd_c[:, s:s + 1], None, ALU.mult)
            dve.drain().then_inc(cnorm_ready, 1)
            for j in range(NC):
                b = job_full(dve, mj, ("cT", j))
                nc.vector.tensor_scalar(cT[:, j, :], b[:, :], norm_cols[:, j:j + 1], None, ALU.mult)
            dve.wait_ge(trig_ready, 1)
            raw = c_tok[:, :, QL + KVL:]
            nc.vector.tensor_tensor(k_rope, raw, raw, ALU.mult)
            dve.drain()
            nc.vector.tensor_reduce(krope_ss, k_rope, AX, ALU.add)
            dve.drain()
            nc.vector.tensor_tensor(k_rope, raw, head_gain[:, 1, NOPE:].unsqueeze(1).to_broadcast([P, NT, ROPE]), ALU.mult)
            dve.drain()
            rotate(dve, k_rope, [v[:, 0:NT, :] for v in rtmp], cos8.rearrange("p (t h) f -> p t h f", h=2)[:, :, 0, :],
                   sin8.rearrange("p (t h) f -> p t h f", h=2)[:, :, 0, :])

        NQ, NKV = QL // P, KVL // P

        def prep_names(u):
            return [("kv", u, 0), ("kv", u, 1)], [("q", u, 0), ("q", u, 1)], [("Tk", u, 0), ("Tk", u, 1)], [("Tq", u, 0), ("Tq", u, 1)]

        def number(names):
            return Jobs([(x, n % NB) for n, x in enumerate(names)])

        names = []
        for u in range(2):
            kv_, q_, tk_, tq_ = prep_names(u)
            names += [("S", u, 0, t) for t in range(NT)] + kv_ + [("S", u, 1, t) for t in range(NT)] + q_
            names += [("PT", u, 0, t) for t in range(NT)] + tk_ + [("PT", u, 1, t) for t in range(NT)] + [("o", u)] + tq_
        aj = number(names)
        ij = number(sum(prep_names(0), []))
        SCALE = QK ** -0.5

        def project_heads(pe, jobs, kind, u):
            w, n0, n, width = (wq_sl, 0, NQ, 2 * QK) if kind == "q" else (wkv_sl, NQ, NKV, 2 * (NOPE + VH))
            for z in range(2):
                b = open_job(pe, jobs, (kind, u, z))
                for y in range(2):
                    t = 2 * z + y
                    for j in range(n):
                        last = nc.tensor.matmul(b[:, y * width:(y + 1) * width], cT[:, n0 + j, t * P:(t + 1) * P], w[:, j, :],
                                                start=(j == 0), stop=(j == n - 1))
                last.then_inc(full[jobs[(kind, u, z)][0]], 1)

        def turn_heads(pe, jobs, kind, u, tok):
            for h in range(2):
                b = open_job(pe, jobs, (kind, u, h))
                for t in range(NT):
                    last = nc.tensor.transpose(b[0:QK, t * P:(t + 1) * P], tok[:, 2 * t + h, :], ident[:, :])
                last.then_inc(full[jobs[(kind, u, h)][0]], 1)

        def keys_act(act, jobs, u, v):
            if u > 0:
                act.wait_ge(full[jobs[("Tk", u - 1, 1)][0]], jobs[("Tk", u - 1, 1)][1])
            for z in range(2):
                b = job_full(act, jobs, ("kv", u, z))
                kv = b[:, :].rearrange("p (g c) -> p g c", g=4)
                nc.scalar.activation(k_sq[:, 4 * z:4 * z + 4, :], kv[:, :, 0:NOPE], ACT.Square).then_inc(ksq_ready, 1)
                nc.scalar.copy(k_tok[:, 4 * z:4 * z + 4, 0:NOPE], kv[:, :, 0:NOPE])
                nc.scalar.copy(v[:, 2 * z:2 * z + 2, :, :].rearrange("p t h v -> p (t h) v"), kv[:, :, NOPE:]).then_inc(free[jobs[("kv", u, z)][0]], 1)

        def queries_act(act, jobs, u):
            if u > 0:
                act.wait_ge(full[jobs[("Tq", u - 1, 1)][0]], jobs[("Tq", u - 1, 1)][1])
            for z in range(2):
                b = job_full(act, jobs, ("q", u, z))
                nc.scalar.activation(q_sq[:, 4 * z:4 * z + 4, :].rearrange("p g c -> p (g c)"), b[:, 0:4 * QK], ACT.Square).then_inc(qksq_ready, 1)
                nc.scalar.copy(q_tok[:, 4 * z:4 * z + 4, :].rearrange("p g c -> p (g c)"), b[:, 0:4 * QK]).then_inc(free[jobs[("q", u, z)][0]], 1)

        def turned_act(act, jobs, kind, u, dst, col):
            b = job_full(act, jobs, (kind, u, 0))
            nc.scalar.activation(dst[0:QK, :], b[0:QK, :], ACT.Identity, scale=gain_cols[0:QK, col:col + 1]).then_inc(free[jobs[(kind, u, 0)][0]], 1)

        def turned_dve(dve, jobs, kind, u, dst, col):
            b = job_full(dve, jobs, (kind, u, 1))
            nc.vector.tensor_scalar(dst[0:QK, :], b[0:QK, :], gain_cols[0:QK, col:col + 1], None, ALU.mult).then_inc(free[jobs[(kind, u, 1)][0]], 1)

        def keys_sum_dve(dve, u):
            dve.wait_ge(ksq_ready, 2 * u + 2)
            nc.vector.tensor_reduce(kss, k_sq, AX, ALU.add)
            dve.drain()
            nc.vector.tensor_tensor(kss.rearrange("p (t h) -> p t h", h=2), kss.rearrange("p (t h) -> p t h", h=2),
                                    krope_ss.unsqueeze(2).to_broadcast([P, NT, 2]), ALU.add).then_inc(qkss_ready, 1)

        def keys_scale_dve(dve, jobs, u):
            job_read(dve, jobs, ("kv", u, 1))
            dve.wait_ge(krstd_ready, u + 1)
            nc.vector.tensor_tensor(k_tok[:, :, 0:NOPE], k_tok[:, :, 0:NOPE], krstd.unsqueeze(2).to_broadcast([P, 8, NOPE]), ALU.mult)
            for h in range(2):
                nc.vector.tensor_tensor(k_tok[:, :, NOPE:].rearrange("p (t h) c -> p t h c", h=2)[:, :, h, :], k_rope,
                                        krstd.rearrange("p (t h) -> p t h", h=2)[:, :, h:h + 1].to_broadcast([P, NT, ROPE]), ALU.mult)
            dve.drain().then_inc(k_ready, 1)

        def keys_pool(pool, u):
            pool.wait_ge(qkss_ready, 2 * u + 1)
            nc.gpsimd.tensor_scalar(kss, kss, 1.0 / QK, NORM_EPS, ALU.mult, ALU.add)
            pool.drain()
            nc.gpsimd.tensor_tensor(krstd, kss, mhalf[:, 0:8], ALU.pow).then_inc(krstd_ready, 1)

        def rotate(dve, x, tmp, c, s):
            x1, x2 = x[:, :, 0:HALF], x[:, :, HALF:]
            for o, v, y in ((0, x1, c), (1, x2, s), (2, x2, c), (3, x1, s)):
                nc.vector.tensor_tensor(tmp[o], v, y, ALU.mult)
            dve.drain()
            nc.vector.tensor_tensor(x1, tmp[0], tmp[1], ALU.subtract)
            nc.vector.tensor_tensor(x2, tmp[2], tmp[3], ALU.add)

        def queries_dve(dve, jobs, u):
            dve.wait_ge(qksq_ready, 2 * u + 2)
            nc.vector.tensor_reduce(qss, q_sq, AX, ALU.add).then_inc(qkss_ready, 1)
            job_read(dve, jobs, ("q", u, 1))
            x = q_tok[:, :, NOPE:]
            nc.vector.tensor_tensor(x, x, head_gain[:, 0, NOPE:].unsqueeze(1).to_broadcast([P, 8, ROPE]), ALU.mult)
            dve.drain()
            rotate(dve, x, rtmp, cos8, sin8)
            dve.drain().then_inc(qk_ready, 1)

        def queries_pool(pool, u, parity):
            pool.wait_ge(qkss_ready, 2 * u + 2)
            nc.gpsimd.tensor_scalar(qss, qss, 1.0 / QK, NORM_EPS, ALU.mult, ALU.add)
            pool.drain()
            nc.gpsimd.tensor_tensor(q_scale[parity], qss, mhalf[:, 0:8], ALU.pow)
            pool.drain()
            nc.gpsimd.tensor_scalar(q_scale_neg[parity], q_scale[parity], -SCALE, None, ALU.mult)
            nc.gpsimd.tensor_scalar(q_scale[parity], q_scale[parity], SCALE, None, ALU.mult).then_inc(qkrstd_ready, 1)

        def attn_first_pe(pe):
            pe.wait_ge(ld_pair2, 32)
            project_heads(pe, ij, "kv", 0)
            project_heads(pe, ij, "q", 0)
            pe.wait_ge(k_ready, 1)
            turn_heads(pe, ij, "Tk", 0, k_tok)
            pe.wait_ge(qk_ready, 1)
            turn_heads(pe, ij, "Tq", 0, q_tok)

        def attn_first_act(act):
            keys_act(act, ij, 0, v_tok[0])
            queries_act(act, ij, 0)
            turned_act(act, ij, "Tk", 0, qkT[0][1], 1)
            turned_act(act, ij, "Tq", 0, qkT[0][0], 0)

        def attn_first_dve(dve):
            keys_sum_dve(dve, 0)
            keys_scale_dve(dve, ij, 0)
            queries_dve(dve, ij, 0)
            turned_dve(dve, ij, "Tk", 0, qkT[1][1], 1)
            turned_dve(dve, ij, "Tq", 0, qkT[1][0], 0)

        def attn_first_pool(pool):
            keys_pool(pool, 0)
            queries_pool(pool, 0, 0)

        def attn_pe(pe, it):
            for u in range(2):
                if u > 0:
                    job_read(pe, aj, ("Tk", u - 1, 0))
                    job_read(pe, aj, ("Tk", u - 1, 1))
                for h in range(2):
                    if u > 0:
                        job_read(pe, aj, ("Tq", u - 1, h))
                    for t in range(NT):
                        b = open_job(pe, aj, ("S", u, h, t))
                        nc.tensor.matmul(b[:, :], qkT[h][0][0:QK, t * P:(t + 1) * P], qkT[h][1][0:QK, :],
                                         start=True, stop=True).then_inc(full[aj[("S", u, h, t)][0]], 1)
                    if h == 0:
                        pe.wait_ge(ld_pair2, (it * 2 + (u + 2)) * 32)
                        project_heads(pe, aj, "kv", u)
                    else:
                        project_heads(pe, aj, "q", u)
                for h in range(2):
                    pe.wait_ge(prob_ready, NT * (2 * u + h + 1))
                    for t in range(NT):
                        b = open_job(pe, aj, ("PT", u, h, t))
                        for q in range(NT):
                            last = nc.tensor.transpose(b[:, q * P:(q + 1) * P], prob[h][:, q, t * P:(t + 1) * P], ident[:, :])
                        last.then_inc(full[aj[("PT", u, h, t)][0]], 1)
                    if h == 0:
                        pe.wait_ge(k_ready, u + 1)
                        turn_heads(pe, aj, "Tk", u, k_tok)
                b = open_job(pe, aj, ("o", u))
                for t in range(NT):
                    for h in range(2):
                        job_read(pe, aj, ("PT", u, h, t))
                        last = nc.tensor.matmul(b[h * VH:(h + 1) * VH, :], v_tok[u][:, t, h, :], probT[h][:, t, :],
                                                start=(t == 0), stop=(t == NT - 1))
                last.then_inc(full[aj[("o", u)][0]], 1)
                pe.wait_ge(qk_ready, u + 1)
                turn_heads(pe, aj, "Tq", u, q_tok)

        def attn_act(act, it):
            for u in range(2):
                for h in range(2):
                    if u > 0:
                        act.wait_ge(full[aj[("PT", u - 1, h, NT - 1)][0]], aj[("PT", u - 1, h, NT - 1)][1])
                    for t in range(NT):
                        n = NT * h + t
                        act.wait_ge(max_ready, 4 * u + 2 * h + t // 2 + 1)
                        b = job_full(act, aj, ("S", u, h, t))
                        nc.scalar.activation(prob[h][:, t, :], b[:, :], ACT.Exp, bias=nmx[:, n:n + 1],
                                             scale=q_scale[u][:, 2 * t + h:2 * t + h + 1], accum_out=lsum[:, n:n + 1])
                        act.drain().then_inc(free[aj[("S", u, h, t)][0]], 1)
                    if h == 0:
                        keys_act(act, aj, u, v_tok[1 - u])
                queries_act(act, aj, u)
                for h in range(2):
                    for t in (0, 2):
                        b = job_full(act, aj, ("PT", u, h, t))
                        nc.scalar.copy(probT[h][:, t, :], b[:, :]).then_inc(free[aj[("PT", u, h, t)][0]], 1)
                    if h == 0:
                        turned_act(act, aj, "Tk", u, qkT[0][1], 1)
                b = job_full(act, aj, ("o", u))
                nc.scalar.copy(hT[:, bass.ds(it * 2 + u, 1), :].rearrange("p a s -> p (a s)"), b[:, :]).then_inc(free[aj[("o", u)][0]], 1)
                turned_act(act, aj, "Tq", u, qkT[0][0], 0)

        def attn_pool(pool, it):
            for u in range(2):
                keys_pool(pool, u)
                queries_pool(pool, u, 1 - u)

        def attn_dve(dve, it):
            for u in range(2):
                def row_max(h):
                    for z in range(2):
                        for t in (2 * z, 2 * z + 1):
                            b = job_full(dve, aj, ("S", u, h, t))
                            nc.vector.tensor_reduce(mx[:, NT * h + t:NT * h + t + 1], b[:, :], AX, ALU.max)
                        if h == 0 and z == 0 and u > 0:
                            dve.wait_ge(qkrstd_ready, u)
                        dve.drain()
                        n = NT * h + 2 * z
                        nc.vector.tensor_tensor(nmx[:, n:n + 2], mx[:, n:n + 2],
                                                q_scale_neg[u].rearrange("p (t h) -> p h t", h=2)[:, h, 2 * z:2 * z + 2],
                                                ALU.mult).then_inc(max_ready, 1)

                def normed(h):
                    for z in range(2):
                        n = NT * h + 2 * z
                        job_read(dve, aj, ("S", u, h, 2 * z))
                        job_read(dve, aj, ("S", u, h, 2 * z + 1))
                        nc.vector.reciprocal(linv[:, n:n + 2], lsum[:, n:n + 2])
                        dve.drain()
                        for t in (2 * z, 2 * z + 1):
                            nc.vector.tensor_scalar(prob[h][:, t, :], prob[h][:, t, :], linv[:, NT * h + t:NT * h + t + 1], None,
                                                    ALU.mult).then_inc(prob_ready, 1)

                def rows_turned(h):
                    for t in (1, 3):
                        b = job_full(dve, aj, ("PT", u, h, t))
                        nc.vector.tensor_copy(probT[h][:, t, :], b[:, :]).then_inc(free[aj[("PT", u, h, t)][0]], 1)

                row_max(0)
                normed(0)
                keys_sum_dve(dve, u)
                row_max(1)
                keys_scale_dve(dve, aj, u)
                normed(1)
                rows_turned(0)
                turned_dve(dve, aj, "Tk", u, qkT[1][1], 1)
                queries_dve(dve, aj, u)
                rows_turned(1)
                turned_dve(dve, aj, "Tq", u, qkT[1][0], 0)

        def attn_loads(sp, pair):
            sp.dma_start(wq_sl, a["mla_w_uq"][0].rearrange("(k p) n -> p k n", p=P)[:, :, bass.ds(pair * (2 * QK), 2 * QK)]).then_inc(ld_pair2, 16)
            sp.dma_start(wkv_sl, a["mla_w_ukv"][0].rearrange("(k p) n -> p k n", p=P)[:, :, bass.ds(pair * (2 * (NOPE + VH)), 2 * (NOPE + VH))]).then_inc(ld_pair2, 16)

        @block.gpsimd
        def _(pool):
            nc.gpsimd.memset(ident[:, :], 0.0)
            nc.gpsimd.memset(mhalf, -0.5)
            pool.drain()
            nc.gpsimd.affine_select(out=ident[:, :], in_=ident[:, :], compare_op=ALU.not_equal, fill=1.0,
                                    base=0, pattern=[[-1, P]], channel_multiplier=1)
            everyone = ("pe", "act", "dve", "sp")
            meet_pool(pool, [])
            norm_pool(pool)
            meet_pool(pool, norm_sems)
            meet_pool(pool, inputs_sems, everyone)
            masks_pool(pool)
            meet_pool(pool, [consts_ready])
            meet_pool(pool, prep_sems, everyone)
            with pool.Fori(0, NPAIR // 2) as it:
                pairs_pool(pool, it)
                meet_pool(pool, pairs_sems, everyone)
            y_rstd(pool, 1)
            meet_pool(pool, banks + y_sems, everyone)
            for layer in range(2):
                if layer == 1:
                    norm_pool(pool)
                    meet_pool(pool, norm_sems)
                    mla_in_pool(pool)
                    meet_pool(pool, mla_in_sems, everyone)
                    attn_first_pool(pool)
                    meet_pool(pool, heads_sems, everyone)
                    with pool.Fori(0, NPAIR // 2) as it:
                        attn_pool(pool, it)
                        meet_pool(pool, attn_sems, everyone)
                meet_pool(pool, banks)
                norm_pool(pool)
                meet_pool(pool, norm_sems)
                route_pool(pool)
                meet_pool(pool, route_sems, credit=1)
                meet_pool(pool, moe_sems, everyone)

        @block.tensor
        def _(pe):
            meet(pe, "pe")
            norm_pe(pe)
            meet(pe, "pe")
            pre_pe(pe)
            meet(pe, "pe")
            meet(pe, "pe")
            first_pe(pe)
            meet(pe, "pe")
            with pe.Fori(0, NPAIR // 2) as it:
                pairs_pe(pe, it)
                meet(pe, "pe")
            last_y_pe(pe)
            meet(pe, "pe")
            for layer in range(2):
                if layer == 1:
                    norm_pe(pe)
                    meet(pe, "pe")
                    mla_in_pe(pe)
                    meet(pe, "pe")
                    attn_first_pe(pe)
                    meet(pe, "pe")
                    with pe.Fori(0, NPAIR // 2) as it:
                        attn_pe(pe, it)
                        meet(pe, "pe")
                out_pe(pe, layer)
                meet(pe, "pe")
                norm_pe(pe)
                meet(pe, "pe")
                route_pe(pe, layer)
                meet(pe, "pe")
                with pe.Fori(0, NE // 2) as it:
                    moe_pe(pe, it, layer)
                meet(pe, "pe")

        @block.scalar
        def _(act):
            meet(act, "act")
            norm_act(act, True)
            meet(act, "act")
            pre_act(act)
            meet(act, "act")
            meet(act, "act")
            first_act(act)
            meet(act, "act")
            with act.Fori(0, NPAIR // 2) as it:
                pairs_act(act, it)
                meet(act, "act")
            last_y_act(act)
            meet(act, "act")
            for layer in range(2):
                if layer == 1:
                    norm_act(act, False)
                    meet(act, "act")
                    mla_in_act(act)
                    meet(act, "act")
                    attn_first_act(act)
                    meet(act, "act")
                    with act.Fori(0, NPAIR // 2) as it:
                        attn_act(act, it)
                        meet(act, "act")
                meet(act, "act")
                norm_act(act, False)
                meet(act, "act")
                route_act(act)
                meet(act, "act")
                with act.Fori(0, NE // 2) as it:
                    moe_act(act, it)
                meet(act, "act")

        @block.vector
        def _(dve):
            meet(dve, "dve")
            norm_dve(dve, 0)
            meet(dve, "dve")
            pre_dve(dve)
            meet(dve, "dve")
            masks_dve(dve)
            meet(dve, "dve")
            first_dve(dve)
            meet(dve, "dve")
            with dve.Fori(0, NPAIR // 2) as it:
                pairs_dve(dve, it)
                meet(dve, "dve")
            last_y_dve(dve)
            meet(dve, "dve")
            for layer in range(2):
                if layer == 1:
                    norm_dve(dve, 2)
                    meet(dve, "dve")
                    mla_in_dve(dve)
                    meet(dve, "dve")
                    attn_first_dve(dve)
                    meet(dve, "dve")
                    with dve.Fori(0, NPAIR // 2) as it:
                        attn_dve(dve, it)
                        meet(dve, "dve")
                out_dve(dve, layer)
                meet(dve, "dve")
                norm_dve(dve, 2 * layer + 1)
                meet(dve, "dve")
                route_dve(dve)
                meet(dve, "dve")
                dve.sem_inc(pick_ready, 1)
                with dve.Fori(0, NE // 2) as it:
                    moe_dve(dve, it)
                meet(dve, "dve")

        @block.sync
        def _(sp):
            load_x(sp, ld_x)
            load_gain(sp, 0)
            for dst, w in ((w1_sb, "rw_w1"), (a1_sb, "rw_a1")):
                for e in range(2):
                    sp.dma_start(dst[:, :, e * LORA:(e + 1) * LORA], a[w][0, e].rearrange("(k p) n -> p k n", p=P)).then_inc(ld_lora, 16)
            for lo, hi in ((0, GATE // 2), (GATE // 2, GATE)):
                sp.dma_start(g1_sb[:, :, lo:hi], a["rw_g1"][0].rearrange("(k p) n -> p k n", p=P)[:, :, lo:hi]).then_inc(ld_lora, 16)
            rows = [(V_MU, a["rw_mu"][0].rearrange("g (k p) -> (g k) p", p=P), 6), (V_KK, a["rw_kk"][0].rearrange("(k p) -> k p", p=P), 1),
                    (V_KA, a["rw_ka"][0].rearrange("(k p) -> k p", p=P), 1), (V_W0, a["rw_w0"][0].rearrange("g (k p) -> (g k) p", p=P), 2),
                    (V_A0, a["rw_a0"][0].rearrange("g (k p) -> (g k) p", p=P), 2), (V_GNG, a["rw_gn_g"][0].rearrange("(k p) -> k p", p=P), 1),
                    (V_GNB, a["rw_gn_b"][0].rearrange("(k p) -> k p", p=P), 1), (V_RK, a["rw_rk"][0].rearrange("(k u) j -> k (u j)", u=2), 1)]
            for at, src, n in rows:
                sp.dma_start(vec_rows[at * ND:(at + n) * ND, :], src).then_inc(ld_vec, 16)
            meet(sp, "sp")
            pair_loads(sp, 0)
            gate_loads(sp, 0)
            meet(sp, "sp")
            pair_loads(sp, 1)
            with sp.Fori(0, NPAIR // 2) as it:
                for u in range(2):
                    sp.wait_ge(ydone_ready, u + 1)
                    sp.dma_start(y_dram[bass.ds((it * 2 + (u + NPAIR - 1)) & (NPAIR - 1), 1)].rearrange("a p s -> p a s"), y_out[u].unsqueeze(1)).then_inc(y_stored, 16)
                    for x in ("g", "v"):
                        sp.wait_ge(full[rj[(x, u)][0]], rj[(x, u)][1])
                    gate_loads(sp, (it * 2 + (u + 1)) & (NPAIR - 1))
                    pair_loads(sp, (it * 2 + (u + 2)) & (NPAIR - 1))
                sp.wait_ge(y_stored, it * 32 + 32)
                sp.sem_inc(waited_sp, 1)
                meet(sp, "sp")
            sp.wait_ge(ld_pair, 16 * 5 * (NPAIR + 2))
            sp.wait_ge(ld_gate, 16 * 2 * (NPAIR + 1))
            sp.dma_start(yT[:, 0:NPAIR - 1, :], y_dram[0:NPAIR - 1].rearrange("k p s -> p k s")).then_inc(ld_y, 16)
            wo = [a[w][0].rearrange("(k p) n -> p k n", p=P) for w in ("rw_wo", "mla_w_o")]
            router = [a["moe_router"][n].rearrange("(k p) n -> p k n", p=P) for n in range(2)]
            sp.dma_start(wo_sb, wo[0]).then_inc(ld_wo[0], 16)
            load_x(sp, ld_x2)
            load_gain(sp, 1)
            sp.dma_start(router_sb, router[0]).then_inc(ld_router[0], 16)
            meet(sp, "sp")
            load_experts(sp, 0)
            meet(sp, "sp")
            load_gain(sp, 2)
            sp.dma_start(win_sb, a["mla_w_in"][0].rearrange("(k p) n -> p k n", p=P)).then_inc(ld_win, 16)
            sp.dma_start(norm_rows[0:QL // P, :], a["mla_q_norm_g"][0].rearrange("(k p) -> k p", p=P)).then_inc(ld_mla, 16)
            sp.dma_start(norm_rows[QL // P:(QL + KVL) // P, :], a["mla_kv_norm_g"][0].rearrange("(k p) -> k p", p=P)).then_inc(ld_mla, 16)
            sp.dma_start(head_gain[:, 0, :], a["mla_q_head_g"][0:1, :].to_broadcast([P, QK])).then_inc(ld_mla, 16)
            sp.dma_start(head_gain[:, 1, :], a["mla_k_head_g"][0:1, :].to_broadcast([P, QK])).then_inc(ld_mla, 16)
            sp.dma_start(pos_i, a["positions"][0].rearrange("(t p) -> p t", p=P), allow_slow_non_contiguous=True).then_inc(ld_mla, 16)
            for z, g in enumerate(("mla_q_head_g", "mla_k_head_g")):
                sp.dma_start(gain_cols[0:NOPE, z:z + 1], a[g][0, 0:NOPE].rearrange("(p o) -> p o", o=1), allow_slow_non_contiguous=True).then_inc(ld_mla, 16)
            attn_loads(sp, 0)
            meet(sp, "sp")
            sp.dma_start(wo_sb, wo[1]).then_inc(ld_wo[1], 16)
            load_gain(sp, 3)
            meet(sp, "sp")
            attn_loads(sp, 1)
            with sp.Fori(0, NPAIR // 2) as it:
                for u in range(2):
                    sp.wait_ge(full[aj[("q", u, 1)][0]], aj[("q", u, 1)][1])
                    attn_loads(sp, (it * 2 + (u + 2)) & (NPAIR - 1))
                meet(sp, "sp")
            sp.wait_ge(ld_pair2, 32 * (NPAIR + 2))
            sp.dma_start(router_sb, router[1]).then_inc(ld_router[1], 16)
            load_experts(sp, 1)
            meet(sp, "sp")
            o = a["out"][0].rearrange("(t p) d -> p t d", p=P)
            for t in range(NT):
                sp.dma_start(o[:, t, :], x_sb[:, t, :]).then_inc(stored, 16)
            sp.wait_ge(stored, 16 * NT)


_INS = ['x', 'positions', 'norm_mix_g', 'norm_ffn_g', 'rw_mu', 'rw_wr', 'rw_wk', 'rw_wv', 'rw_wo', 'rw_w0', 'rw_w1',
        'rw_w2', 'rw_a0', 'rw_a1', 'rw_a2', 'rw_g1', 'rw_g2', 'rw_kk', 'rw_ka', 'rw_rk', 'rw_gn_g', 'rw_gn_b',
        'mla_w_in', 'mla_q_norm_g', 'mla_kv_norm_g', 'mla_w_uq', 'mla_w_ukv', 'mla_q_head_g', 'mla_k_head_g',
        'mla_w_o', 'moe_router', 'moe_w_gate', 'moe_w_up', 'moe_w_down']


def kernel(**inputs):
    import concourse.bacc as bacc
    from concourse.bass_utils import run_bass_kernel_spmd

    nc = bacc.Bacc("TRN2", target_bir_lowering=False, num_devices=1)
    arrays, args = {}, {}
    for name in _INS:
        arrays[f"in_{name}"] = np.ascontiguousarray(inputs[name])
        args[name] = nc.dram_tensor(f"in_{name}", arrays[f"in_{name}"].shape, mybir.dt.from_np(arrays[f"in_{name}"].dtype),
                                    kind="ExternalInput").ap()
    args["out"] = nc.dram_tensor("out_dram", (1, S, D), F32, kind="ExternalOutput").ap()
    trunk(nc, args)
    r = run_bass_kernel_spmd(nc, [arrays], core_ids=[0])
    return r.results[0]["out_dram"]
```
